# Optimizing a Trainium2 kernel written in Bass

```python
import math
import jax, jax.numpy as jnp
from jax import lax
import numpy as np

D_MODEL = 2048
BATCH = 1
SEQ = 512
DEPTH = 1
DEC_BATCH = 8
DEC_SEQ = 4
PAST_LEN = 4096
PAGE_SIZE = 128

N_META = 16
ATT_WIDTH = D_MODEL // 2
HEAD_DIM_A = 64
V_DIM_A = 2 * HEAD_DIM_A
N_HEADS_A = ATT_WIDTH // V_DIM_A
MLSTM_WIDTH = D_MODEL - ATT_WIDTH
N_HEADS_M = 4
HEAD_DIM_M = MLSTM_WIDTH // N_HEADS_M
CONV_W = 4
CHUNK = 64
Q_BLOCK = 128
D_FF = 4 * D_MODEL
PROJ_WIDTH = 3 * ATT_WIDTH + 3 * MLSTM_WIDTH + 2 * N_HEADS_M
FORGET_BIAS = 3.0
EPS = 1e-6

kernel_name = "hymba_diffattn_mlstm_decoder_step"

def rms_norm(x, g):
    xf = x.astype(jnp.float32)
    y = xf * lax.rsqrt(jnp.mean(xf * xf, axis=-1, keepdims=True) + EPS)
    return (y * g.astype(jnp.float32)).astype(x.dtype)

def alibi_slopes():
    return 2.0 ** (-8.0 * jnp.arange(1, N_HEADS_A + 1, dtype=jnp.float32) / N_HEADS_A)

def diff_lambda(lambda_qk, lam_init):
    l = lambda_qk.astype(jnp.float32)
    return jnp.exp(jnp.sum(l[0] * l[1])) - jnp.exp(jnp.sum(l[2] * l[3])) + lam_init

def mixer_projections(x, norm_g, w_in, q_g, k_g):
    B, T, _ = x.shape
    z = rms_norm(x, norm_g) @ w_in
    widths = [ATT_WIDTH] * 3 + [MLSTM_WIDTH] * 3 + [N_HEADS_M]
    offs = []
    acc = 0
    for w in widths:
        acc += w
        offs.append(acc)
    qa, ka, va, u, vm, og, gi, gf = jnp.split(z, offs, axis=-1)
    qa = rms_norm(qa.reshape(B, T, N_HEADS_A, 2, HEAD_DIM_A), q_g)
    ka = rms_norm(ka.reshape(B, T, N_HEADS_A, 2, HEAD_DIM_A), k_g)
    va = va.reshape(B, T, N_HEADS_A, V_DIM_A)
    return qa, ka, va, u, vm, og, gi, gf

def diff_attend(q, k, v, q_pos, k_pos, lam, slopes):
    s = jnp.einsum("bqhmd,bkhmd->bhmqk", q, k, preferred_element_type=jnp.float32) * (HEAD_DIM_A ** -0.5)
    dist = q_pos[:, None] - k_pos[None, :]
    bias = -slopes[:, None, None] * dist.astype(jnp.float32)[None]
    s = jnp.where((dist >= 0)[None, None, None], s + bias[None, :, None], -jnp.inf)
    p = jax.nn.softmax(s, axis=-1)
    a = p[:, :, 0] - lam * p[:, :, 1]
    return jnp.einsum("bhqk,bkhd->bqhd", a.astype(v.dtype), v)

def prompt_attention(qa, ka, va, lam, slopes):
    B, T = qa.shape[:2]
    pos = jnp.arange(T)
    out_meta = diff_attend(qa[:, :N_META], ka[:, :N_META], va[:, :N_META], pos[:N_META], pos[:N_META], lam, slopes)
    n_blk = (T - N_META) // Q_BLOCK
    q_blocks = jnp.moveaxis(qa[:, N_META:].reshape(B, n_blk, Q_BLOCK, N_HEADS_A, 2, HEAD_DIM_A), 1, 0)
    p_blocks = pos[N_META:].reshape(n_blk, Q_BLOCK)
    out_blocks = lax.map(lambda qp: diff_attend(qp[0], ka, va, qp[1], pos, lam, slopes), (q_blocks, p_blocks))
    out_real = jnp.moveaxis(out_blocks, 0, 1).reshape(B, T - N_META, N_HEADS_A, V_DIM_A)
    return jnp.concatenate([out_meta, out_real], axis=1)

def mlstm_features(u, vm, gi, gf, conv_buf, conv_w, conv_b, w_qm, w_km, gate_bias):
    B, T, _ = u.shape
    up = jnp.concatenate([conv_buf.astype(u.dtype), u], axis=1)
    conv = conv_b
    for j in range(CONV_W):
        conv = conv + up[:, j:j + T] * conv_w[j]
    ua = jax.nn.silu(conv).reshape(B, T, N_HEADS_M, HEAD_DIM_M)
    q = jnp.einsum("bthd,hde->bthe", ua, w_qm).astype(jnp.float32)
    k = (jnp.einsum("bthd,hde->bthe", ua, w_km) * HEAD_DIM_M ** -0.5).astype(jnp.float32)
    v = vm.reshape(B, T, N_HEADS_M, HEAD_DIM_M).astype(jnp.float32)
    ig = (gi + gate_bias[0]).astype(jnp.float32)
    lf = jax.nn.log_sigmoid((gf + gate_bias[1]).astype(jnp.float32))
    return (q, k, v, ig, lf), up[:, -(CONV_W - 1):]

def mlstm_chunk(state, feats):
    C0, n0, m0 = state
    q, k, v, ig, lf = feats
    L = q.shape[1]
    b = jnp.moveaxis(jnp.cumsum(lf, axis=1), 1, -1)
    i_ = jnp.moveaxis(ig, 1, -1)
    causal = jnp.tril(jnp.ones((L, L), dtype=bool))
    d = jnp.where(causal, b[..., :, None] - b[..., None, :] + i_[..., None, :], -jnp.inf)
    inter = b + m0[..., None]
    m = jnp.maximum(inter, jnp.max(d, axis=-1))
    w_inter = jnp.exp(inter - m)
    s = jnp.einsum("bthd,bshd->bhts", q, k) * jnp.exp(d - m[..., None])
    num = w_inter[..., None] * jnp.einsum("bthd,bhde->bhte", q, C0) + jnp.einsum("bhts,bshe->bhte", s, v)
    den = w_inter * jnp.einsum("bthd,bhd->bht", q, n0) + jnp.sum(s, axis=-1)
    h = num / jnp.maximum(jnp.abs(den), jnp.exp(-m))[..., None]
    m_end = m[..., -1]
    w_c = jnp.exp(b[..., -1] + m0 - m_end)
    w_s = jnp.exp(b[..., -1:] - b + i_ - m_end[..., None])
    C = w_c[..., None, None] * C0 + jnp.einsum("bhs,bshd,bshe->bhde", w_s, k, v)
    n = w_c[..., None] * n0 + jnp.einsum("bhs,bshd->bhd", w_s, k)
    return (C, n, m_end), jnp.moveaxis(h, 1, 2)

def prompt_mlstm(feats):
    q = feats[0]
    B = q.shape[0]
    state = (jnp.zeros((B, N_HEADS_M, HEAD_DIM_M, HEAD_DIM_M), jnp.float32),
             jnp.zeros((B, N_HEADS_M, HEAD_DIM_M), jnp.float32),
             jnp.zeros((B, N_HEADS_M), jnp.float32))
    state, h_meta = mlstm_chunk(state, tuple(a[:, :N_META] for a in feats))
    def to_chunks(a):
        r = a[:, N_META:]
        nc = r.shape[1] // CHUNK
        return jnp.moveaxis(r.reshape(B, nc, CHUNK, *r.shape[2:]), 1, 0)
    state, h_chunks = lax.scan(mlstm_chunk, state, tuple(to_chunks(a) for a in feats))
    h_real = jnp.moveaxis(h_chunks, 0, 1).reshape(B, -1, N_HEADS_M, HEAD_DIM_M)
    return jnp.concatenate([h_meta, h_real], axis=1), state

def mlstm_output(h, og, g):
    B, T = h.shape[:2]
    hn = rms_norm(h, g)
    o = jax.nn.sigmoid(og.astype(jnp.float32)).reshape(B, T, N_HEADS_M, HEAD_DIM_M)
    return (hn * o).reshape(B, T, MLSTM_WIDTH).astype(og.dtype)

def finish_layer(x, a_heads, m_out, lam_init, attn_out_norm, w_out, norm_ffn, w_up, w_down):
    B, T, _ = x.shape
    a = (rms_norm(a_heads, attn_out_norm) * (1.0 - lam_init)).reshape(B, T, ATT_WIDTH)
    x = x + jnp.concatenate([a.astype(x.dtype), m_out.astype(x.dtype)], axis=-1) @ w_out
    hf = rms_norm(x, norm_ffn) @ w_up
    return x + jnp.square(jax.nn.relu(hf)) @ w_down

def setup_inputs(seed: int = 0) -> dict:
    key = jax.random.key(seed)
    ks = jax.random.split(key, 28)
    n_pages = PAST_LEN // PAGE_SIZE
    n_pool = (DEC_BATCH * n_pages * 5) // 4
    def nrm(k, shape, scale=1.0):
        return jax.random.normal(k, shape, jnp.float32) * scale
    perm = jax.random.permutation(ks[8], n_pool)
    page_table = perm[: DEC_BATCH * n_pages].reshape(DEC_BATCH, n_pages).astype(jnp.int32)
    return {
        "x_prompt": nrm(ks[0], (BATCH, SEQ, D_MODEL)),
        "x_sample": nrm(ks[1], (DEC_BATCH, DEC_SEQ, D_MODEL)),
        "cache_k": nrm(ks[2], (DEPTH, n_pool, PAGE_SIZE, N_HEADS_A, 2 * HEAD_DIM_A)),
        "cache_v": nrm(ks[3], (DEPTH, n_pool, PAGE_SIZE, N_HEADS_A, V_DIM_A)),
        "state_C": nrm(ks[4], (DEPTH, DEC_BATCH, N_HEADS_M, HEAD_DIM_M, HEAD_DIM_M), 0.5),
        "state_n": nrm(ks[5], (DEPTH, DEC_BATCH, N_HEADS_M, HEAD_DIM_M), 0.5),
        "state_m": 1.0 + nrm(ks[6], (DEPTH, DEC_BATCH, N_HEADS_M), 0.5),
        "state_conv": nrm(ks[7], (DEPTH, DEC_BATCH, CONV_W - 1, MLSTM_WIDTH)),
        "page_table": page_table,
        "meta_tokens": nrm(ks[9], (N_META, D_MODEL)),
        "norm_mix": 1.0 + nrm(ks[10], (DEPTH, D_MODEL), 0.02),
        "w_in": nrm(ks[11], (DEPTH, D_MODEL, PROJ_WIDTH), D_MODEL ** -0.5),
        "q_norm": 1.0 + nrm(ks[12], (DEPTH, HEAD_DIM_A), 0.02),
        "k_norm": 1.0 + nrm(ks[13], (DEPTH, HEAD_DIM_A), 0.02),
        "lambda_qk": nrm(ks[14], (DEPTH, 4, HEAD_DIM_A), 0.1),
        "attn_out_norm": 1.0 + nrm(ks[15], (DEPTH, V_DIM_A), 0.02),
        "conv_w": nrm(ks[16], (DEPTH, CONV_W, MLSTM_WIDTH), CONV_W ** -0.5),
        "conv_b": nrm(ks[17], (DEPTH, MLSTM_WIDTH), 0.02),
        "w_qm": nrm(ks[18], (DEPTH, N_HEADS_M, HEAD_DIM_M, HEAD_DIM_M), HEAD_DIM_M ** -0.5),
        "w_km": nrm(ks[19], (DEPTH, N_HEADS_M, HEAD_DIM_M, HEAD_DIM_M), HEAD_DIM_M ** -0.5),
        "gate_bias": jnp.stack([nrm(ks[20], (DEPTH, N_HEADS_M), 0.1),
                                FORGET_BIAS + nrm(ks[21], (DEPTH, N_HEADS_M), 0.1)], axis=1),
        "mlstm_out_norm": 1.0 + nrm(ks[22], (DEPTH, HEAD_DIM_M), 0.02),
        "w_out": nrm(ks[23], (DEPTH, D_MODEL, D_MODEL), D_MODEL ** -0.5),
        "norm_ffn": 1.0 + nrm(ks[24], (DEPTH, D_MODEL), 0.02),
        "w_up": nrm(ks[25], (DEPTH, D_MODEL, D_FF), D_MODEL ** -0.5),
        "w_down": nrm(ks[26], (DEPTH, D_FF, D_MODEL), D_FF ** -0.5),
    }

def reference(x_prompt, x_sample, cache_k, cache_v, state_C, state_n, state_m, state_conv, page_table,
              meta_tokens, norm_mix, w_in, q_norm, k_norm, lambda_qk, attn_out_norm, conv_w, conv_b,
              w_qm, w_km, gate_bias, mlstm_out_norm, w_out, norm_ffn, w_up, w_down):
    slopes = alibi_slopes()
    B, S, _ = x_prompt.shape
    Bd, Ts, _ = x_sample.shape
    past_len = page_table.shape[1] * PAGE_SIZE
    T = S + N_META
    xp = jnp.concatenate([jnp.broadcast_to(meta_tokens.astype(x_prompt.dtype)[None], (B, N_META, D_MODEL)), x_prompt], axis=1)
    xs = x_sample
    pos_q_s = past_len + jnp.arange(Ts)
    pos_k_s = jnp.arange(past_len + Ts)
    kp, vp, Cp, np_, mp, cp = [], [], [], [], [], []
    ksl, vsl, Csl, nsl, msl, csl = [], [], [], [], [], []
    for l in range(DEPTH):
        lam_init = 0.8 - 0.6 * math.exp(-0.3 * l)
        lam = diff_lambda(lambda_qk[l], lam_init)
        qa, ka, va, u, vm, og, gi, gf = mixer_projections(xp, norm_mix[l], w_in[l], q_norm[l], k_norm[l])
        a_p = prompt_attention(qa, ka, va, lam, slopes)
        feats, conv_p = mlstm_features(u, vm, gi, gf, jnp.zeros((B, CONV_W - 1, MLSTM_WIDTH), u.dtype),
                                       conv_w[l], conv_b[l], w_qm[l], w_km[l], gate_bias[l])
        h_p, (C_p, n_p, m_p) = prompt_mlstm(feats)
        xp = finish_layer(xp, a_p, mlstm_output(h_p, og, mlstm_out_norm[l]), lam_init,
                          attn_out_norm[l], w_out[l], norm_ffn[l], w_up[l], w_down[l])
        kp.append(ka.reshape(B, T, N_HEADS_A, 2 * HEAD_DIM_A))
        vp.append(va)
        Cp.append(C_p)
        np_.append(n_p)
        mp.append(m_p)
        cp.append(conv_p)
        qs, kss, vs, us, vms, ogs, gis, gfs = mixer_projections(xs, norm_mix[l], w_in[l], q_norm[l], k_norm[l])
        past_k = cache_k[l, page_table].reshape(Bd, past_len, N_HEADS_A, 2, HEAD_DIM_A)
        past_v = cache_v[l, page_table].reshape(Bd, past_len, N_HEADS_A, V_DIM_A)
        k_all = jnp.concatenate([past_k.astype(kss.dtype), kss], axis=1)
        v_all = jnp.concatenate([past_v.astype(vs.dtype), vs], axis=1)
        a_s = diff_attend(qs, k_all, v_all, pos_q_s, pos_k_s, lam, slopes)
        feats_s, conv_s = mlstm_features(us, vms, gis, gfs, state_conv[l], conv_w[l], conv_b[l],
                                         w_qm[l], w_km[l], gate_bias[l])
        st = (state_C[l].astype(jnp.float32), state_n[l].astype(jnp.float32), state_m[l].astype(jnp.float32))
        (C_s, n_s, m_s), h_s = mlstm_chunk(st, feats_s)
        xs = finish_layer(xs, a_s, mlstm_output(h_s, ogs, mlstm_out_norm[l]), lam_init,
                          attn_out_norm[l], w_out[l], norm_ffn[l], w_up[l], w_down[l])
        ksl.append(kss.reshape(Bd, Ts, N_HEADS_A, 2 * HEAD_DIM_A))
        vsl.append(vs)
        Csl.append(C_s)
        nsl.append(n_s)
        msl.append(m_s)
        csl.append(conv_s)
    y_prompt = xp[:, N_META:]
    y_sample = xs
    return (y_prompt, y_sample,
            jnp.stack(kp), jnp.stack(vp), jnp.stack(Cp), jnp.stack(np_), jnp.stack(mp), jnp.stack(cp),
            jnp.stack(ksl), jnp.stack(vsl), jnp.stack(Csl), jnp.stack(nsl), jnp.stack(msl), jnp.stack(csl))


_drawn_inputs = setup_inputs


def setup_inputs(seed=0):
    import zlib

    import numpy as np

    out = dict(_drawn_inputs(seed))
    spreads = {}
    factors = {'q_norm': 6.061,
     'k_norm': 2.809,
     'attn_out_norm': 5.543,
     'mlstm_out_norm': 8.0,
     'norm_ffn': 3.432}
    for name, (base, spread) in spreads.items():
        noise = np.random.default_rng([zlib.crc32(name.encode()), seed]).standard_normal(out[name].shape)
        drawn = base * np.exp(spread * noise) if base else spread * noise
        out[name] = __import__('jax').numpy.asarray(drawn.astype(out[name].dtype))
    for name, factor in factors.items():
        out[name] = (out[name] * factor).astype(out[name].dtype)
    return out
```

```python
from contextlib import ExitStack, contextmanager
import math

import concourse.bass as bass
from concourse import mybir

F32 = mybir.dt.float32
F32R = mybir.dt.float32r
I32 = mybir.dt.int32
ALU = mybir.AluOpType
ACT = mybir.ActivationFunctionType
AX = mybir.AxisListType.X

P = 128
N_META = 16
EPS = 1e-6
FILL = -1.0e30
LAM_INIT = 0.8 - 0.6 * math.exp(-0.3 * 0)


class Dims:

    def __init__(self, a):
        _, self.seq, self.dm = a["x_prompt"].shape
        self.nb, self.ns, _ = a["x_sample"].shape
        _, self.pool, self.page, self.ha, self.vd = a["cache_k"].shape
        self.hd = self.vd // 2
        self.pages = a["page_table"].shape[1]
        _, _, self.hm, self.md, _ = a["state_C"].shape
        self.aw = self.ha * self.vd
        self.mw = self.hm * self.md
        self.ff = a["w_up"].shape[2]
        self.pw = a["w_in"].shape[2]
        self.tp = self.seq + N_META
        self.tsmp = self.nb * self.ns
        self.t = self.tp + self.tsmp
        self.kc = self.dm // P
        self.tt = 112
        self.nt = self.t // self.tt
        self.half = self.t // 2
        assert self.nt * self.tt == self.t and self.kc * P == self.dm and self.half <= 512


class Flow:

    RAW = 4
    SPLIT = 2

    def __init__(self, nc, ctx, d, tag, sems):
        sb = lambda n, s, t: ctx.enter_context(nc.sbuf_tensor(f"{tag}_{n}", s, t))
        self.raw = sb("raw", [P, self.RAW, 16 * P], F32)
        self.hi = sb("hi", [P, self.SPLIT, 16 * P], F32R)
        self.lo = sb("lo", [P, self.SPLIT, 16 * P], F32R)
        self.landed = [sems(f"{tag}_landed{i}") for i in range(self.RAW)]
        self.hi_made = sems(f"{tag}_hi_made")
        self.lo_made = sems(f"{tag}_lo_made")
        self.used = sems(f"{tag}_used")


def exact_passes(nc, out, whi, wlo, xhi, xlo, first, last):
    nc.tensor.matmul(out, wlo, xhi, start=first, stop=False)
    nc.tensor.matmul(out, whi, xlo, start=False, stop=False)
    return nc.tensor.matmul(out, whi, xhi, start=False, stop=last)


@contextmanager
def stage(nc):
    with ExitStack() as ctx:
        made = []

        def sems(name):
            sem = ctx.enter_context(nc.semaphore(name))
            made.append(sem)
            return sem

        yield sems
        with nc.Block() as block:
            @block.sync
            def _(sp):
                for sem in made:
                    sp.sem_clear(sem)


class Consts:

    def __init__(self, nc, ctx, d):
        sb = lambda n, s, t=F32: ctx.enter_context(nc.sbuf_tensor(n, s, t))
        self.ident = sb("ident", [P, P])
        self.ones = sb("ones", [P, P])
        self.halves = sb("halves", [P, P])
        self.slopes = sb("slopes", [P, d.ha])
        self.neg_lam = sb("neg_lam", [P, 1])


def setup(nc, d, a, sems, c):
    with ExitStack() as ctx:
        sb = lambda n, s, t=F32: ctx.enter_context(nc.sbuf_tensor(n, s, t))
        lqk = sb("lqk", [1, 4, d.hd])
        prod = sb("lqk_prod", [1, 2, d.hd])
        dots = sb("lqk_dots", [1, 2])
        exps = sb("lqk_exps", [1, 2])
        lam = sb("lam", [1, 1])
        spread = ctx.enter_context(nc.psum_tensor("lam_spread", [P, 512], F32))
        filled, made, lqk_in = sems("consts_filled"), sems("consts_made"), sems("lqk_in")
        dotted, raised, lam_made, lam_spread, lam_done = (sems(n) for n in (
            "lam_dotted", "lam_raised", "lam_made", "lam_spread", "lam_done"))
        block = ctx.enter_context(nc.Block())

        @block.gpsimd
        def _(pool):
            nc.gpsimd.memset(c.ident[:, :], 0.0).then_inc(filled, 1)
            pool.wait_ge(filled, 1)
            nc.gpsimd.affine_select(out=c.ident[:, :], in_=c.ident[:, :], compare_op=ALU.not_equal, fill=1.0,
                                    base=0, pattern=[[-1, P]], channel_multiplier=1).then_inc(made, 1)
            nc.gpsimd.memset(c.halves[:, :], 0.0).then_inc(filled, 1)
            pool.wait_ge(filled, 2)
            for m in range(2):
                s = slice(m * d.hd, (m + 1) * d.hd)
                nc.gpsimd.memset(c.halves[s, s], 1.0 / d.hd).then_inc(made, 1)
                pool.wait_ge(made, 2 + m)
            for h in range(d.ha):
                nc.gpsimd.memset(c.slopes[:, h:h + 1], 2.0 ** (-8.0 * (h + 1) / d.ha)).then_inc(made, 1)
                pool.wait_ge(made, 4 + h)

        @block.sync
        def _(sp):
            sp.dma_start(lqk[:, :, :], a["lambda_qk"]).then_inc(lqk_in, 16)

        @block.vector
        def _(dve):
            nc.vector.memset(c.ones[:, :], 1.0).then_inc(dotted, 1)
            dve.wait_ge(lqk_in, 16)
            pairs = lqk[:, :, :].rearrange("o (a b) e -> o a b e", b=2)
            nc.vector.tensor_tensor(prod[:, :, :], pairs[:, :, 0, :], pairs[:, :, 1, :], ALU.mult).then_inc(dotted, 1)
            dve.wait_ge(dotted, 2)
            nc.vector.tensor_reduce(dots[:, :], prod[:, :, :], AX, ALU.add).then_inc(dotted, 1)
            dve.wait_ge(raised, 1)
            nc.vector.tensor_scalar(lam[:, :], exps[:, 0:1], exps[:, 1:2], LAM_INIT, ALU.subtract,
                                    ALU.add).then_inc(lam_made, 1)
            dve.wait_ge(lam_spread, 1)
            nc.vector.tensor_scalar(c.neg_lam[:, :], spread[:, 0:1], -1.0, None, ALU.mult).then_inc(lam_done, 1)
            dve.wait_ge(lam_done, 1)

        @block.scalar
        def _(act):
            act.wait_ge(dotted, 3)
            nc.scalar.activation(exps[:, :], dots[:, :], ACT.Exp).then_inc(raised, 1)

        @block.tensor
        def _(pe):
            pe.wait_ge(lam_made, 1)
            nc.tensor.matmul(spread[:, 0:1], c.ones[0:1, :], lam[:, :], start=True, stop=True).then_inc(lam_spread, 1)


def embed_and_norm(nc, d, a, sems, ident, xhi, xlo, xt_dram):
    with ExitStack() as ctx:
        sb = lambda n, s, t=F32: ctx.enter_context(nc.sbuf_tensor(n, s, t))
        rows = sb("x_rows", [d.tt, d.nt, d.dm])
        xt = sb("xt", [P, d.kc, d.t])
        gain = sb("norm_mix_cols", [P, d.kc])
        norm = NormBuffers(nc, ctx, d, sems, "mix")
        turned = [ctx.enter_context(nc.psum_tensor(f"x_turned{i}", [P, 2, 512], F32)) for i in range(2)]
        rows_in, gain_in = sems("x_rows_in"), sems("norm_mix_in")
        turned_ready, xt_ready, xt_stored = sems("x_turned_ready"), sems("xt_ready"), sems("xt_stored")
        split = 4 * d.tt
        n_last = d.seq - 4 * d.tt + N_META
        block = ctx.enter_context(nc.Block())

        @block.sync
        def _(sp):
            x = a["x_prompt"][0]
            head = d.tt - N_META
            sp.dma_start(rows[0:N_META, 0, :], a["meta_tokens"]).then_inc(rows_in, 16)
            sp.dma_start(rows[N_META:d.tt, 0, :], x[0:head, :]).then_inc(rows_in, 16)
            for t in range(1, d.nt - 1):
                r0 = head + (t - 1) * d.tt
                sp.dma_start(rows[:, t, :], x[r0:r0 + d.tt, :]).then_inc(rows_in, 16)
            sp.dma_start(rows[0:n_last, d.nt - 1, :], x[d.seq - n_last:d.seq, :]).then_inc(rows_in, 16)
            sp.dma_start(rows[n_last:d.tt, d.nt - 1, :],
                         a["x_sample"].rearrange("b s m -> (b s) m")).then_inc(rows_in, 16)
            sp.dma_start(gain[:, :], a["norm_mix"][0].rearrange("(k p) -> p k", p=P),
                         allow_slow_non_contiguous=True).then_inc(gain_in, 16)
            sp.wait_ge(xt_ready, 2 * d.kc)
            sp.dma_start(xt_dram.rearrange("(k p) t -> p k t", p=P), xt[:, :, :]).then_inc(xt_stored, 16)
            sp.wait_ge(xt_stored, 16)

        @block.tensor
        def _(pe):
            pe.wait_ge(rows_in, 16 * (d.nt + 2))
            for k in range(d.kc):
                if k >= 2:
                    pe.wait_ge(xt_ready, 2 * (k - 1))
                for t in range(d.nt):
                    out = turned[k % 2][:, t // 4, (t % 4) * d.tt:(t % 4 + 1) * d.tt]
                    mm = nc.tensor.transpose(out, rows[:, t, k * P:(k + 1) * P], ident[0:d.tt, 0:d.tt])
                mm.then_inc(turned_ready, 1)
            norm_tensor(nc, pe, d, norm)

        @block.scalar
        def _(act):
            norm_scalar(nc, act, d, norm, xhi)

        @block.vector
        def _(dve):
            for k in range(d.kc):
                dve.wait_ge(turned_ready, k + 1)
                nc.vector.tensor_copy(xt[:, k, 0:split], turned[k % 2][:, 0, 0:split]).then_inc(xt_ready, 1)
                nc.vector.tensor_copy(xt[:, k, split:d.t],
                                      turned[k % 2][:, 1, 0:d.t - split]).then_inc(xt_ready, 1)
            dve.wait_ge(xt_ready, 2 * d.kc)
            dve.wait_ge(gain_in, 16)
            norm_vector(nc, dve, d, norm, xt, gain, xhi, xlo)


class NormBuffers:

    def __init__(self, nc, ctx, d, sems, tag):
        sb = lambda n, s, t=F32: ctx.enter_context(nc.sbuf_tensor(f"{tag}_{n}", s, t))
        self.sq = sb("sq", [P, 2, d.t])
        self.mean = [ctx.enter_context(nc.psum_tensor(f"{tag}_mean{i}", [P, 512], F32)) for i in range(2)]
        self.over = sb("over_width", [P, P])
        self.root = sb("root", [P, d.t])
        self.rstd = sb("rstd", [P, d.t])
        self.xn = sb("xn", [P, 2, d.t])
        self.ready = sems(f"{tag}_over_ready")
        self.squared = sems(f"{tag}_squared")
        self.summed = sems(f"{tag}_summed")
        self.meaned = sems(f"{tag}_meaned")
        self.rooted = sems(f"{tag}_rooted")
        self.inverted = sems(f"{tag}_inverted")
        self.scaled = sems(f"{tag}_scaled")
        self.hi_made = sems(f"{tag}_xhi_made")
        self.lo_made = sems(f"{tag}_xlo_made")


def norm_tensor(nc, pe, d, n):
    for k in range(d.kc):
        pe.wait_ge(n.squared, k + 2)
        for h in range(2):
            mm = nc.tensor.matmul(n.mean[h][:, 0:d.half], n.over[:, :],
                                  n.sq[:, k % 2, h * d.half:(h + 1) * d.half],
                                  start=(k == 0), stop=(k == d.kc - 1))
        mm.then_inc(n.summed, 1)


def norm_scalar(nc, act, d, n, xhi):
    act.wait_ge(n.meaned, 2)
    nc.scalar.activation(n.root[:, :], n.root[:, :], ACT.Sqrt).then_inc(n.rooted, 1)
    for k in range(d.kc):
        act.wait_ge(n.scaled, k + 1)
        nc.scalar.activation(xhi[:, k, :], n.xn[:, k % 2, :], ACT.Copy).then_inc(n.hi_made, 1)


def norm_vector(nc, dve, d, n, xt, gain, xhi, xlo):
    nc.vector.memset(n.over[:, :], 1.0 / d.dm).then_inc(n.squared, 1)
    for k in range(d.kc):
        if k >= 2:
            dve.wait_ge(n.summed, k - 1)
        nc.vector.tensor_tensor(n.sq[:, k % 2, :], xt[:, k, :], xt[:, k, :], ALU.mult).then_inc(n.squared, 1)
    dve.wait_ge(n.summed, d.kc)
    for h in range(2):
        nc.vector.tensor_scalar(n.root[:, h * d.half:(h + 1) * d.half], n.mean[h][:, 0:d.half],
                                EPS, None, ALU.add).then_inc(n.meaned, 1)
    dve.wait_ge(n.rooted, 1)
    nc.vector.reciprocal(n.rstd[:, :], n.root[:, :]).then_inc(n.inverted, 1)
    dve.wait_ge(n.inverted, 1)
    for k in range(d.kc):
        if k >= 2:
            dve.wait_ge(n.lo_made, k - 1)
        nc.vector.scalar_tensor_tensor(n.xn[:, k % 2, :], xt[:, k, :], gain[:, k:k + 1], n.rstd[:, :],
                                       ALU.mult, ALU.mult).then_inc(n.scaled, 1)
        if k >= 1:
            norm_trailing(nc, dve, n, xhi, xlo, k - 1)
    norm_trailing(nc, dve, n, xhi, xlo, d.kc - 1)


def norm_trailing(nc, dve, n, xhi, xlo, k):
    dve.wait_ge(n.hi_made, k + 1)
    nc.vector.tensor_tensor(xlo[:, k, :], n.xn[:, k % 2, :], xhi[:, k, :].bitcast(F32),
                            ALU.subtract).then_inc(n.lo_made, 1)


def input_projection(nc, d, a, sems, xhi, xlo, z_dram):
    n_tiles = (d.pw - 2 * d.hm) // P
    ng = 2 * d.hm
    GROUP = Flow.RAW
    with ExitStack() as ctx:
        sb = lambda n, s, t=F32: ctx.enter_context(nc.sbuf_tensor(n, s, t))
        flow = Flow(nc, ctx, d, "win", sems)
        zc = sb("z_out", [P, GROUP, d.t])
        gate_raw, gate_hi, gate_lo = sb("gate_raw", [P, d.kc, ng]), sb("gate_hi", [P, d.kc, ng], F32R), \
            sb("gate_lo", [P, d.kc, ng], F32R)
        acc = [[ctx.enter_context(nc.psum_tensor(f"z_acc{i}{h}", [P, 512], F32)) for h in range(2)]
               for i in range(2)]
        copied = sems("z_copied")
        stored = [sems(f"z_stored{i}") for i in range(GROUP)]
        gate_in = sems("gate_in")
        w = a["w_in"][0].rearrange("(k p) n -> p k n", p=P)
        raw = [flow.raw[:, j, :].rearrange("p (k n) -> p k n", k=d.kc) for j in range(GROUP)]
        hi = [flow.hi[:, j, :].rearrange("p (k n) -> p k n", k=d.kc) for j in range(2)]
        lo = [flow.lo[:, j, :].rearrange("p (k n) -> p k n", k=d.kc) for j in range(2)]
        z_rows = z_dram[0:n_tiles * P, :].rearrange("(c p) t -> c p t", p=P)
        block = ctx.enter_context(nc.Block())

        @block.sync
        def _(sp):
            for j in range(GROUP):
                sp.dma_start(raw[j], w[:, :, j * P:(j + 1) * P]).then_inc(flow.landed[j], 16)
            sp.dma_start(gate_raw[:, :, :], w[:, :, n_tiles * P:d.pw]).then_inc(gate_in, 16)
            with sp.Fori(0, n_tiles // GROUP - 1) as g:
                i = g * GROUP
                for j in range(GROUP):
                    sp.wait_ge(flow.lo_made, i + j + 1)
                    sp.dma_start(raw[j], w[:, :, bass.ds((i + GROUP + j) * P, P)]).then_inc(flow.landed[j], 16)
                    sp.wait_ge(copied, 2 * (i + j) + 2)
                    sp.dma_start(z_rows[i + j], zc[:, j, :]).then_inc(stored[j], 16)
            for j in range(GROUP):
                n = n_tiles - GROUP + j
                sp.wait_ge(copied, 2 * n + 2)
                sp.dma_start(z_rows[n], zc[:, j, :]).then_inc(stored[j], 16)
            sp.wait_ge(copied, 2 * n_tiles + 2)
            sp.dma_start(z_dram[n_tiles * P:n_tiles * P + ng, :], zc[0:ng, 0, :]).then_inc(stored[0], 16)
            sp.wait_ge(stored[0], 16 * (n_tiles // GROUP + 1))
            for j in range(1, GROUP):
                sp.wait_ge(stored[j], 16 * (n_tiles // GROUP))

        def act_group(act, i, first):
            for j in range(GROUP):
                act.wait_ge(flow.landed[j], i * (16 // GROUP) + 16)
                if not (first and j < 2):
                    act.wait_ge(flow.used, i + j - 1)
                nc.scalar.activation(flow.hi[:, j % 2, :], flow.raw[:, j, :], ACT.Copy).then_inc(flow.hi_made, 1)

        @block.scalar
        def _(act):
            act_group(act, 0, True)
            with act.Fori(1, n_tiles // GROUP) as g:
                act_group(act, g * GROUP, False)
            act.wait_ge(gate_in, 16)
            nc.scalar.activation(gate_hi[:, :, :], gate_raw[:, :, :], ACT.Copy).then_inc(flow.hi_made, 1)

        def dve_copy_out(dve, n, j, rows=P):
            dve.wait_ge(flow.used, n + 1)
            for h in range(2):
                nc.vector.tensor_copy(zc[0:rows, j, h * d.half:(h + 1) * d.half],
                                      acc[j % 2][h][0:rows, 0:d.half]).then_inc(copied, 1)

        def dve_group(dve, i, nth):
            for j in range(GROUP):
                dve.wait_ge(flow.hi_made, i + j + 1)
                nc.vector.tensor_tensor(flow.lo[:, j % 2, :], flow.raw[:, j, :],
                                        flow.hi[:, j % 2, :].bitcast(F32), ALU.subtract).then_inc(flow.lo_made, 1)
                if nth + (j > 0) >= 2:
                    dve.wait_ge(stored[(j - 1) % GROUP], i * (16 // GROUP) - (16 if j == 0 else 0))
                if nth + (j > 0) >= 1:
                    dve_copy_out(dve, i + j - 1, (j - 1) % GROUP)

        @block.vector
        def _(dve):
            dve_group(dve, 0, 0)
            dve_group(dve, GROUP, 1)
            with dve.Fori(2, n_tiles // GROUP) as g:
                dve_group(dve, g * GROUP, 2)
            dve.wait_ge(flow.hi_made, n_tiles + 1)
            nc.vector.tensor_tensor(gate_lo[:, :, :], gate_raw[:, :, :], gate_hi[:, :, :].bitcast(F32),
                                    ALU.subtract).then_inc(flow.lo_made, 1)
            dve.wait_ge(stored[GROUP - 1], 16 * (n_tiles // GROUP - 1))
            dve_copy_out(dve, n_tiles - 1, GROUP - 1)
            dve.wait_ge(stored[0], 16 * (n_tiles // GROUP))
            dve_copy_out(dve, n_tiles, 0, ng)

        def pe_tile(pe, n, j, whi, wlo, rows=P, first=False):
            pe.wait_ge(flow.lo_made, n + 1)
            if not first:
                pe.wait_ge(copied, 2 * n - 2)
            for h in range(2):
                cols = slice(h * d.half, (h + 1) * d.half)
                for k in range(d.kc):
                    mm = exact_passes(nc, acc[j % 2][h][0:rows, 0:d.half], whi[:, k, :], wlo[:, k, :],
                                      xhi[:, k, cols], xlo[:, k, cols], k == 0, k == d.kc - 1)
            mm.then_inc(flow.used, 1)

        @block.tensor
        def _(pe):
            for j in range(2):
                pe_tile(pe, j, j, hi[j], lo[j], first=True)
            with pe.Fori(1, n_tiles // 2) as g:
                for j in range(2):
                    pe_tile(pe, g * 2 + j, j, hi[j], lo[j])
            pe_tile(pe, n_tiles, 0, gate_hi[:, :, :], gate_lo[:, :, :], ng)


def heads_prepare(nc, d, a, sems, c, z_dram, zn_dram, k_rows, v_rows, ks_rows, vs_rows):
    TT, LAST = d.tt, d.tp - 4 * d.tt
    with ExitStack() as ctx:
        sb = lambda n, s, t=F32: ctx.enter_context(nc.sbuf_tensor(n, s, t))
        z = [sb(f"zqkv{s}", [P, 3, d.t]) for s in range(2)]
        sq = [sb(f"qk_sq{s}", [P, 4, d.half]) for s in range(2)]
        root = [sb(f"qk_root{s}", [P, 4, d.half]) for s in range(2)]
        gains = sb("qk_gains", [P, 2])
        rows = [[sb(f"kv_rows{s}{w}", [TT, 5, P]) for w in range(2)] for s in range(2)]
        srow = [[sb(f"kv_srow{s}{w}", [d.tsmp, P]) for w in range(2)] for s in range(2)]
        mean = ctx.enter_context(nc.psum_tensor("qk_mean", [P, 4, 512], F32))
        turned = [ctx.enter_context(nc.psum_tensor(f"kv_turned{w}", [P, 2, 512], F32)) for w in range(2)]
        gains_in = sems("qk_gains_in")
        landed = [sems(f"zqkv_in{s}") for s in range(2)]
        squared, meaned, rooting, rooted, inverted, normed, turned_ready, rows_a, rows_b = (sems(n) for n in (
            "qk_squared", "qk_meaned", "qk_rooting", "qk_rooted", "qk_inverted", "qk_normed", "kv_turned_ready",
            "kv_rows_a", "kv_rows_b"))
        stored = [sems(f"kv_stored{s}") for s in range(2)]
        STORES = 7
        zh = z_dram[0:3 * d.aw, :].rearrange("(w h p) t -> h p w t", w=3, p=P)
        znh = zn_dram.rearrange("(w h p) t -> h p w t", w=2, p=P)
        krow = [x[0:4 * TT, :].rearrange("(t p) (h e) -> h p t e", p=TT, e=P) for x in (k_rows, v_rows)]
        klast = [x[4 * TT:d.tp, :].rearrange("p (h e) -> h p e", e=P) for x in (k_rows, v_rows)]
        ksmp = [x.rearrange("p (h e) -> h p e", e=P) for x in (ks_rows, vs_rows)]
        block = ctx.enter_context(nc.Block())

        def sync_head(sp, g, s, more):
            h = g * 2 + s
            sp.wait_ge(normed, 2 * h + 2)
            sp.dma_start(znh[h], z[s][:, 0:2, :]).then_inc(stored[s], 16)
            sp.wait_ge(rows_b, 2 * h + 2)
            sp.wait_ge(rows_a, 2 * h + 2)
            for w in range(2):
                sp.dma_start(krow[w][h], rows[s][w][:, 0:4, :]).then_inc(stored[s], 16)
                sp.dma_start(klast[w][h], rows[s][w][0:LAST, 4, :]).then_inc(stored[s], 16)
                sp.dma_start(ksmp[w][h], srow[s][w][:, :]).then_inc(stored[s], 16)
            if more:
                sp.wait_ge(stored[s], g * (16 * STORES) + 16 * STORES)
                sp.dma_start(z[s][:, :, :], zh[h + 2]).then_inc(landed[s], 16)

        @block.sync
        def _(sp):
            for i, name in enumerate(("q_norm", "k_norm")):
                for m in range(2):
                    sp.dma_start(gains[m * d.hd:(m + 1) * d.hd, i:i + 1], a[name].rearrange("o e -> e o"),
                                 allow_slow_non_contiguous=True).then_inc(gains_in, 16)
            for s in range(2):
                sp.dma_start(z[s][:, :, :], zh[s]).then_inc(landed[s], 16)
            with sp.Fori(0, d.ha // 2 - 1) as g:
                for s in range(2):
                    sync_head(sp, g, s, True)
            for s in range(2):
                sync_head(sp, d.ha // 2 - 1, s, False)
            for s in range(2):
                sp.wait_ge(stored[s], 16 * STORES * (d.ha // 2))

        def dve_head(dve, g, s, first):
            h = g * 2 + s
            dve.wait_ge(landed[s], g * 16 + 16)
            nc.vector.tensor_tensor(sq[s][:, :, :], z[s][:, 0:2, :].rearrange("p w (b t) -> p (w b) t", b=2),
                                    z[s][:, 0:2, :].rearrange("p w (b t) -> p (w b) t", b=2),
                                    ALU.mult).then_inc(squared, 1)
            dve.wait_ge(meaned, h + 1)
            nc.vector.tensor_scalar(root[s][:, :, :], mean[:, :, 0:d.half], EPS, None, ALU.add).then_inc(rooting, 1)
            dve.wait_ge(rooted, h + 1)
            nc.vector.reciprocal(root[s][:, :, :], root[s][:, :, :]).then_inc(inverted, 1)
            dve.wait_ge(inverted, h + 1)
            for w in range(2):
                nc.vector.scalar_tensor_tensor(z[s][:, w, :], z[s][:, w, :], gains[:, w:w + 1],
                                               root[s][:, 2 * w:2 * w + 2, :].rearrange("p b t -> p (b t)"),
                                               ALU.mult, ALU.mult).then_inc(normed, 1)
            if not first:
                dve.wait_ge(stored[s], g * (16 * STORES))
            for w in range(2):
                dve.wait_ge(turned_ready, 2 * h + w + 1)
                nc.vector.tensor_copy(rows[s][w][0:LAST, 4, :], turned[w][0:LAST, 1, 0:P])
                nc.vector.tensor_copy(srow[s][w][:, :], turned[w][0:d.tsmp, 1, P:2 * P]).then_inc(rows_b, 1)

        @block.vector
        def _(dve):
            dve.wait_ge(gains_in, 64)
            for s in range(2):
                dve_head(dve, 0, s, True)
            with dve.Fori(1, d.ha // 2) as g:
                for s in range(2):
                    dve_head(dve, g, s, False)

        def act_head(act, g, s, first):
            h = g * 2 + s
            act.wait_ge(rooting, h + 1)
            nc.scalar.activation(root[s][:, :, :], root[s][:, :, :], ACT.Sqrt).then_inc(rooted, 1)
            if not first:
                act.wait_ge(stored[s], g * (16 * STORES))
            for w in range(2):
                act.wait_ge(turned_ready, 2 * h + w + 1)
                nc.scalar.activation(rows[s][w][:, 0:4, :],
                                     turned[w][0:TT, 0, :].rearrange("p (t e) -> p t e", e=P),
                                     ACT.Copy).then_inc(rows_a, 1)

        @block.scalar
        def _(act):
            for s in range(2):
                act_head(act, 0, s, True)
            with act.Fori(1, d.ha // 2) as g:
                for s in range(2):
                    act_head(act, g, s, False)

        def pe_head(pe, g, s, first):
            h = g * 2 + s
            pe.wait_ge(squared, h + 1)
            if not (first and s == 0):
                pe.wait_ge(rooting, h)
            for b in range(4):
                mm = nc.tensor.matmul(mean[:, b, 0:d.half], c.halves[:, :], sq[s][:, b, :], start=True, stop=True)
            mm.then_inc(meaned, 1)
            pe.wait_ge(normed, 2 * h + 2)
            if not (first and s == 0):
                pe.wait_ge(rows_a, 2 * h)
                pe.wait_ge(rows_b, 2 * h)
            for w in range(2):
                for t in range(4):
                    nc.tensor.transpose(turned[w][0:TT, 0, t * P:(t + 1) * P],
                                        z[s][:, 1 + w, t * TT:(t + 1) * TT], c.ident[:, :])
                nc.tensor.transpose(turned[w][0:LAST, 1, 0:P], z[s][:, 1 + w, 4 * TT:d.tp], c.ident[:, :])
                nc.tensor.transpose(turned[w][0:d.tsmp, 1, P:2 * P], z[s][:, 1 + w, d.tp:d.t],
                                    c.ident[:, :]).then_inc(turned_ready, 1)

        @block.tensor
        def _(pe):
            for s in range(2):
                pe_head(pe, 0, s, True)
            with pe.Fori(1, d.ha // 2) as g:
                for s in range(2):
                    pe_head(pe, g, s, False)


def prompt_attention(nc, d, a, sems, c, zn_dram, v_rows, mix):
    TT, NT, TP = d.tt, d.nt, d.tp
    EDGE = 3 * TT
    WIDE = NT * TT
    with ExitStack() as ctx:
        sb = lambda n, s, t=F32: ctx.enter_context(nc.sbuf_tensor(n, s, t))
        ps = lambda n, s: ctx.enter_context(nc.psum_tensor(n, s, F32))
        qk = [sb(f"at_qk{s}", [P, 2, TP]) for s in range(2)]
        v = [sb(f"at_v{s}", [TT, NT, P]) for s in range(2)]
        dist = sb("at_dist", [TT, WIDE])
        mask = sb("at_mask", [TT, WIDE])
        bias = [sb(f"at_bias{s}", [TT, WIDE]) for s in range(2)]
        sc = [[sb(f"at_sc{u}{m}", [TT, WIDE]) for m in range(2)] for u in range(2)]
        top = [sb(f"at_top{u}", [TT, 2]) for u in range(2)]
        low = [sb(f"at_low{u}", [TT, 2]) for u in range(2)]
        den = [sb(f"at_den{u}", [TT, 2]) for u in range(2)]
        inv = [sb(f"at_inv{u}", [TT, 2]) for u in range(2)]
        at = [sb(f"at_t{u}", [TT, NT, TT]) for u in range(2)]
        scores = [ps(f"at_scores{m}", [P, 2, 512]) for m in range(2)]
        turn = ps("at_turn", [P, 2, 512])
        outp = [ps(f"at_out{u}", [P, 512]) for u in range(2)]
        landed = [sems(f"at_landed{s}") for s in range(2)]
        dist_made, bias_made, scored, biased, topped, lowered, raised, inverted, scaled, mixed, turned, turned_out, \
            valued, placed = (sems(n) for n in (
                "at_dist_made", "at_bias_made", "at_scored", "at_biased", "at_topped", "at_lowered", "at_raised",
                "at_inverted", "at_scaled", "at_mixed", "at_turned", "at_turned_out", "at_valued", "at_placed"))
        znh = zn_dram.rearrange("(w h p) t -> h p w t", w=2, p=P)
        vh = v_rows[0:4 * TT, :].rearrange("(t p) (h e) -> h p t e", p=TT, e=P)
        vlast = v_rows[4 * TT:TP, :].rearrange("p (h e) -> h p e", e=P)
        LAST = TP - 4 * TT
        nq = [TT] * (NT - 1) + [LAST]
        keys = [min((t + 1) * TT, TP) for t in range(NT)]
        block = ctx.enter_context(nc.Block())

        def load(sp, h, s):
            sp.dma_start(qk[s][:, :, :], znh[h][:, :, 0:TP]).then_inc(landed[s], 16)
            sp.dma_start(v[s][:, 0:4, :], vh[h]).then_inc(landed[s], 16)
            sp.dma_start(v[s][0:LAST, 4, :], vlast[h]).then_inc(landed[s], 16)

        @block.sync
        def _(sp):
            for s in range(2):
                load(sp, s, s)
            with sp.Fori(0, d.ha // 2 - 1) as g:
                for s in range(2):
                    sp.wait_ge(valued, g * (2 * NT) + (s + 1) * NT)
                    load(sp, g * 2 + (s + 2), s)

        @block.gpsimd
        def _(pool):
            nc.gpsimd.iota(dist[:, :], pattern=[[1, WIDE]], base=-4 * TT, channel_multiplier=-1,
                           allow_small_or_imprecise_dtypes=True).then_inc(dist_made, 1)
            pool.wait_ge(dist_made, 1)
            nc.gpsimd.memset(mask[:, :], 0.0).then_inc(dist_made, 1)
            pool.wait_ge(dist_made, 2)
            nc.gpsimd.affine_select(out=mask[:, :], in_=mask[:, :], compare_op=ALU.is_ge, fill=FILL,
                                    base=4 * TT, pattern=[[-1, WIDE]], channel_multiplier=1).then_inc(dist_made, 1)

        def pe_scores(pe, g, s, t, skip):
            u, n = (s * NT + t) % 2, g * (2 * NT) + (s * NT + t)
            if t == 0:
                pe.wait_ge(landed[s], g * 48 + 48)
            for m in range(2):
                if not skip:
                    pe.wait_ge(biased, n * 2 - 1 + m)
                half = slice(m * d.hd, (m + 1) * d.hd)
                lhs = qk[s][half, 0, t * TT:t * TT + nq[t]]
                first = min(EDGE, keys[t])
                mm = nc.tensor.matmul(scores[m][0:nq[t], 0, 0:first], lhs, qk[s][half, 1, 0:first],
                                      start=True, stop=True)
                if keys[t] > EDGE:
                    mm = nc.tensor.matmul(scores[m][0:nq[t], 1, 0:keys[t] - EDGE], lhs,
                                          qk[s][half, 1, EDGE:keys[t]], start=True, stop=True)
                mm.then_inc(scored, 1)

        def pe_values(pe, g, s, t):
            u, n = (s * NT + t) % 2, g * (2 * NT) + (s * NT + t)
            pe.wait_ge(mixed, n + 1)
            if isinstance(n, int) and n == 0:
                pass
            else:
                pe.wait_ge(turned_out, n * 2)
            for j in range(t + 1):
                mm = nc.tensor.transpose(turn[0:nq[j], j // 4, (j % 4) * TT:(j % 4) * TT + nq[t]],
                                         sc[u][0][0:nq[t], j * TT:j * TT + nq[j]], c.ident[0:nq[t], 0:nq[t]])
            mm.then_inc(turned, 1)
            pe.wait_ge(turned_out, n * 2 + 2)
            if not (isinstance(n, int) and n < 2):
                pe.wait_ge(placed, n - 1)
            for j in range(t + 1):
                mm = nc.tensor.matmul(outp[u][:, 0:nq[t]], v[s][0:nq[j], j, :], at[u][0:nq[j], j, 0:nq[t]],
                                      start=(j == 0), stop=(j == t))
            mm.then_inc(valued, 1)

        def pairs(eng, run):
            def body(g, first):
                for s in range(2):
                    for t in range(NT):
                        run(g, s, t, first and s == 0 and t == 0)
            body(0, True)
            with eng.Fori(1, d.ha // 2) as g:
                body(g, False)

        def before(g, s, t):
            if t:
                return g, s, t - 1
            return (g, 0, NT - 1) if s else (g - 1, 1, NT - 1)

        @block.tensor
        def _(pe):
            def run(g, s, t, first):
                pe_scores(pe, g, s, t, first)
                if not first:
                    pe_values(pe, *before(g, s, t))
            pairs(pe, run)
            pe_values(pe, d.ha // 2 - 1, 1, NT - 1)

        def dve_scores(dve, g, s, t):
            u, n = (s * NT + t) % 2, g * (2 * NT) + (s * NT + t)
            if t == 0:
                nc.vector.scalar_tensor_tensor(bias[s][:, :], dist[:, :], c.slopes[0:TT, bass.ds(g * 2 + s, 1)],
                                               mask[:, :], ALU.mult, ALU.add).then_inc(bias_made, 1)
                dve.wait_ge(bias_made, g * 2 + s + 1)
            if not (isinstance(n, int) and n < 2):
                dve.wait_ge(turned, n - 1)
            b0 = (4 - t) * TT
            for m in range(2):
                dve.wait_ge(scored, n * 2 + m + 1)
                first = min(EDGE, keys[t])
                ins = nc.vector.scalar_tensor_tensor(sc[u][m][0:nq[t], 0:first], scores[m][0:nq[t], 0, 0:first],
                                                     d.hd ** -0.5, bias[s][0:nq[t], b0:b0 + first],
                                                     ALU.mult, ALU.add)
                if keys[t] > EDGE:
                    ins = nc.vector.scalar_tensor_tensor(
                        sc[u][m][0:nq[t], EDGE:keys[t]], scores[m][0:nq[t], 1, 0:keys[t] - EDGE], d.hd ** -0.5,
                        bias[s][0:nq[t], b0 + EDGE:b0 + keys[t]], ALU.mult, ALU.add)
                ins.then_inc(biased, 1)
                dve.wait_ge(biased, n * 2 + m + 1)
                nc.vector.tensor_reduce(top[u][0:nq[t], m:m + 1], sc[u][m][0:nq[t], 0:keys[t]], AX,
                                        ALU.max).then_inc(topped, 1)
            dve.wait_ge(topped, n * 2 + 2)
            nc.vector.tensor_scalar(low[u][0:nq[t], :], top[u][0:nq[t], :], -1.0, None, ALU.mult).then_inc(lowered, 1)

        def dve_mix(dve, g, s, t):
            u, n = (s * NT + t) % 2, g * (2 * NT) + (s * NT + t)
            dve.wait_ge(raised, n * 2 + 2)
            nc.vector.reciprocal(inv[u][0:nq[t], :], den[u][0:nq[t], :]).then_inc(inverted, 1)
            dve.wait_ge(inverted, n + 1)
            nc.vector.tensor_scalar(sc[u][1][0:nq[t], 0:keys[t]], sc[u][1][0:nq[t], 0:keys[t]],
                                    inv[u][0:nq[t], 1:2], c.neg_lam[0:nq[t], :], ALU.mult,
                                    ALU.mult).then_inc(scaled, 1)
            dve.wait_ge(scaled, n + 1)
            nc.vector.scalar_tensor_tensor(sc[u][0][0:nq[t], 0:keys[t]], sc[u][0][0:nq[t], 0:keys[t]],
                                           inv[u][0:nq[t], 0:1], sc[u][1][0:nq[t], 0:keys[t]],
                                           ALU.mult, ALU.add).then_inc(mixed, 1)

        @block.vector
        def _(dve):
            dve.wait_ge(dist_made, 3)

            def run(g, s, t, first):
                dve_scores(dve, g, s, t)
                if not first:
                    dve_mix(dve, *before(g, s, t))
            pairs(dve, run)
            dve_mix(dve, d.ha // 2 - 1, 1, NT - 1)

        def act_exp(act, g, s, t):
            u, n = (s * NT + t) % 2, g * (2 * NT) + (s * NT + t)
            act.wait_ge(lowered, n + 1)
            for m in range(2):
                nc.scalar.activation(sc[u][m][0:nq[t], 0:keys[t]], sc[u][m][0:nq[t], 0:keys[t]], ACT.Exp,
                                     bias=low[u][0:nq[t], m:m + 1],
                                     accum_out=den[u][0:nq[t], m:m + 1]).then_inc(raised, 1)

        def act_out(act, g, s, t):
            u, n = (s * NT + t) % 2, g * (2 * NT) + (s * NT + t)
            act.wait_ge(turned, n + 1)
            if not (isinstance(n, int) and n < 2):
                act.wait_ge(valued, n - 1)
            full = min(t + 1, 4) - (1 if t < 4 and nq[t] < TT else 0)
            for j0, j1, rows in ((0, full, TT), (4, t + 1, LAST)):
                if j0 < j1:
                    nc.scalar.activation(at[u][0:rows, j0:j1, 0:nq[t]],
                                         turn[0:rows, j0 // 4, 0:(j1 - j0) * TT].rearrange(
                                             "p (j q) -> p j q", q=TT)[:, :, 0:nq[t]],
                                         ACT.Copy).then_inc(turned_out, 1 if t == 4 else 2)
            act.wait_ge(valued, n + 1)
            nc.scalar.activation(mix[:, bass.ds(g * 2 + s, 1), t * TT:t * TT + nq[t]],
                                 outp[u][:, 0:nq[t]].rearrange("p (o q) -> p o q", o=1),
                                 ACT.Copy).then_inc(placed, 1)

        @block.scalar
        def _(act):
            def run(g, s, t, first):
                act_exp(act, g, s, t)
                if not first:
                    act_out(act, *before(g, s, t))
            pairs(act, run)
            act_out(act, d.ha // 2 - 1, 1, NT - 1)


G_SOURCE, G_NEGTOP, G_FLOOR, G_INTER = range(4)


def gates(nc, d, a, sems, z_dram, g_dram, m_prompt, m_sample):
    H, T, TP = d.hm, d.t, d.tp
    n_z = d.pw - 2 * H
    with ExitStack() as ctx:
        sb = lambda n, s, t=F32: ctx.enter_context(nc.sbuf_tensor(n, s, t))
        gi, gf, neg, mag, soft, lf, b, src, top, m, fl, it, ones = (sb(f"g_{n}", [H, T]) for n in (
            "i", "f", "neg", "mag", "soft", "lf", "b", "src", "top", "m", "floor", "inter", "ones"))
        m0 = sb("g_m0", [H, d.nb])
        gb = sb("g_bias", [H, 2])
        ins, step, sact, outs = sems("g_in"), sems("g_step"), sems("g_act"), sems("g_out")
        rows_ready = sems("g_rows_ready")
        smp = lambda x: x[:, TP:T].rearrange("h (b s) -> h b s", s=d.ns)
        block = ctx.enter_context(nc.Block())

        @block.sync
        def _(sp):
            sp.dma_start(gi[:, :], z_dram[n_z:n_z + H, :]).then_inc(ins, 16)
            sp.dma_start(gf[:, :], z_dram[n_z + H:n_z + 2 * H, :]).then_inc(ins, 16)
            sp.dma_start(m0[:, :], a["state_m"].rearrange("o b h -> h (o b)"),
                         allow_slow_non_contiguous=True).then_inc(ins, 16)
            sp.dma_start(gb[:, :], a["gate_bias"].rearrange("o w h -> h (o w)"),
                         allow_slow_non_contiguous=True).then_inc(ins, 16)
            sp.wait_ge(sact, 4)
            for row, x in ((G_SOURCE, src), (G_NEGTOP, neg), (G_FLOOR, fl), (G_INTER, it)):
                sp.dma_start(g_dram[row], x[:, :]).then_inc(outs, 16)
            sp.dma_start(m_prompt.rearrange("o b h -> h (o b)"), m[:, TP - 1:TP],
                         allow_slow_non_contiguous=True).then_inc(outs, 16)
            sp.dma_start(m_sample.rearrange("o b h -> h (o b)"), smp(m)[:, :, d.ns - 1],
                         allow_slow_non_contiguous=True).then_inc(outs, 16)
            sp.wait_ge(outs, 96)

        @block.vector
        def _(dve):
            n = [0]

            def done(instruction):
                instruction.then_inc(step, 1)
                n[0] += 1
                dve.wait_ge(step, n[0])

            V = nc.vector
            dve.wait_ge(ins, 64)
            done(V.memset(ones[:, :], 1.0))
            done(V.tensor_scalar(gi[:, :], gi[:, :], gb[:, 0:1], None, ALU.add))
            done(V.tensor_scalar(gf[:, :], gf[:, :], gb[:, 1:2], None, ALU.add))
            done(V.tensor_scalar(neg[:, :], gf[:, :], -1.0, None, ALU.mult))
            done(V.tensor_tensor(mag[:, :], gf[:, :], neg[:, :], ALU.max))
            dve.wait_ge(sact, 2)
            done(V.scalar_tensor_tensor(lf[:, :], gf[:, :], 0.0, soft[:, :], ALU.min, ALU.subtract))
            done(V.tensor_tensor_scan(b[:, 0:TP], ones[:, 0:TP], lf[:, 0:TP], 0.0, ALU.mult, ALU.add))
            done(V.tensor_copy(smp(b)[:, :, 0], smp(lf)[:, :, 0]))
            for j in range(1, d.ns):
                done(V.tensor_tensor(smp(b)[:, :, j], smp(b)[:, :, j - 1], smp(lf)[:, :, j], ALU.add))
            done(V.tensor_tensor(src[:, :], gi[:, :], b[:, :], ALU.subtract))
            done(V.tensor_tensor_scan(top[:, 0:TP], src[:, 0:TP], src[:, 0:TP], 0.0, ALU.max, ALU.max))
            done(V.tensor_tensor(smp(top)[:, :, 0], smp(src)[:, :, 0], m0[:, :], ALU.max))
            for j in range(1, d.ns):
                done(V.tensor_tensor(smp(top)[:, :, j], smp(top)[:, :, j - 1], smp(src)[:, :, j], ALU.max))
            done(V.tensor_tensor(m[:, :], b[:, :], top[:, :], ALU.add))
            done(V.tensor_scalar(neg[:, :], top[:, :], -1.0, None, ALU.mult))
            done(V.memset(it[:, 0:TP], 0.0))
            done(V.tensor_tensor(smp(it), m0[:, :].rearrange("h (b o) -> h b o", o=1).to_broadcast(
                [H, d.nb, d.ns]), smp(neg), ALU.add))
            dve.sem_inc(rows_ready, 1)

        @block.scalar
        def _(act):
            act.wait_ge(step, 5)
            nc.scalar.activation(mag[:, :], mag[:, :], ACT.Exp, scale=-1.0).then_inc(sact, 1)
            act.wait_ge(sact, 1)
            nc.scalar.activation(soft[:, :], mag[:, :], ACT.Ln, bias=1.0).then_inc(sact, 1)
            act.wait_ge(rows_ready, 1)
            nc.scalar.activation(fl[:, :], m[:, :], ACT.Exp, scale=-1.0).then_inc(sact, 1)
            nc.scalar.activation(it[:, :], it[:, :], ACT.Exp).then_inc(sact, 1)


def mlstm_features(nc, d, a, sems, c, z_dram, qk_dram, kt_dram, vt_dram, conv_prompt, conv_sample):
    T, TP, TT, NS, NB = d.t, d.tp, d.tt, d.ns, d.nb
    W = a["conv_w"].shape[1]
    PRE = W - 1
    SEG = PRE + TP
    U = SEG + NB * (PRE + NS)
    TAIL = U - TP
    LAST = TP - 4 * TT
    E = d.md // P
    cu, cv = 3 * d.ha, 3 * d.ha + d.hm * E
    with ExitStack() as ctx:
        sb = lambda n, s, t=F32: ctx.enter_context(nc.sbuf_tensor(n, s, t))
        ps = lambda n, s: ctx.enter_context(nc.psum_tensor(n, s, F32))
        u = [sb(f"u{s}", [P, E, U]) for s in range(2)]
        conv = [sb(f"conv{s}", [P, E, U]) for s in range(2)]
        sig = [sb(f"conv_sig{s}", [P, E, U]) for s in range(2)]
        ua = [sb(f"ua{s}", [P, E, T]) for s in range(2)]
        vz = [sb(f"vm{s}", [P, E, T]) for s in range(2)]
        wqk = [sb(f"wqk{s}", [P, 2, E, d.md]) for s in range(2)]
        qk = [sb(f"mqk{s}", [P, 2 * E, T]) for s in range(2)]
        rows = [sb(f"mrows{s}", [TT, 2, 5, d.md]) for s in range(2)]
        srow = [sb(f"msrow{s}", [d.tsmp, 2, d.md]) for s in range(2)]
        tail = [sb(f"conv_tail{s}", [TAIL, d.md]) for s in range(2)]
        srows = sb("state_conv_rows", [NB * PRE, d.mw])
        state = sb("state_conv_t", [P, d.hm * E, NB * PRE])
        cw = sb("conv_w_cols", [P, W, d.hm * E])
        cb = sb("conv_b_cols", [P, d.hm * E])
        proj = [ps(f"mproj{i}", [P, 2, 512]) for i in range(2)]
        turn = [ps(f"mturn{i}", [P, 2, 512]) for i in range(2)]
        cin, state_turned, state_out = sems("conv_in"), sems("conv_state_turned"), sems("conv_state_out")
        landed = [sems(f"mf_landed{s}") for s in range(2)]
        stored = [sems(f"mf_stored{s}") for s in range(2)]
        padded, tapped, gated, active, projected, proj_out, turned, rows_a, rows_b = (sems(f"mf_{n}") for n in (
            "padded", "tapped", "gated", "active", "projected", "proj_out", "turned", "rows_a", "rows_b"))
        STORES, LOADS = 1 + 6 + 1 + NB, 5
        zc = z_dram[0:(cv + d.hm * E) * P, :].rearrange("(c e p) t -> c p e t", e=E, p=P)
        qk_out = qk_dram.rearrange("(h c p) t -> h p c t", h=d.hm, p=P)
        seg = lambda x: x.rearrange("p e (b s) -> p e b s", s=PRE + NS)
        block = ctx.enter_context(nc.Block())

        def load(sp, h, s):
            zu, zv = zc[h + cu // E], zc[h + cv // E]
            sp.dma_start(u[s][:, :, PRE:SEG], zu[:, :, 0:TP]).then_inc(landed[s], 16)
            sp.dma_start(vz[s][:, :, :], zv).then_inc(landed[s], 16)
            sp.dma_start(ua[s][:, :, TP:T], zu[:, :, TP:T]).then_inc(landed[s], 16)
            for i, name in enumerate(("w_qm", "w_km")):
                sp.dma_start(wqk[s][:, i, :, :], a[name][0][h].rearrange("(k p) n -> p k n", p=P)).then_inc(landed[s], 16)

        def store(sp, g, s):
            h = g * 2 + s
            sp.wait_ge(proj_out, h * 2 * E + 2 * E)
            sp.dma_start(qk_out[h], qk[s][:, :, :]).then_inc(stored[s], 16)
            sp.wait_ge(rows_a, h * 2 * E + 2 * E)
            sp.wait_ge(rows_b, h * (2 * E + 1) + 2 * E + 1)
            for w, dram in enumerate((kt_dram, vt_dram)):
                col = dram.rearrange("t (h n) -> h t n", n=d.md)[h]
                sp.dma_start(col[0:4 * TT].rearrange("(t p) n -> p t n", p=TT),
                             rows[s][:, w, 0:4, :]).then_inc(stored[s], 16)
                sp.dma_start(col[4 * TT:TP], rows[s][0:LAST, w, 4, :]).then_inc(stored[s], 16)
                sp.dma_start(col[TP:T], srow[s][:, w, :]).then_inc(stored[s], 16)
            cols = lambda x: x.rearrange("w (h n) -> h w n", n=d.md)[h]
            sp.dma_start(cols(conv_prompt[0, 0]), tail[s][0:PRE, :]).then_inc(stored[s], 16)
            for b in range(NB):
                r = PRE + b * (PRE + NS) + NS
                sp.dma_start(cols(conv_sample[0, b]), tail[s][r:r + PRE, :]).then_inc(stored[s], 16)

        @block.sync
        def _(sp):
            sp.dma_start(srows[:, :], a["state_conv"].rearrange("o b w n -> (o b w) n")).then_inc(cin, 16)
            for j in range(W):
                sp.dma_start(cw[:, j, :], a["conv_w"][0, j].rearrange("(c p) -> p c", p=P),
                             allow_slow_non_contiguous=True).then_inc(cin, 16)
            sp.dma_start(cb[:, :], a["conv_b"][0].rearrange("(c p) -> p c", p=P),
                         allow_slow_non_contiguous=True).then_inc(cin, 16)
            for s in range(2):
                load(sp, s, s)
            for g in range(d.hm // 2):
                for s in range(2):
                    store(sp, g, s)
                    if g * 2 + s + 2 < d.hm:
                        sp.wait_ge(active, (g * 2 + s + 1) * 4)
                        sp.wait_ge(stored[s], 16 * STORES * (g + 1))
                        load(sp, g * 2 + s + 2, s)
            for s in range(2):
                sp.wait_ge(stored[s], 16 * STORES * (d.hm // 2))

        @block.vector
        def _(dve):
            for s in range(2):
                nc.vector.memset(u[s][:, :, 0:PRE], 0.0).then_inc(padded, 1)
            dve.wait_ge(cin, 16 * (W + 2))
            for k in range(d.hm * E):
                dve.wait_ge(state_turned, k + 1)
                nc.vector.tensor_copy(state[:, k, :], turn[k % 2][:, 0, 0:NB * PRE]).then_inc(state_out, 1)
            dve.wait_ge(state_out, d.hm * E)
            for h in range(d.hm):
                s = h % 2
                dve.wait_ge(landed[s], 16 * LOADS * (h // 2 + 1))
                nc.vector.tensor_copy(seg(u[s][:, :, SEG:U])[:, :, :, 0:PRE],
                                      state[:, h * E:(h + 1) * E, :].rearrange(
                                          "p e (b w) -> p e b w", w=PRE)).then_inc(padded, 1)
                nc.vector.tensor_copy(seg(u[s][:, :, SEG:U])[:, :, :, PRE:PRE + NS],
                                      ua[s][:, :, TP:T].rearrange("p e (b s) -> p e b s", s=NS)).then_inc(padded, 1)
                dve.wait_ge(padded, 2 * h + 4)
                for j in range(W):
                    for e in range(E):
                        k = h * E + e
                        x = u[s][:, e, j:j + U - PRE]
                        if j == 0:
                            nc.vector.tensor_scalar(conv[s][:, e, 0:U - PRE], x, cw[:, j, k:k + 1], cb[:, k:k + 1],
                                                    ALU.mult, ALU.add).then_inc(tapped, 1)
                        else:
                            nc.vector.scalar_tensor_tensor(conv[s][:, e, 0:U - PRE], x, cw[:, j, k:k + 1],
                                                           conv[s][:, e, 0:U - PRE], ALU.mult, ALU.add).then_inc(tapped, 1)
                    dve.wait_ge(tapped, (h * W + j + 1) * E)
                dve.wait_ge(gated, h + 1)
                for e in range(E):
                    nc.vector.tensor_tensor(ua[s][:, e, 0:TP], conv[s][:, e, 0:TP], sig[s][:, e, 0:TP],
                                            ALU.mult).then_inc(active, 1)
                    nc.vector.tensor_tensor(
                        ua[s][:, e, TP:T].rearrange("p (b s) -> p b s", s=NS),
                        seg(conv[s][:, :, SEG:U])[:, e, :, 0:NS], seg(sig[s][:, :, SEG:U])[:, e, :, 0:NS],
                        ALU.mult).then_inc(active, 1)
                if h >= 2:
                    dve.wait_ge(stored[s], 16 * STORES * (h // 2))
                for w in range(2):
                    for e in range(E):
                        dve.wait_ge(turned, h * (2 * E + 1) + w * E + e + 1)
                        tp = turn[(w * E + e) % 2]
                        nc.vector.tensor_copy(rows[s][0:LAST, w, 4, e * P:(e + 1) * P], tp[0:LAST, 1, 0:P])
                        nc.vector.tensor_copy(srow[s][:, w, e * P:(e + 1) * P],
                                              tp[0:d.tsmp, 1, P:2 * P]).then_inc(rows_b, 1)
                dve.wait_ge(turned, (h + 1) * (2 * E + 1))
                nc.vector.tensor_copy(tail[s][:, :], turn[0][0:TAIL, 0, 0:d.md]).then_inc(rows_b, 1)

        @block.scalar
        def _(act):
            for h in range(d.hm):
                s = h % 2
                act.wait_ge(tapped, (h + 1) * W * E)
                nc.scalar.activation(sig[s][:, :, 0:U - PRE], conv[s][:, :, 0:U - PRE], ACT.Sigmoid).then_inc(gated, 1)
                if h >= 2:
                    act.wait_ge(stored[s], 16 * STORES * (h // 2))
                for i in range(2 * E):
                    act.wait_ge(projected, h * 2 * E + i + 1)
                    nc.scalar.activation(qk[s][:, i, :].rearrange("p (b t) -> p b t", b=2),
                                         proj[i % 2][:, :, 0:d.half], ACT.Copy,
                                         scale=1.0 if i < E else d.md ** -0.5).then_inc(proj_out, 1)
                for w in range(2):
                    for e in range(E):
                        act.wait_ge(turned, h * (2 * E + 1) + w * E + e + 1)
                        nc.scalar.activation(rows[s][:, w, 0:4, e * P:(e + 1) * P],
                                             turn[(w * E + e) % 2][0:TT, 0, :].rearrange("p (t n) -> p t n", n=P),
                                             ACT.Copy).then_inc(rows_a, 1)

        @block.tensor
        def _(pe):
            pe.wait_ge(cin, 16 * (W + 2))
            for k in range(d.hm * E):
                if k >= 2:
                    pe.wait_ge(state_out, k - 1)
                nc.tensor.transpose(turn[k % 2][:, 0, 0:NB * PRE], srows[:, k * P:(k + 1) * P],
                                    c.ident[0:NB * PRE, 0:NB * PRE]).then_inc(state_turned, 1)
            for h in range(d.hm):
                s = h % 2
                pe.wait_ge(active, 2 * E * (h + 1))
                for i in range(2 * E):
                    m, e = i // E, i % E
                    n = h * 2 * E + i
                    if n >= 2:
                        pe.wait_ge(proj_out, n - 1)
                    for half in range(2):
                        for k in range(E):
                            mm = nc.tensor.matmul(proj[i % 2][:, half, 0:d.half],
                                                  wqk[s][:, m, k, e * P:(e + 1) * P],
                                                  ua[s][:, k, half * d.half:(half + 1) * d.half],
                                                  start=(k == 0), stop=(k == E - 1))
                    mm.then_inc(projected, 1)
                for w in range(2):
                    for e in range(E):
                        i = w * E + e
                        tp = turn[i % 2]
                        if w == 0:
                            pe.wait_ge(proj_out, h * 2 * E + E + e + 1)
                        if i < 2:
                            if h:
                                pe.wait_ge(rows_a, h * 2 * E)
                                pe.wait_ge(rows_b, h * (2 * E + 1))
                            else:
                                pe.wait_ge(state_out, d.hm * E)
                        else:
                            pe.wait_ge(rows_a, h * 2 * E + i - 1)
                            pe.wait_ge(rows_b, h * (2 * E + 1) + i - 1)
                        x = qk[s][:, E + e, :] if w == 0 else vz[s][:, e, :]
                        for t in range(4):
                            nc.tensor.transpose(tp[0:TT, 0, t * P:(t + 1) * P], x[:, t * TT:(t + 1) * TT],
                                                c.ident[:, :])
                        nc.tensor.transpose(tp[0:LAST, 1, 0:P], x[:, 4 * TT:TP], c.ident[:, :])
                        nc.tensor.transpose(tp[0:d.tsmp, 1, P:2 * P], x[:, TP:T],
                                            c.ident[:, :]).then_inc(turned, 1)
                pe.wait_ge(rows_a, h * 2 * E + 2 * E - 1)
                pe.wait_ge(rows_b, h * (2 * E + 1) + 2 * E - 1)
                for e in range(E):
                    mm = nc.tensor.transpose(turn[0][0:TAIL, 0, e * P:(e + 1) * P], u[s][:, e, TP:U], c.ident[:, :])
                mm.then_inc(turned, 1)



def prompt_mlstm(nc, d, a, sems, c, qk_dram, kt_dram, vt_dram, g_dram, mix, c_prompt, n_prompt):
    T, TP, TT, NT = d.t, d.tp, d.tt, d.nt
    LAST = TP - (NT - 1) * TT
    E = d.md // P
    n = [TT] * (NT - 1) + [LAST]
    with ExitStack() as ctx:
        sb = lambda x, s, t=F32: ctx.enter_context(nc.sbuf_tensor(x, s, t))
        ps = lambda x, s: ctx.enter_context(nc.psum_tensor(x, s, F32))
        qk = [sb(f"ml_qk{s}", [P, 2 * E, TP]) for s in range(2)]
        v = [sb(f"ml_v{s}", [TT, NT, d.md + 1]) for s in range(2)]
        kt = [sb(f"ml_kt{s}", [TT, NT, d.md]) for s in range(2)]
        negtop = [sb(f"ml_negtop{s}", [TT, TP]) for s in range(2)]
        floor = [sb(f"ml_floor{s}", [P, TP]) for s in range(2)]
        src = [sb(f"ml_src{s}", [TT, NT]) for s in range(2)]
        w = [sb(f"ml_w{s}", [TT, NT, TP]) for s in range(2)]
        tri = sb("ml_tri", [TT, TT])
        mag = [sb(f"ml_mag{i}", [P, TT]) for i in range(2)]
        state = [sb(f"ml_state{s}", [P, E, d.md + 1]) for s in range(2)]
        score = [ps(f"ml_score{i}", [P, 2, 512]) for i in range(2)]
        num = [ps(f"ml_num{i}", [P, 512]) for i in range(2)]
        acc = [ps(f"ml_acc{e}", [P, 512]) for e in range(E)]
        tri_made, ones_made = sems("ml_tri_made"), sems("ml_ones_made")
        landed = [sems(f"ml_landed{s}") for s in range(2)]
        stored = [sems(f"ml_stored{s}") for s in range(2)]
        shifted, raised, keyed, cut, weighed, scored, summed, abs_made, floored, inverted, placed, state_summed, \
            state_out = (sems(f"ml_{x}") for x in (
                "shifted", "raised", "keyed", "cut", "weighed", "scored", "summed", "abs_made", "floored",
                "inverted", "placed", "state_summed", "state_out"))
        LOADS = 9
        qk_in = qk_dram.rearrange("(h c p) t -> h p c t", h=d.hm, p=P)
        block = ctx.enter_context(nc.Block())

        def rows(x, h):
            return x.rearrange("t (h n) -> h t n", n=d.md)[h]

        def load(sp, h, s):
            def get(out, src_ap, **kw):
                sp.dma_start(out, src_ap, **kw).then_inc(landed[s], 16)
            get(qk[s][:, :, :], qk_in[h][:, :, 0:TP])
            for out, x in ((v[s][:, :, 0:d.md], rows(vt_dram, h)), (kt[s][:, :, :], rows(kt_dram, h))):
                get(out[:, 0:NT - 1, :], x[0:(NT - 1) * TT].rearrange("(t p) n -> p t n", p=TT))
                get(out[0:LAST, NT - 1, :], x[(NT - 1) * TT:TP])
            get(negtop[s][:, :], g_dram[G_NEGTOP, h:h + 1, 0:TP].to_broadcast([TT, TP]))
            get(floor[s][:, :], g_dram[G_FLOOR, h:h + 1, 0:TP].to_broadcast([P, TP]))
            get(src[s][:, 0:NT - 1], g_dram[G_SOURCE, h, 0:(NT - 1) * TT].rearrange("(t p) -> p t", p=TT),
                allow_slow_non_contiguous=True)
            get(src[s][0:LAST, NT - 1:NT], g_dram[G_SOURCE, h:h + 1, (NT - 1) * TT:TP].rearrange("o p -> p o"),
                allow_slow_non_contiguous=True)

        @block.sync
        def _(sp):
            for s in range(2):
                load(sp, s, s)
            for h in range(d.hm):
                s = h % 2
                sp.wait_ge(state_out, E * (h + 1))
                sp.dma_start(c_prompt[0, 0, h].rearrange("(e p) n -> p e n", p=P),
                             state[s][:, :, 0:d.md]).then_inc(stored[s], 16)
                sp.dma_start(n_prompt[0, 0, h].rearrange("(e p) -> p e", p=P), state[s][:, :, d.md],
                             allow_slow_non_contiguous=True).then_inc(stored[s], 16)
                if h + 2 < d.hm:
                    sp.wait_ge(placed, NT * (h + 1))
                    load(sp, h + 2, s)
            for s in range(2):
                sp.wait_ge(stored[s], 32 * (d.hm // 2))

        @block.gpsimd
        def _(pool):
            nc.gpsimd.memset(tri[:, :], 1.0).then_inc(tri_made, 1)
            pool.wait_ge(tri_made, 1)
            nc.gpsimd.affine_select(out=tri[:, :], in_=tri[:, :], compare_op=ALU.is_ge, fill=0.0, base=0,
                                    pattern=[[1, TT]], channel_multiplier=-1).then_inc(tri_made, 1)

        def pe_scores(pe, h, j):
            s, i = h % 2, h * NT + j
            if i >= 2:
                pe.wait_ge(weighed, i - 1)
            width = TP - j * TT
            for b, (c0, c1) in enumerate(((0, width // 2), (width // 2, width)) if width > 512 else ((0, width),)):
                for e in range(E):
                    mm = nc.tensor.matmul(score[i % 2][0:n[j], b, 0:c1 - c0],
                                          qk[s][:, E + e, j * TT:j * TT + n[j]],
                                          qk[s][:, e, j * TT + c0:j * TT + c1], start=(e == 0), stop=(e == E - 1))
            mm.then_inc(scored, 1)

        def pe_sum(pe, h, t):
            s, i = h % 2, h * NT + t
            pe.wait_ge(weighed, i + 1)
            if i >= 2:
                pe.wait_ge(placed, i - 1)
            cols = slice(t * TT, t * TT + n[t])
            for e in range(E + 1):
                for j in range(t + 1):
                    lhs = v[s][0:n[j], j, e * P:(e + 1) * P] if e < E else c.ones[0:n[j], :]
                    mm = nc.tensor.matmul(num[i % 2][:, e * TT:e * TT + n[t]], lhs, w[s][0:n[j], j, cols],
                                          start=(j == 0), stop=(j == t))
            mm.then_inc(summed, 1)

        def pe_state(pe, h):
            s = h % 2
            pe.wait_ge(keyed, NT * (h + 1))
            if h:
                pe.wait_ge(state_out, E * h)
            for e in range(E):
                for j in range(NT):
                    mm = nc.tensor.matmul(acc[e][:, 0:d.md + 1], kt[s][0:n[j], j, e * P:(e + 1) * P],
                                          v[s][0:n[j], j, :], start=(j == 0), stop=(j == NT - 1))
                mm.then_inc(state_summed, 1)

        @block.tensor
        def _(pe):
            pe.wait_ge(ones_made, 2)
            for h in range(d.hm):
                pe.wait_ge(landed[h % 2], 16 * LOADS * (h // 2 + 1))
                for j in range(NT):
                    pe_scores(pe, h, j)
                    if j:
                        pe_sum(pe, h, j - 1)
                pe_state(pe, h)
                pe_sum(pe, h, NT - 1)

        def dve_weigh(dve, h, j):
            s, i = h % 2, h * NT + j
            width = TP - j * TT
            dve.wait_ge(raised, i + 1)
            row = w[s][0:n[j], j, :]
            nc.vector.tensor_scalar(kt[s][0:n[j], j, :], kt[s][0:n[j], j, :], row[:, TP - 1:TP], None,
                                    ALU.mult).then_inc(keyed, 1)
            dve.wait_ge(keyed, i + 1)
            nc.vector.tensor_tensor(row[:, j * TT:j * TT + n[j]], row[:, j * TT:j * TT + n[j]],
                                    tri[0:n[j], 0:n[j]], ALU.mult).then_inc(cut, 1)
            dve.wait_ge(cut, i + 1)
            dve.wait_ge(scored, i + 1)
            for b, (c0, c1) in enumerate(((0, width // 2), (width // 2, width)) if width > 512 else ((0, width),)):
                ins = nc.vector.tensor_tensor(row[:, j * TT + c0:j * TT + c1], score[i % 2][0:n[j], b, 0:c1 - c0],
                                              row[:, j * TT + c0:j * TT + c1], ALU.mult)
            ins.then_inc(weighed, 1)

        def dve_place(dve, h, t):
            s, i = h % 2, h * NT + t
            dve.wait_ge(abs_made, i + 1)
            cols = slice(t * TT, t * TT + n[t])
            m = mag[i % 2][:, 0:n[t]]
            nc.vector.tensor_tensor(m, m, floor[s][:, cols], ALU.max).then_inc(floored, 1)
            dve.wait_ge(floored, i + 1)
            nc.vector.reciprocal(m, m).then_inc(inverted, 1)
            dve.wait_ge(inverted, i + 1)
            for e in range(E):
                ins = nc.vector.tensor_tensor(mix[:, d.ha + h * E + e, cols], num[i % 2][:, e * TT:e * TT + n[t]],
                                              m, ALU.mult)
            ins.then_inc(placed, 1)

        @block.vector
        def _(dve):
            for s in range(2):
                nc.vector.memset(v[s][:, :, d.md:d.md + 1], 1.0).then_inc(ones_made, 1)
            dve.wait_ge(tri_made, 2)
            for h in range(d.hm):
                s = h % 2
                dve.wait_ge(landed[s], 16 * LOADS * (h // 2 + 1))
                if h >= 2:
                    dve.wait_ge(summed, NT * (h - 1))
                for j in range(NT):
                    nc.vector.tensor_scalar(w[s][0:n[j], j, j * TT:TP], negtop[s][0:n[j], j * TT:TP],
                                            src[s][0:n[j], j:j + 1], 0.0, ALU.add, ALU.min).then_inc(shifted, 1)
                for j in range(NT):
                    dve_weigh(dve, h, j)
                    if j:
                        dve_place(dve, h, j - 1)
                dve_place(dve, h, NT - 1)

        @block.scalar
        def _(act):
            for h in range(d.hm):
                s = h % 2
                for j in range(NT):
                    act.wait_ge(shifted, h * NT + j + 1)
                    nc.scalar.activation(w[s][0:n[j], j, j * TT:TP], w[s][0:n[j], j, j * TT:TP],
                                         ACT.Exp).then_inc(raised, 1)

                def magnitude(t):
                    i = h * NT + t
                    act.wait_ge(summed, i + 1)
                    if i >= 2:
                        act.wait_ge(placed, i - 1)
                    nc.scalar.activation(mag[i % 2][:, 0:n[t]], num[i % 2][:, E * TT:E * TT + n[t]],
                                         ACT.Abs).then_inc(abs_made, 1)
                for t in range(NT - 1):
                    magnitude(t)
                if h >= 2:
                    act.wait_ge(stored[s], 32 * (h // 2))
                for e in range(E):
                    act.wait_ge(state_summed, E * h + e + 1)
                    nc.scalar.activation(state[s][:, e, :], acc[e][:, 0:d.md + 1], ACT.Copy).then_inc(state_out, 1)
                magnitude(NT - 1)


def sample_mlstm(nc, d, a, sems, c, qk_dram, kt_dram, vt_dram, g_dram, mix, c_sample, n_sample):
    T, TP, NB, NS, TS = d.t, d.tp, d.nb, d.ns, d.tsmp
    E, MD = d.md // P, d.md
    with ExitStack() as ctx:
        sb = lambda x, s, t=F32: ctx.enter_context(nc.sbuf_tensor(x, s, t))
        ps = lambda x, s: ctx.enter_context(nc.psum_tensor(x, s, F32))
        qk = [sb(f"sm_qk{s}", [P, 2 * E, TS]) for s in range(2)]
        qn = [sb(f"sm_qn{s}", [P, E, TS]) for s in range(2)]
        v = [sb(f"sm_v{s}", [TS, MD + 1]) for s in range(2)]
        kt = [sb(f"sm_kt{s}", [TS, MD]) for s in range(2)]
        kw = [sb(f"sm_kw{s}", [TS, NB, MD]) for s in range(2)]
        negtop = [sb(f"sm_negtop{s}", [TS, TS]) for s in range(2)]
        floor = [sb(f"sm_floor{s}", [P, TS]) for s in range(2)]
        inter = [sb(f"sm_inter{s}", [P, TS]) for s in range(2)]
        src = [sb(f"sm_src{s}", [TS, 1]) for s in range(2)]
        c0 = [sb(f"sm_c0{s}", [P, NB, E, MD + 1]) for s in range(2)]
        w = [sb(f"sm_w{s}", [TS, TS]) for s in range(2)]
        sw = [sb(f"sm_sw{s}", [TS, TS]) for s in range(2)]
        own = sb("sm_own", [TS, TS])
        mag = sb("sm_mag", [P, TS])
        score = ps("sm_score", [P, 512])
        num = [ps(f"sm_num{e}", [P, 512]) for e in range(E + 1)]
        acc = [ps(f"sm_acc{i}", [P, 512]) for i in range(4)]
        own_made, ones_made = sems("sm_own_made"), sems("sm_ones_made")
        landed = [sems(f"sm_landed{s}") for s in range(2)]
        stored = [sems(f"sm_stored{s}") for s in range(2)]
        shifted, raised, masked, weighed, scaled, normed, scored, summed, abs_made, floored, inverted, placed, \
            keyed, updated, state_new = (sems(f"sm_{x}") for x in (
                "shifted", "raised", "masked", "weighed", "scaled", "normed", "scored", "summed", "abs_made",
                "floored", "inverted", "placed", "keyed", "updated", "state_new"))
        LOADS = 7 + 2 * NB
        qk_in = qk_dram.rearrange("(h c p) t -> h p c t", h=d.hm, p=P)
        block = ctx.enter_context(nc.Block())

        def load(sp, h, s):
            def get(out, x, **kw_):
                sp.dma_start(out, x, **kw_).then_inc(landed[s], 16)
            rows = lambda x: x.rearrange("t (h n) -> h t n", n=MD)[h][TP:T]
            get(qk[s][:, :, :], qk_in[h][:, :, TP:T])
            get(v[s][:, 0:MD], rows(vt_dram))
            get(kt[s][:, :], rows(kt_dram))
            get(negtop[s][:, :], g_dram[G_NEGTOP, h:h + 1, TP:T].to_broadcast([TS, TS]))
            get(floor[s][:, :], g_dram[G_FLOOR, h:h + 1, TP:T].to_broadcast([P, TS]))
            get(inter[s][:, :], g_dram[G_INTER, h:h + 1, TP:T].to_broadcast([P, TS]))
            get(src[s][:, :], g_dram[G_SOURCE, h:h + 1, TP:T].rearrange("o p -> p o"),
                allow_slow_non_contiguous=True)
            for b in range(NB):
                get(c0[s][:, b, :, 0:MD], a["state_C"][0, b, h].rearrange("(e p) n -> p e n", p=P))
                get(c0[s][:, b, :, MD], a["state_n"][0, b, h].rearrange("(e p) -> p e", p=P),
                    allow_slow_non_contiguous=True)

        @block.sync
        def _(sp):
            for s in range(2):
                load(sp, s, s)
            for h in range(d.hm):
                s = h % 2
                for b in range(NB):
                    sp.wait_ge(state_new, E * (h * NB + b + 1))
                    sp.dma_start(c_sample[0, b, h].rearrange("(e p) n -> p e n", p=P),
                                 c0[s][:, b, :, 0:MD]).then_inc(stored[s], 16)
                    sp.dma_start(n_sample[0, b, h].rearrange("(e p) -> p e", p=P), c0[s][:, b, :, MD],
                                 allow_slow_non_contiguous=True).then_inc(stored[s], 16)
                if h + 2 < d.hm:
                    sp.wait_ge(stored[s], 32 * NB * (h // 2 + 1))
                    sp.wait_ge(placed, h + 1)
                    load(sp, h + 2, s)
            for s in range(2):
                sp.wait_ge(stored[s], 32 * NB * (d.hm // 2))

        @block.gpsimd
        def _(pool):
            own3 = own[:, :].rearrange("p (b s) -> p b s", s=NS)
            nc.gpsimd.memset(own[:, :], 1.0).then_inc(own_made, 1)
            pool.wait_ge(own_made, 1)
            nc.gpsimd.affine_select(out=own[:, :], in_=own[:, :], compare_op=ALU.is_ge, fill=0.0, base=0,
                                    pattern=[[1, TS]], channel_multiplier=-1).then_inc(own_made, 1)
            pool.wait_ge(own_made, 2)
            nc.gpsimd.affine_select(out=own3, in_=own3, compare_op=ALU.is_ge, fill=0.0, base=0,
                                    pattern=[[-NS, NB], [0, NS]], channel_multiplier=1).then_inc(own_made, 1)

        @block.vector
        def _(dve):
            V = nc.vector
            for s in range(2):
                V.memset(v[s][:, MD:MD + 1], 1.0).then_inc(ones_made, 1)
            dve.wait_ge(own_made, 3)
            for h in range(d.hm):
                s = h % 2
                dve.wait_ge(landed[s], 16 * LOADS * (h // 2 + 1))
                V.tensor_scalar(w[s][:, :], negtop[s][:, :], src[s][:, :], 0.0, ALU.add, ALU.min).then_inc(shifted, 1)
                if h >= 2:
                    dve.wait_ge(summed, h - 1)
                dve.wait_ge(scored, h + 1)
                for e in range(E):
                    V.tensor_tensor(qk[s][:, e, :], qk[s][:, e, :], inter[s][:, :], ALU.mult).then_inc(scaled, 1)
                dve.wait_ge(scaled, E * (h + 1))
                for e in range(E):
                    V.tensor_tensor(qn[s][:, e, :].rearrange("p (b s) -> p b s", s=NS),
                                    qk[s][:, e, :].rearrange("p (b s) -> p b s", s=NS),
                                    c0[s][:, :, e, MD:MD + 1].to_broadcast([P, NB, NS]), ALU.mult).then_inc(normed, 1)
                dve.wait_ge(raised, h + 1)
                V.tensor_tensor(w[s][:, :], w[s][:, :], own[:, :], ALU.mult).then_inc(masked, 1)
                dve.wait_ge(masked, h + 1)
                V.tensor_tensor(sw[s][:, :], score[0:TS, 0:TS], w[s][:, :], ALU.mult).then_inc(weighed, 1)
                if h >= 2:
                    dve.wait_ge(updated, E * NB * (h - 1))
                for b in range(NB):
                    last = b * NS + NS - 1
                    V.tensor_scalar(kw[s][:, b, :], kt[s][:, :], w[s][:, last:last + 1], None,
                                    ALU.mult).then_inc(keyed, 1)
                dve.wait_ge(abs_made, h + 1)
                V.tensor_tensor(mag[:, :], mag[:, :], floor[s][:, :], ALU.max).then_inc(floored, 1)
                dve.wait_ge(floored, h + 1)
                V.reciprocal(mag[:, :], mag[:, :]).then_inc(inverted, 1)
                dve.wait_ge(inverted, h + 1)
                for e in range(E):
                    ins = V.tensor_tensor(mix[:, d.ha + h * E + e, TP:T], num[e][:, 0:TS], mag[:, :], ALU.mult)
                ins.then_inc(placed, 1)
                for b in range(NB):
                    last = b * NS + NS - 1
                    for e in range(E):
                        i = (h * NB + b) * E + e
                        dve.wait_ge(updated, i + 1)
                        V.scalar_tensor_tensor(c0[s][:, b, e, :], c0[s][:, b, e, :], inter[s][:, last:last + 1],
                                               acc[i % 4][:, 0:MD + 1], ALU.mult, ALU.add).then_inc(state_new, 1)

        @block.scalar
        def _(act):
            for h in range(d.hm):
                s = h % 2
                act.wait_ge(shifted, h + 1)
                nc.scalar.activation(w[s][:, :], w[s][:, :], ACT.Exp).then_inc(raised, 1)
                act.wait_ge(summed, h + 1)
                if h:
                    act.wait_ge(placed, h)
                nc.scalar.activation(mag[:, :], num[E][:, 0:TS], ACT.Abs).then_inc(abs_made, 1)

        @block.tensor
        def _(pe):
            pe.wait_ge(ones_made, 2)
            for h in range(d.hm):
                s = h % 2
                pe.wait_ge(landed[s], 16 * LOADS * (h // 2 + 1))
                if h:
                    pe.wait_ge(weighed, h)
                for e in range(E):
                    mm = nc.tensor.matmul(score[0:TS, 0:TS], qk[s][:, E + e, :], qk[s][:, e, :],
                                          start=(e == 0), stop=(e == E - 1))
                mm.then_inc(scored, 1)
                pe.wait_ge(weighed, h + 1)
                pe.wait_ge(normed, E * (h + 1))
                if h:
                    pe.wait_ge(placed, h)
                for e in range(E):
                    nc.tensor.matmul(num[e][:, 0:TS], v[s][:, e * P:(e + 1) * P], sw[s][:, :], start=True,
                                     stop=False, skip_group_check=True)
                    for b in range(NB):
                        cols = slice(b * NS, (b + 1) * NS)
                        for k in range(E):
                            nc.tensor.matmul(num[e][:, cols], c0[s][:, b, k, e * P:(e + 1) * P], qk[s][:, k, cols],
                                             start=False, stop=(b == NB - 1 and k == E - 1), skip_group_check=True)
                nc.tensor.matmul(num[E][:, 0:TS], c.ones[0:TS, :], sw[s][:, :], start=True, stop=False)
                for k in range(E):
                    mm = nc.tensor.matmul(num[E][:, 0:TS], c.ones[:, :], qn[s][:, k, :], start=False,
                                          stop=(k == E - 1))
                mm.then_inc(summed, 1)
                for b in range(NB):
                    for e in range(E):
                        i = (h * NB + b) * E + e
                        if e == 0:
                            pe.wait_ge(keyed, h * NB + b + 1)
                        if i >= 4:
                            pe.wait_ge(state_new, i - 3)
                        nc.tensor.matmul(acc[i % 4][:, 0:MD + 1], kw[s][:, b, e * P:(e + 1) * P], v[s][:, :],
                                         start=True, stop=True).then_inc(updated, 1)


def decode_attention(nc, d, a, sems, c, zn_dram, vs_rows, mix):
    HA, VD, HD, NS, NB, TP, TS = d.ha, d.vd, d.hd, d.ns, d.nb, d.tp, d.tsmp
    PG, R = d.pages, d.ha * 2 * d.ns
    PAST, KEYS = PG * P, PG * P + TS
    RING = 8
    GR = PG // 2
    EV = GR + 1
    PIECES = 4
    PW = KEYS // PIECES
    assert d.page == P and PG % RING == 0 and KEYS % PIECES == 0 and d.aw == 2 * 512 and NB % 2 == 0
    with ExitStack() as ctx:
        sb = lambda x, s, t=F32: ctx.enter_context(nc.sbuf_tensor(x, s, t))
        ps = lambda x, s: ctx.enter_context(nc.psum_tensor(x, s, F32))
        ring = sb("dc_pages", [P, RING, d.aw])
        kh = [sb(f"dc_kh{i}", [P, HA, 2 * P], F32R) for i in range(2)]
        kl = [sb(f"dc_kl{i}", [P, HA, 2 * P], F32R) for i in range(2)]
        vslot = lambda x, p: x[(p % 4) // 2][:, :, :].rearrange("p h t -> p (h t)")[:, (p % 2) * d.aw:(p % 2 + 1) * d.aw]
        sc = [sb(f"dc_scores{i}", [R, KEYS]) for i in range(2)]
        bias = sb("dc_bias", [R, PAST])
        own_bias = sb("dc_own_bias", [R, NB, TS])
        ph, pl = ([sb(f"dc_{x}{i}", [P, PG, R], F32R) for i in range(2)] for x in ("ph", "pl"))
        pown = [sb(f"dc_pown{i}", [TS, R]) for i in range(2)]
        qs, ks = sb("dc_qs", [P, HA, TS]), sb("dc_ks", [P, HA, TS])
        vown = sb("dc_vown", [TS, d.aw])
        qh = [sb(f"dc_qh{i}", [P, HA, R], F32R) for i in range(2)]
        ql = [sb(f"dc_ql{i}", [P, HA, R], F32R) for i in range(2)]
        qflat = sb("dc_q", [P, HA * (R + 2 * NS)])
        qf = qflat[:, 0:HA * R].rearrange("p (h r) -> p h r", r=R)
        qdiag = qflat[:, :].rearrange("p (h x) -> p h x", x=R + 2 * NS)
        own_rows = sb("dc_own_rows", [R, d.aw])
        kept = sb("dc_kept", [R, VD])
        comb = sb("dc_comb", [R, TS])
        heads = sb("dc_heads", [R, HA])
        line = sb("dc_line", [1, 3, R])
        cols = sb("dc_cols", [R, 3])
        tops, low, dens, coef = sb("dc_tops", [R, PIECES + 1]), sb("dc_low", [R, 2]), \
            sb("dc_dens", [R, 2, PIECES]), sb("dc_coef", [R, 2])
        ptab = sb("dc_page_table", [1, NB * PG], I32)
        pk = [ps(f"dc_pk{i}", [P, 1024]) for i in range(2)]
        pscore = [ps(f"dc_pscore{i}", [P, 512]) for i in range(2)]
        pout = ps("dc_pout", [P, 1024])
        table_in, inputs_in, lined, columns, consts = (sems(f"dc_{x}") for x in (
            "table_in", "inputs_in", "lined", "columns", "consts"))
        own_bias_steps = sems("dc_own_bias_steps")
        page_in = [sems(f"dc_page_in{i}") for i in range(RING)]
        kturned, khi, klo, q_laid, qhi, qlo, scored, biased, topped, lowered, raised, pturned, phi, plo, \
            own_turned, own_out, vhi, vlo, valued, summed, inverted, kept_all, kept_one, combined, placed = (
                sems(f"dc_{x}") for x in (
                    "kturned", "khi", "klo", "q_laid", "qhi", "qlo", "scored", "biased", "topped",
                    "lowered", "raised", "pturned", "phi", "plo", "own_turned", "own_out", "vhi", "vlo", "valued",
                    "summed", "inverted", "kept_all", "kept_one", "combined", "placed"))
        pages = [x[0].rearrange("n p h e -> n p (h e)") for x in (a["cache_k"], a["cache_v"])]
        block = ctx.enter_context(nc.Block())

        def load_phase(sp, which, b, freed, freed_before):
            def page(p, slot, given_back, count):
                idx = sp.value_load(ptab[0:1, bass.ds(b * PG + p, 1)], min_val=0, max_val=d.pool - 1)
                if given_back is not None:
                    sp.wait_ge(given_back, count)
                sp.dma_start(ring[:, slot, :], pages[which][idx]).then_inc(page_in[slot], 16)
            for slot in range(RING):
                if freed_before is None:
                    page(slot, slot, None, 0)
                else:
                    page(slot, slot, freed_before[0], freed_before[1] + (slot + 1))
            with sp.Fori(0, PG // RING - 1) as i:
                for slot in range(RING):
                    page((i + 1) * RING + slot, slot, freed, b * PG + i * RING + (slot + 1))

        @block.sync
        def _(sp):
            sp.dma_start(ptab[:, :], a["page_table"].rearrange("(o b) g -> o (b g)", o=1)).then_inc(table_in, 16)
            zs = zn_dram.rearrange("(w h p) t -> w p h t", w=2, p=P)
            sp.dma_start(qs[:, :, :], zs[0][:, :, TP:d.t]).then_inc(inputs_in, 16)
            sp.dma_start(ks[:, :, :], zs[1][:, :, TP:d.t]).then_inc(inputs_in, 16)
            sp.dma_start(vown[:, :], vs_rows).then_inc(inputs_in, 16)
            sp.wait_ge(table_in, 16)
            last = PG - RING
            load_phase(sp, 0, 0, kturned, None)
            load_phase(sp, 0, 1, kturned, (kturned, last))
            load_phase(sp, 1, 0, vlo, (kturned, PG + last))
            with sp.Fori(1, NB // 2) as g:
                b = g * 2
                load_phase(sp, 0, b, kturned, (vlo, (b - 2) * PG + last))
                load_phase(sp, 1, b - 1, vlo, (kturned, b * PG + last))
                load_phase(sp, 0, b + 1, kturned, (vlo, (b - 1) * PG + last))
                load_phase(sp, 1, b, vlo, (kturned, (b + 1) * PG + last))
            load_phase(sp, 1, NB - 1, vlo, (vlo, (NB - 2) * PG + last))

        @block.gpsimd
        def _(pool):
            n = [0]

            def done(instruction):
                instruction.then_inc(lined, 1)
                n[0] += 1
                pool.wait_ge(lined, n[0])
            G = nc.gpsimd
            l3 = lambda i: line[:, i, :].rearrange("o (h m q) -> o h m q", m=2, q=NS)
            for h in range(HA):
                done(G.memset(l3(0)[:, h, :, :], 2.0 ** (-8.0 * (h + 1) / HA)))
            done(G.iota(line[:, 1, :], pattern=[[0, 2 * HA], [1, NS]], base=0, channel_multiplier=0,
                        allow_small_or_imprecise_dtypes=True))
            done(G.memset(line[:, 2, :], 1.0))
            done(G.iota(bias[:, :], pattern=[[1, PAST]], base=-PAST, channel_multiplier=0,
                        allow_small_or_imprecise_dtypes=True))
            done(G.iota(own_bias[:, :, :], pattern=[[0, NB * NB], [1, NS]], base=0, channel_multiplier=0,
                        allow_small_or_imprecise_dtypes=True))
            done(G.memset(heads[:, :], 1.0))
            done(G.affine_select(out=heads[:, :], in_=heads[:, :], compare_op=ALU.is_ge, fill=0.0, base=0,
                                 pattern=[[-2 * NS, HA]], channel_multiplier=1))
            done(G.affine_select(out=heads[:, :], in_=heads[:, :], compare_op=ALU.is_ge, fill=0.0,
                                 base=2 * NS - 1, pattern=[[2 * NS, HA]], channel_multiplier=-1))
            pool.wait_ge(consts, 5)
            ob = own_bias[:, :, :].rearrange("r b (s j) -> r b s j", j=NS)
            G.affine_select(out=ob, in_=ob, compare_op=ALU.is_equal, fill=FILL, base=0,
                            pattern=[[1, NB], [-1, NB], [0, NS]], channel_multiplier=0).then_inc(consts, 1)

        LINED = HA + 7
        TURNED_AT = (PG - 3, PG - 1)
        TURN_AT = PG - 5

        def pe_k(pe, b, s, f, hook=None, very_first=False):
            pe.wait_ge(qlo, b + 1)

            def body(i, first):
                for slot in range(RING):
                    n = b * PG + i * RING + slot
                    pe.wait_ge(page_in[slot], f * (16 * PG // RING) + i * 16 + 16)
                    if first and slot == 0 and hook is not None:
                        pe.wait_ge(plo, b * 2)
                    if not (very_first and first and slot < 2):
                        pe.wait_ge(klo, n - 1)
                    for h in range(HA):
                        mm = nc.tensor.transpose(pk[slot % 2][:, h * P:(h + 1) * P],
                                                 ring[:, slot, h * P:(h + 1) * P], c.ident[:, :])
                    mm.then_inc(kturned, 1)
                    if slot % 2 == 1 and not (first and slot == 1):
                        group(i * (RING // 2) + slot // 2 - 1, (slot // 2 - 1) % 2, first and slot <= 5)
                    if first and slot == 3 and hook is not None:
                        pe_combine(pe, hook)

            def group(g, k, early):
                pe.wait_ge(klo, b * PG + g * 2 + 2)
                if hook is not None and early and k == 0:
                    pe.wait_ge(own_out, b)
                if hook is not None and early and k == 1:
                    pe.wait_ge(placed, hook + 1)
                if not (very_first and early):
                    pe.wait_ge(biased, b * EV if early else b * EV + g - 1)
                for h in range(HA):
                    mm = exact_passes(nc, pscore[k][0:R, 0:2 * P], qh[s][:, h, :], ql[s][:, h, :],
                                      kh[k][:, h, :], kl[k][:, h, :], h == 0, h == HA - 1)
                mm.then_inc(scored, 1)

            body(0, True)
            with pe.Fori(1, PG // RING) as i:
                body(i, False)
            group(GR - 1, (GR - 1) % 2, False)
            pe.wait_ge(biased, b * EV + (GR - 1))
            for h in range(HA):
                mm = nc.tensor.matmul(pscore[0][0:R, 0:TS], qf[:, h, :], ks[:, h, :], start=(h == 0),
                                      stop=(h == HA - 1))
            mm.then_inc(scored, 1)

        def pe_turn(pe, b, s, kphases):
            pe.wait_ge(raised, b * PIECES + PIECES)
            pe.wait_ge(klo, kphases * PG)
            pe.wait_ge(biased, kphases * EV)
            for i in range(2):
                for j in range(PG // 2):
                    p = i * (PG // 2) + j
                    out, x = pk[i][:, j * R:(j + 1) * R], sc[s][:, p * P:(p + 1) * P]
                    mm = nc.tensor.matmul(out, x, c.ident[0:R, 0:R], start=True, stop=True) if p == 0 else \
                        nc.tensor.transpose(out, x, c.ident[0:R, 0:R])
                mm.then_inc(pturned, 1)
            nc.tensor.transpose(pscore[0][0:TS, 0:R], sc[s][:, PAST:KEYS], c.ident[0:R, 0:R]).then_inc(own_turned, 1)

        def pe_v(pe, b, s, following):
            for p in range(PG):
                if p % (PG // 2) == 0:
                    pe.wait_ge(plo, b * 2 + 1 + p // (PG // 2))
                pe.wait_ge(vlo, b * PG + p + 1)
                if p == 0 and not (isinstance(b, int) and b == 0):
                    pe.wait_ge(kept_all, b)
                for half in range(2):
                    cs = slice(half * 512, half * 512 + 512)
                    mm = exact_passes(nc, pout[0:R, cs], ph[s][:, p, :], pl[s][:, p, :], vslot(kh, p)[:, cs],
                                      vslot(kl, p)[:, cs], p == 0, False)
                mm.then_inc(valued, 1)
                if following is not None and p == TURN_AT:
                    pe_turn(pe, following, 1 - s, following + 1)
            pe.wait_ge(own_out, b + 1)
            for half in range(2):
                cs = slice(half * 512, half * 512 + 512)
                mm = nc.tensor.matmul(pout[0:R, cs], pown[s][:, :], vown[:, cs], start=False, stop=True)
            mm.then_inc(summed, 1)

        def pe_combine(pe, b):
            pe.wait_ge(kept_one, b + 1)
            nc.tensor.matmul(pscore[1][:, 0:TS], kept[:, :], comb[:, :], start=True, stop=True).then_inc(combined, 1)

        @block.tensor
        def _(pe):
            pe.wait_ge(lined, LINED)
            pe.wait_ge(columns, 1)
            for i in range(3):
                mm = nc.tensor.matmul(pscore[1][0:R, i:i + 1], line[0:1, i, :], c.ones[0:1, 0:1], start=True, stop=True)
            mm.then_inc(columns, 1)
            pe_k(pe, 0, 0, 0, very_first=True)
            pe_k(pe, 1, 1, 1)
            pe_turn(pe, 0, 0, 2)
            pe_v(pe, 0, 0, 1)

            def pair(g):
                b = g * 2
                pe_k(pe, b, 0, g * 4 - 1, hook=b - 2)
                pe_v(pe, b - 1, 1, b)
                pe_k(pe, b + 1, 1, g * 4 + 1, hook=b - 1)
                pe_v(pe, b, 0, b + 1)
            with pe.Fori(1, NB // 2 - 1) as g:
                pair(g)
            pair(NB // 2 - 1)
            pe_combine(pe, NB - 2)
            pe.wait_ge(placed, NB - 1)
            pe_v(pe, NB - 1, 1, None)
            pe_combine(pe, NB - 1)

        def dve_q(dve, b, s, first):
            if not first:
                dve.wait_ge(scored, b * EV)
            for m in range(2):
                rows = slice(m * HD, (m + 1) * HD)
                nc.vector.tensor_copy(qdiag[rows, :, m * NS:(m + 1) * NS],
                                      qs[rows, :, bass.ds(b * NS, NS)]).then_inc(q_laid, 1)

        def dve_q_low(dve, b, s):
            dve.wait_ge(qhi, b + 1)
            nc.vector.tensor_tensor(ql[s][:, :, :], qf[:, :, :], qh[s][:, :, :].bitcast(F32),
                                    ALU.subtract).then_inc(qlo, 1)

        def dve_k(dve, b, s, hook=None):
            def take(g, k):
                dve.wait_ge(scored, b * EV + g + 1)
                at = slice(g * 2 * P, (g + 1) * 2 * P) if isinstance(g, int) else bass.ds(g * 2 * P, 2 * P)
                nc.vector.scalar_tensor_tensor(sc[s][:, at], pscore[k][0:R, 0:2 * P], HD ** -0.5, bias[:, at],
                                               ALU.mult, ALU.add).then_inc(biased, 1)

            def body(i, first):
                for slot in range(RING):
                    n = b * PG + i * RING + slot
                    k = (slot // 2) % 2
                    dve.wait_ge(khi, n + 1)
                    nc.vector.tensor_tensor(kl[k][:, :, (slot % 2) * P:(slot % 2 + 1) * P],
                                            pk[slot % 2][:, :].rearrange("p (h t) -> p h t", h=HA),
                                            kh[k][:, :, (slot % 2) * P:(slot % 2 + 1) * P].bitcast(F32),
                                            ALU.subtract).then_inc(klo, 1)
                    if first and slot == 1 and hook is not None:
                        dve_rows(dve, hook, s)
                    if slot % 2 == 1 and not (first and slot == 1):
                        take(i * (RING // 2) + slot // 2 - 1, (slot // 2 - 1) % 2)
            body(0, True)
            with dve.Fori(1, PG // RING) as i:
                body(i, False)
            take(GR - 1, (GR - 1) % 2)
            dve.wait_ge(scored, b * EV + EV)
            nc.vector.scalar_tensor_tensor(sc[s][:, PAST:KEYS], pscore[0][0:R, 0:TS], HD ** -0.5,
                                           own_bias[:, bass.ds(b, 1), :].rearrange("r o t -> r (o t)"),
                                           ALU.mult, ALU.add).then_inc(biased, 1)

        def dve_top(dve, b, s, i):
            if i == 0:
                dve.wait_ge(biased, b * EV + EV)
            if i < PIECES:
                nc.vector.tensor_reduce(tops[:, i:i + 1], sc[s][:, i * PW:(i + 1) * PW], AX,
                                        ALU.max).then_inc(topped, 1)
            else:
                dve.wait_ge(topped, b * (PIECES + 1) + PIECES)
                nc.vector.tensor_reduce(tops[:, PIECES:PIECES + 1], tops[:, 0:PIECES], AX,
                                        ALU.max).then_inc(topped, 1)
                dve.wait_ge(topped, b * (PIECES + 1) + PIECES + 1)
                nc.vector.tensor_scalar(low[:, s:s + 1], tops[:, PIECES:PIECES + 1], -1.0, None,
                                        ALU.mult).then_inc(lowered, 1)

        def dve_turn(dve, b, s, i):
            dve.wait_ge(phi, b * 2 + i + 1)
            half = slice(i * (PG // 2), (i + 1) * (PG // 2))
            nc.vector.tensor_tensor(pl[s][:, half, :], pk[i][:, :].rearrange("p (j r) -> p j r", r=R),
                                    ph[s][:, half, :].bitcast(F32), ALU.subtract).then_inc(plo, 1)

        def dve_v(dve, b, s, following, next_q):
            for p in range(PG):
                dve.wait_ge(vhi, b * PG + p + 1)
                nc.vector.tensor_tensor(vslot(kl, p), ring[:, p % RING, :], vslot(kh, p).bitcast(F32),
                                        ALU.subtract).then_inc(vlo, 1)
                if following is not None and p % 3 == 1 and p // 3 <= PIECES:
                    dve_top(dve, following, 1 - s, p // 3)
                if next_q is not None and p == 16:
                    dve_q(dve, next_q, s, False)
                if next_q is not None and p == 20:
                    dve_q_low(dve, next_q, s)
                if following is not None and p in TURNED_AT:
                    dve_turn(dve, following, 1 - s, TURNED_AT.index(p))

        def dve_rows(dve, b, s):
            nc.vector.tensor_reduce(coef[:, 0:1], dens[:, s, :], AX, ALU.add).then_inc(inverted, 1)
            dve.wait_ge(inverted, b * 3 + 1)
            nc.vector.reciprocal(coef[:, 1:2], coef[:, 0:1]).then_inc(inverted, 1)
            dve.wait_ge(inverted, b * 3 + 2)
            nc.vector.tensor_tensor(coef[:, 0:1], coef[:, 1:2], cols[:, 2:3], ALU.mult).then_inc(inverted, 1)
            dve.wait_ge(inverted, b * 3 + 3)
            dve.wait_ge(summed, b + 1)
            if not (isinstance(b, int) and b == 0):
                dve.wait_ge(kept_one, b)
            for h in range(2):
                ins = nc.vector.scalar_tensor_tensor(
                    own_rows[:, h * 512:(h + 1) * 512].rearrange("r (h e) -> r h e", e=VD),
                    pout[0:R, h * 512:(h + 1) * 512].rearrange("r (h e) -> r h e", e=VD), coef[:, 0:1],
                    heads[:, h * 4:h * 4 + 4].rearrange("r (h o) -> r h o", o=1).to_broadcast([R, 4, VD]),
                    ALU.mult, ALU.mult)
            ins.then_inc(kept_all, 1)
            dve.wait_ge(kept_all, b + 1)
            if not (isinstance(b, int) and b == 0):
                dve.wait_ge(combined, b)
            nc.vector.tensor_reduce(kept[:, :], own_rows[:, :].rearrange("r (h e) -> r e h", e=VD), AX,
                                    ALU.add).then_inc(kept_one, 1)

        @block.vector
        def _(dve):
            V = nc.vector
            dve.wait_ge(lined, LINED)
            l3 = line[:, 2, :].rearrange("o (h m q) -> o h m q", m=2, q=NS)
            V.tensor_scalar(l3[:, :, 1, :], l3[:, :, 1, :], c.neg_lam[0:1, :], None, ALU.mult).then_inc(columns, 1)
            idn = c.ident[0:R, 0:R].rearrange("r (h m q) -> r h m q", m=2, q=NS)
            V.tensor_tensor(comb[:, :].rearrange("r (h q) -> r h q", q=NS), idn[:, :, 0, :], idn[:, :, 1, :],
                            ALU.add).then_inc(consts, 1)
            V.memset(qflat[:, :], 0.0).then_inc(consts, 1)
            dve.wait_ge(columns, 2)
            V.tensor_copy(cols[:, :], pscore[1][0:R, 0:3]).then_inc(consts, 1)
            dve.wait_ge(consts, 3)
            V.tensor_scalar(bias[:, :], bias[:, :], cols[:, 1:2], cols[:, 0:1], ALU.subtract, ALU.mult)\
                .then_inc(consts, 1)
            ob = own_bias[:, :, :].rearrange("r b t -> r (b t)")
            V.tensor_scalar(sc[0][:, 0:NB * TS], ob, cols[:, 1:2], 0.0, ALU.subtract, ALU.is_gt).then_inc(own_bias_steps, 1)
            dve.wait_ge(own_bias_steps, 1)
            V.tensor_scalar(ob, ob, cols[:, 1:2], cols[:, 0:1], ALU.subtract, ALU.mult).then_inc(own_bias_steps, 1)
            dve.wait_ge(own_bias_steps, 2)
            V.scalar_tensor_tensor(ob, sc[0][:, 0:NB * TS], FILL, ob, ALU.mult, ALU.add).then_inc(consts, 1)
            dve.wait_ge(consts, 6)
            dve.wait_ge(inputs_in, 48)
            dve_q(dve, 0, 0, True)
            dve_q_low(dve, 0, 0)
            dve_k(dve, 0, 0)
            for i in range(PIECES + 1):
                dve_top(dve, 0, 0, i)
            dve_q(dve, 1, 1, False)
            dve_q_low(dve, 1, 1)
            dve_k(dve, 1, 1)
            for i in range(2):
                dve_turn(dve, 0, 0, i)
            dve_v(dve, 0, 0, 1, 2)

            def pair(g, next_q):
                b = g * 2
                dve_k(dve, b, 0, b - 2)
                dve_v(dve, b - 1, 1, b, b + 1)
                dve_k(dve, b + 1, 1, b - 1)
                dve_v(dve, b, 0, b + 1, b + 2 if next_q else None)
            with dve.Fori(1, NB // 2 - 1) as g:
                pair(g, True)
            pair(NB // 2 - 1, False)
            dve_rows(dve, NB - 2, 0)
            dve_v(dve, NB - 1, 1, None, None)
            dve_rows(dve, NB - 1, 1)

        def act_q(act, b, s):
            act.wait_ge(q_laid, b * 2 + 2)
            nc.scalar.activation(qh[s][:, :, :], qf[:, :, :], ACT.Copy).then_inc(qhi, 1)

        def act_k(act, b, s, hook=None):
            if not (isinstance(b, int) and b == 0) and hook is None:
                act.wait_ge(scored, b * EV)

            def body(i, first):
                for slot in range(RING):
                    n = b * PG + i * RING + slot
                    k = (slot // 2) % 2
                    act.wait_ge(kturned, n + 1)
                    if first and slot == 0 and hook is not None:
                        act.wait_ge(valued, (b - 1) * PG)
                    if slot % 2 == 0 and not (first and slot < 4):
                        act.wait_ge(scored, b * EV + i * (RING // 2) + (slot // 2 - 1))
                    nc.scalar.activation(kh[k][:, :, (slot % 2) * P:(slot % 2 + 1) * P],
                                         pk[slot % 2][:, :].rearrange("p (h t) -> p h t", h=HA),
                                         ACT.Copy).then_inc(khi, 1)
                    if first and slot == 3 and hook is not None:
                        act_place(act, hook)
            body(0, True)
            with act.Fori(1, PG // RING) as i:
                body(i, False)

        def act_exp(act, b, s, i):
            if i == 0:
                act.wait_ge(lowered, b + 1)
            nc.scalar.activation(sc[s][:, i * PW:(i + 1) * PW], sc[s][:, i * PW:(i + 1) * PW], ACT.Exp,
                                 bias=low[:, s:s + 1], accum_out=dens[:, s, i:i + 1]).then_inc(raised, 1)

        def act_place(act, b):
            act.wait_ge(combined, b + 1)
            nc.scalar.activation(mix[:, 0:HA, bass.ds(TP + b * NS, NS)],
                                 pscore[1][:, 0:TS].rearrange("p (h q) -> p h q", q=NS), ACT.Copy).then_inc(placed, 1)

        def act_turn(act, b, s, i):
            act.wait_ge(pturned, b * 2 + i + 1)
            nc.scalar.activation(ph[s][:, i * (PG // 2):(i + 1) * (PG // 2), :],
                                 pk[i][:, :].rearrange("p (j r) -> p j r", r=R), ACT.Copy).then_inc(phi, 1)
            if i == 1:
                act.wait_ge(own_turned, b + 1)
                nc.scalar.activation(pown[s][:, :], pscore[0][0:TS, 0:R], ACT.Copy).then_inc(own_out, 1)

        def act_v(act, b, s, f, following, next_q, kphases):
            act.wait_ge(scored, kphases * EV)
            for p in range(PG):
                act.wait_ge(page_in[p % RING], f * (16 * PG // RING) + (p // RING + 1) * 16)
                if p >= 4:
                    act.wait_ge(valued, b * PG + p - 3)
                elif following is None:
                    act.wait_ge(valued, (b - 1) * PG + (PG + p - 3))
                nc.scalar.activation(vslot(kh, p), ring[:, p % RING, :], ACT.Copy).then_inc(vhi, 1)
                if following is not None and p in (15, 18, 21, 24):
                    act_exp(act, following, 1 - s, (p - 15) // 3)
                if next_q is not None and p == 17:
                    act_q(act, next_q, s)
                if following is not None and p in TURNED_AT:
                    act_turn(act, following, 1 - s, TURNED_AT.index(p))

        @block.scalar
        def _(act):
            act_q(act, 0, 0)
            act_k(act, 0, 0)
            for i in range(PIECES):
                act_exp(act, 0, 0, i)
            act_q(act, 1, 1)
            act_k(act, 1, 1)
            for i in range(2):
                act_turn(act, 0, 0, i)
            act_v(act, 0, 0, 2, 1, 2, 2)

            def pair(g, next_q):
                b = g * 2
                act_k(act, b, 0, b - 2)
                act_v(act, b - 1, 1, g * 4, b, b + 1, b + 1)
                act_k(act, b + 1, 1, b - 1)
                act_v(act, b, 0, g * 4 + 2, b + 1, b + 2 if next_q else None, b + 2)
            with act.Fori(1, NB // 2 - 1) as g:
                pair(g, True)
            pair(NB // 2 - 1, False)
            act_place(act, NB - 2)
            act_v(act, NB - 1, 1, 2 * NB - 1, None, None, NB)
            act_place(act, NB - 1)


def finish_heads(nc, d, a, sems, c, z_dram, mix, mhi, mlo):
    T, E, NH = d.t, d.md // P, d.ha + d.hm
    cog = (3 * d.aw + 2 * d.mw) // P
    with ExitStack() as ctx:
        sb = lambda x, s, t=F32: ctx.enter_context(nc.sbuf_tensor(x, s, t))
        sq = [sb(f"fh_sq{i}", [P, T]) for i in range(2)]
        root = [sb(f"fh_root{i}", [P, T]) for i in range(2)]
        og = [sb(f"fh_og{i}", [P, E, T]) for i in range(2)]
        gains = sb("fh_gains", [P, 1 + E])
        over = sb("fh_over", [P, 2, P])
        mean = [[ctx.enter_context(nc.psum_tensor(f"fh_mean{i}{h}", [P, 512], F32)) for h in range(2)]
                for i in range(2)]
        gains_in, consts, gated_own = sems("fh_gains_in"), sems("fh_consts"), sems("fh_normed")
        og_in = [sems(f"fh_og_in{i}") for i in range(2)]
        squared, summed, rooting, rooted, inverted, gated, scaled, hi_made, lo_made = (sems(f"fh_{x}") for x in (
            "squared", "summed", "rooting", "rooted", "inverted", "gated", "scaled", "hi_made", "lo_made"))
        parts = [(h, 1) for h in range(d.ha)] + [(d.ha + h * E, E) for h in range(d.hm)]
        first = [sum(w for _, w in parts[:i]) for i in range(NH + 1)]
        ogv = z_dram[0:(cog + d.hm * E) * P, :].rearrange("(c e p) t -> c p e t", e=E, p=P)
        block = ctx.enter_context(nc.Block())

        @block.sync
        def _(sp):
            sp.dma_start(gains[:, 0:1], a["attn_out_norm"].rearrange("o p -> p o"),
                         allow_slow_non_contiguous=True).then_inc(gains_in, 16)
            sp.dma_start(gains[:, 1:1 + E], a["mlstm_out_norm"][0].rearrange("(e p) -> p e", p=P),
                         allow_slow_non_contiguous=True).then_inc(gains_in, 16)
            for h in range(d.hm):
                if h >= 2:
                    sp.wait_ge(scaled, first[d.ha + h - 1])
                sp.dma_start(og[h % 2][:, :, :], ogv[cog // E + h]).then_inc(og_in[h % 2], 16)

        @block.vector
        def _(dve):
            V = nc.vector
            V.memset(over[:, 0, :], 1.0 / d.vd).then_inc(consts, 1)
            V.memset(over[:, 1, :], 1.0 / d.md).then_inc(consts, 1)
            dve.wait_ge(gains_in, 32)
            V.tensor_scalar(gains[:, 0:1], gains[:, 0:1], 1.0 - LAM_INIT, None, ALU.mult).then_inc(consts, 1)
            dve.wait_ge(consts, 3)

            def square(i):
                for j in range(parts[i][1]):
                    n = first[i] + j
                    if n >= 2:
                        dve.wait_ge(summed, n - 1)
                    x = mix[:, n, :]
                    V.tensor_tensor(sq[n % 2][:, :], x, x, ALU.mult).then_inc(squared, 1)

            def root_of(i):
                dve.wait_ge(summed, first[i + 1])
                if i >= 2:
                    dve.wait_ge(scaled, first[i - 1])
                for h in range(2):
                    V.tensor_scalar(root[i % 2][:, h * d.half:(h + 1) * d.half], mean[i % 2][h][:, 0:d.half], EPS,
                                    None, ALU.add).then_inc(rooting, 1)

            def scale(i):
                dve.wait_ge(rooted, i + 1)
                V.reciprocal(root[i % 2][:, :], root[i % 2][:, :]).then_inc(inverted, 1)
                dve.wait_ge(inverted, i + 1)
                for j in range(parts[i][1]):
                    n = first[i] + j
                    gain = gains[:, 0:1] if i < d.ha else gains[:, 1 + j:2 + j]
                    ins = V.scalar_tensor_tensor(mix[:, n, :], mix[:, n, :], gain, root[i % 2][:, :], ALU.mult,
                                                 ALU.mult)
                    if i >= d.ha:
                        ins.then_inc(gated_own, 1)
                        dve.wait_ge(gated_own, n - d.ha + 1)
                        dve.wait_ge(gated, i - d.ha + 1)
                        ins = V.tensor_tensor(mix[:, n, :], mix[:, n, :], og[(i - d.ha) % 2][:, j, :], ALU.mult)
                    ins.then_inc(scaled, 1)
                    if n >= 1:
                        trail(n - 1)

            def trail(n):
                dve.wait_ge(hi_made, n + 1)
                V.tensor_tensor(mlo[:, n, :], mix[:, n, :], mhi[:, n, :].bitcast(F32), ALU.subtract)\
                    .then_inc(lo_made, 1)

            square(0)
            for i in range(NH):
                root_of(i)
                if i + 1 < NH:
                    square(i + 1)
                scale(i)
            trail(d.kc - 1)

        @block.scalar
        def _(act):
            def sigmoid(h):
                act.wait_ge(og_in[h % 2], 16 * (h // 2 + 1))
                nc.scalar.activation(og[h % 2][:, :, :], og[h % 2][:, :, :], ACT.Sigmoid).then_inc(gated, 1)
            for h in range(2):
                sigmoid(h)
            for i in range(NH):
                act.wait_ge(rooting, 2 * i + 2)
                nc.scalar.activation(root[i % 2][:, :], root[i % 2][:, :], ACT.Sqrt).then_inc(rooted, 1)
                for j in range(parts[i][1]):
                    n = first[i] + j
                    act.wait_ge(scaled, n + 1)
                    nc.scalar.activation(mhi[:, n, :], mix[:, n, :], ACT.Copy).then_inc(hi_made, 1)
                if i >= d.ha and i + 2 < NH:
                    sigmoid(i - d.ha + 2)

        @block.tensor
        def _(pe):
            pe.wait_ge(consts, 2)
            for i in range(NH):
                if i >= 2:
                    pe.wait_ge(rooting, 2 * i - 2)
                for j in range(parts[i][1]):
                    n = first[i] + j
                    pe.wait_ge(squared, n + 1)
                    for h in range(2):
                        mm = nc.tensor.matmul(mean[i % 2][h][:, 0:d.half], over[:, 0 if i < d.ha else 1, :],
                                              sq[n % 2][:, h * d.half:(h + 1) * d.half], start=(j == 0),
                                              stop=(j == parts[i][1] - 1))
                    mm.then_inc(summed, 1)


def output_projection(nc, d, a, sems, mhi, mlo, x_dram, xt):
    N, GROUP = d.kc, Flow.RAW
    with ExitStack() as ctx:
        flow = Flow(nc, ctx, d, "wout", sems)
        acc = [[ctx.enter_context(nc.psum_tensor(f"o_acc{i}{h}", [P, 512], F32)) for h in range(2)]
               for i in range(2)]
        residual_in, added = sems("o_residual_in"), sems("o_added")
        w = a["w_out"][0].rearrange("(k p) n -> p k n", p=P)
        tile = lambda x, j: x[:, j, :].rearrange("p (k n) -> p k n", k=d.kc)
        block = ctx.enter_context(nc.Block())

        @block.sync
        def _(sp):
            for j in range(GROUP):
                sp.dma_start(tile(flow.raw, j), w[:, :, j * P:(j + 1) * P]).then_inc(flow.landed[j], 16)
            sp.dma_start(xt[:, :, :], x_dram.rearrange("(k p) t -> p k t", p=P)).then_inc(residual_in, 16)
            with sp.Fori(0, N // GROUP - 1) as g:
                for j in range(GROUP):
                    sp.wait_ge(flow.lo_made, g * GROUP + (j + 1))
                    sp.dma_start(tile(flow.raw, j), w[:, :, bass.ds((g * GROUP + (GROUP + j)) * P, P)])\
                        .then_inc(flow.landed[j], 16)

        def act_group(act, g, first):
            for j in range(GROUP):
                act.wait_ge(flow.landed[j], g * 16 + 16)
                if not (first and j < 2):
                    act.wait_ge(flow.used, g * GROUP + (j - 1))
                nc.scalar.activation(flow.hi[:, j % 2, :], flow.raw[:, j, :], ACT.Copy).then_inc(flow.hi_made, 1)

        @block.scalar
        def _(act):
            act_group(act, 0, True)
            with act.Fori(1, N // GROUP) as g:
                act_group(act, g, False)

        def add(dve, n, j):
            dve.wait_ge(flow.used, n + 1)
            at = bass.ds(n, 1)
            for h in range(2):
                cs = slice(h * d.half, (h + 1) * d.half)
                nc.vector.tensor_tensor(xt[:, at, cs], xt[:, at, cs],
                                        acc[j % 2][h][:, 0:d.half].rearrange("p (o t) -> p o t", o=1),
                                        ALU.add).then_inc(added, 1)

        def dve_group(dve, g, first):
            for j in range(GROUP):
                n = g * GROUP + j
                dve.wait_ge(flow.hi_made, n + 1)
                nc.vector.tensor_tensor(flow.lo[:, j % 2, :], flow.raw[:, j, :], flow.hi[:, j % 2, :].bitcast(F32),
                                        ALU.subtract).then_inc(flow.lo_made, 1)
                if not (first and j == 0):
                    add(dve, n - 1, (j - 1) % 2)

        @block.vector
        def _(dve):
            dve.wait_ge(residual_in, 16)
            dve_group(dve, 0, True)
            with dve.Fori(1, N // GROUP) as g:
                dve_group(dve, g, False)
            add(dve, N - 1, 1)

        def pe_tile(pe, n, j, first=False):
            pe.wait_ge(flow.lo_made, n + 1)
            if not first:
                pe.wait_ge(added, n * 2 - 2)
            whi, wlo = tile(flow.hi, j), tile(flow.lo, j)
            for h in range(2):
                cs = slice(h * d.half, (h + 1) * d.half)
                for k in range(d.kc):
                    mm = exact_passes(nc, acc[j][h][:, 0:d.half], whi[:, k, :], wlo[:, k, :], mhi[:, k, cs],
                                      mlo[:, k, cs], k == 0, k == d.kc - 1)
            mm.then_inc(flow.used, 1)

        @block.tensor
        def _(pe):
            for j in range(2):
                pe_tile(pe, j, j, True)
            with pe.Fori(1, N // 2) as g:
                for j in range(2):
                    pe_tile(pe, g * 2 + j, j)


def second_norm(nc, d, a, sems, xt, xhi, xlo):
    with ExitStack() as ctx:
        gain = ctx.enter_context(nc.sbuf_tensor("norm_ffn_cols", [P, d.kc], F32))
        norm = NormBuffers(nc, ctx, d, sems, "ffn")
        gain_in = sems("norm_ffn_in")
        block = ctx.enter_context(nc.Block())

        @block.sync
        def _(sp):
            sp.dma_start(gain[:, :], a["norm_ffn"][0].rearrange("(k p) -> p k", p=P),
                         allow_slow_non_contiguous=True).then_inc(gain_in, 16)

        @block.tensor
        def _(pe):
            norm_tensor(nc, pe, d, norm)

        @block.scalar
        def _(act):
            norm_scalar(nc, act, d, norm, xhi)

        @block.vector
        def _(dve):
            dve.wait_ge(gain_in, 16)
            norm_vector(nc, dve, d, norm, xt, gain, xhi, xlo)


def mlp(nc, d, a, sems, xhi, xlo, xt):
    G, GROUPS = 4, d.ff // (4 * P)
    OUT = d.kc // G
    assert OUT == 4 and Flow.RAW == G
    with ExitStack() as ctx:
        sb = lambda x, s, t=F32: ctx.enter_context(nc.sbuf_tensor(x, s, t))
        flow = Flow(nc, ctx, d, "ffn", sems)
        hid = sb("hidden", [P, 2, d.t])
        hhi, hlo = (sb(f"hidden_{x}", [P, G, d.t], F32R) for x in ("hi", "lo"))
        acc = [ctx.enter_context(nc.psum_tensor(f"f_acc{i}", [P, 2, 512], F32)) for i in range(4)]
        relued, squared, h_hi, h_lo, added = (sems(f"ffn_{x}") for x in ("relued", "squared", "h_hi", "h_lo", "added"))
        up = a["w_up"][0].rearrange("(k p) n -> p k n", p=P)
        down = a["w_down"][0].rearrange("(g k p) n -> g p k n", k=G, p=P)
        up_tile = lambda x, j: x[:, j, :].rearrange("p (k n) -> p k n", k=d.kc)
        down_tile = lambda x, j: x[:, j, :].rearrange("p (k n) -> p k n", k=G)
        halves = lambda x: x.rearrange("p (h t) -> p h t", h=2)
        block = ctx.enter_context(nc.Block())

        def groups(eng, run):
            run(0, True)
            with eng.Fori(1, GROUPS) as g:
                run(g, False)

        @block.sync
        def _(sp):
            def load(g, first):
                for j in range(G):
                    if not first:
                        sp.wait_ge(flow.lo_made, g * (2 * G) - (G - 1 - j))
                    sp.dma_start(up_tile(flow.raw, j), up[:, :, bass.ds((g * G + j) * P, P)])\
                        .then_inc(flow.landed[j], 16)
                for j in range(G):
                    sp.wait_ge(flow.lo_made, g * (2 * G) + j + 1)
                    sp.dma_start(down_tile(flow.raw, j), down[g][:, :, j * OUT * P:(j + 1) * OUT * P])\
                        .then_inc(flow.landed[j], 16)
            groups(sp, load)

        @block.scalar
        def _(act):
            def split(g, i, first):
                act.wait_ge(flow.landed[i % G], g * 32 + 16 * (i // G + 1))
                if not (first and i < 2):
                    act.wait_ge(flow.used, g * 32 + (4 * i - 4))
                nc.scalar.activation(flow.hi[:, i % 2, :], flow.raw[:, i % G, :], ACT.Copy).then_inc(flow.hi_made, 1)

            def hidden(g, j, first):
                act.wait_ge(flow.used, g * 32 + 4 * (j + 1))
                if not (first and j < 2):
                    act.wait_ge(h_lo, g * G + (j - 1))
                nc.scalar.activation(halves(hid[:, j % 2, :]), acc[j % 2][:, :, 0:d.half], ACT.Relu)\
                    .then_inc(relued, 1)
                act.wait_ge(squared, g * G + (j + 1))
                nc.scalar.activation(hhi[:, j, :], hid[:, j % 2, :], ACT.Copy).then_inc(h_hi, 1)

            def run(g, first):
                for i in range(2 * G):
                    split(g, i, first)
                    if 1 <= i <= G:
                        hidden(g, i - 1, first)
            groups(act, run)

        @block.vector
        def _(dve):
            def hidden(g, j):
                n = g * G + (j + 1)
                dve.wait_ge(relued, n)
                nc.vector.tensor_tensor(hid[:, j % 2, :], hid[:, j % 2, :], hid[:, j % 2, :], ALU.mult)\
                    .then_inc(squared, 1)
                dve.wait_ge(h_hi, n)
                nc.vector.tensor_tensor(hlo[:, j, :], hid[:, j % 2, :], hhi[:, j, :].bitcast(F32), ALU.subtract)\
                    .then_inc(h_lo, 1)

            def add(g, j):
                for i in range(OUT):
                    oc = j * OUT + i
                    dve.wait_ge(flow.used, g * 32 + (4 * (G + j) + i + 1))
                    nc.vector.tensor_tensor(halves(xt[:, oc, :]), halves(xt[:, oc, :]),
                                            acc[2 + i % 2][:, :, 0:d.half], ALU.add).then_inc(added, 1)

            def run(g, first):
                for i in range(2 * G):
                    dve.wait_ge(flow.hi_made, g * (2 * G) + (i + 1))
                    nc.vector.tensor_tensor(flow.lo[:, i % 2, :], flow.raw[:, i % G, :],
                                            flow.hi[:, i % 2, :].bitcast(F32), ALU.subtract).then_inc(flow.lo_made, 1)
                    if i == 0 and not first:
                        add(g - 1, G - 1)
                    if 1 <= i <= G:
                        hidden(g, i - 1)
                    if i > G:
                        add(g, i - G - 1)
            groups(dve, run)
            add(GROUPS - 1, G - 1)

        @block.tensor
        def _(pe):
            def run(g, first):
                for j in range(G):
                    pe.wait_ge(flow.lo_made, g * (2 * G) + (j + 1))
                    if not (first and j < 2):
                        pe.wait_ge(relued, g * G + (j - 1))
                    whi, wlo = up_tile(flow.hi, j % 2), up_tile(flow.lo, j % 2)
                    for h in range(2):
                        cs = slice(h * d.half, (h + 1) * d.half)
                        for k in range(d.kc):
                            mm = exact_passes(nc, acc[j % 2][:, h, 0:d.half], whi[:, k, :], wlo[:, k, :],
                                              xhi[:, k, cs], xlo[:, k, cs], k == 0, k == d.kc - 1)
                            if h and k % 4 == 3:
                                mm.then_inc(flow.used, 1)
                for j in range(G):
                    pe.wait_ge(flow.lo_made, g * (2 * G) + (G + j + 1))
                    whi, wlo = down_tile(flow.hi, j % 2), down_tile(flow.lo, j % 2)
                    for i in range(OUT):
                        if not (first and j == 0 and i < 2):
                            pe.wait_ge(added, g * d.kc + (j * OUT + i - 1))
                        ws = slice(i * P, (i + 1) * P)
                        for ks in (range(G - 1), (G - 1,)):
                            if j == 0 and i == 0 and ks == (G - 1,):
                                pe.wait_ge(h_lo, g * G + G)
                            elif j == 0 and i == 0:
                                pe.wait_ge(h_lo, g * G + (G - 1))
                            for h in range(2):
                                cs = slice(h * d.half, (h + 1) * d.half)
                                for k in ks:
                                    mm = exact_passes(nc, acc[2 + i % 2][:, h, 0:d.half], whi[:, k, ws], wlo[:, k, ws],
                                                      hhi[:, k, cs], hlo[:, k, cs], k == 0, k == G - 1)
                        mm.then_inc(flow.used, 1)
            groups(pe, run)


def emit(nc, d, sems, c, xt, y_prompt, y_sample):
    tiles = [(N_META + i * P, P) for i in range(d.seq // P)] + [(d.tp, d.tsmp)]
    QUAD = 4
    with ExitStack() as ctx:
        y = [ctx.enter_context(nc.sbuf_tensor(f"y_rows{i}", [P, d.dm], F32)) for i in range(2)]
        turned = [ctx.enter_context(nc.psum_tensor(f"y_turned{i}", [P, d.kc * P], F32)) for i in range(2)]
        ready, out_a, out_b = sems("y_turned_ready"), sems("y_out_a"), sems("y_out_b")
        stored = [sems(f"y_stored{i}") for i in range(2)]
        block = ctx.enter_context(nc.Block())
        mid = d.dm // 2

        @block.tensor
        def _(pe):
            for i, (t0, n) in enumerate(tiles):
                if i >= 2:
                    pe.wait_ge(out_a, i - 1)
                    pe.wait_ge(out_b, i - 1)
                for k in range(d.kc):
                    mm = nc.tensor.transpose(turned[i % 2][0:n, k * P:(k + 1) * P], xt[:, k, t0:t0 + n], c.ident[:, :])
                mm.then_inc(ready, 1)

        @block.scalar
        def _(act):
            for i, (t0, n) in enumerate(tiles):
                act.wait_ge(ready, i + 1)
                if i >= 2:
                    act.wait_ge(stored[i % 2], 16 * (i // 2))
                nc.scalar.activation(y[i % 2][0:n, 0:mid], turned[i % 2][0:n, 0:mid], ACT.Copy).then_inc(out_a, 1)

        @block.vector
        def _(dve):
            for i, (t0, n) in enumerate(tiles):
                dve.wait_ge(ready, i + 1)
                if i >= 2:
                    dve.wait_ge(stored[i % 2], 16 * (i // 2))
                nc.vector.tensor_copy(y[i % 2][0:n, mid:], turned[i % 2][0:n, mid:]).then_inc(out_b, 1)

        @block.sync
        def _(sp):
            for i, (t0, n) in enumerate(tiles):
                sp.wait_ge(out_a, i + 1)
                sp.wait_ge(out_b, i + 1)
                dst = y_prompt[0][t0 - N_META:t0 - N_META + n, :] if t0 < d.tp else \
                    y_sample.rearrange("b s m -> (b s) m")
                sp.dma_start(dst, y[i % 2][0:n, :]).then_inc(stored[i % 2], 16)
            for i in range(2):
                sp.wait_ge(stored[i], 16 * ((len(tiles) - i + 1) // 2))


def output_shapes(a):
    d = Dims(a)
    return [(1, d.seq, d.dm), (d.nb, d.ns, d.dm),
            (1, 1, d.tp, d.ha, d.vd), (1, 1, d.tp, d.ha, d.vd), (1, 1, d.hm, d.md, d.md), (1, 1, d.hm, d.md),
            (1, 1, d.hm), (1, 1, a["conv_w"].shape[1] - 1, d.mw),
            (1, d.nb, d.ns, d.ha, d.vd), (1, d.nb, d.ns, d.ha, d.vd), (1, d.nb, d.hm, d.md, d.md),
            (1, d.nb, d.hm, d.md), (1, d.nb, d.hm), (1, d.nb, a["conv_w"].shape[1] - 1, d.mw)]


def build(nc, a, outs):
    d = Dims(a)
    y_prompt, y_sample, k_prompt, v_prompt, c_prompt, n_prompt, m_prompt, conv_prompt, \
        k_sample, v_sample, c_sample, n_sample, m_sample, conv_sample = outs
    with ExitStack() as ctx:
        scratch = lambda n, s: nc.dram_tensor(n, s, F32).ap()
        tokens = lambda x: x.rearrange("o b t h e -> (o b t) (h e)")
        c = Consts(nc, ctx, d)
        with stage(nc) as sems:
            setup(nc, d, a, sems, c)
        xt_dram = scratch("xt_scratch", [d.dm, d.t])
        z_dram = scratch("z_scratch", [d.pw, d.t])
        zn_dram = scratch("zn_scratch", [2 * d.aw, d.t])
        qk_dram = scratch("qk_scratch", [2 * d.mw, d.t])
        kt_dram = scratch("kt_scratch", [d.t, d.mw])
        vt_dram = scratch("vt_scratch", [d.t, d.mw])
        g_dram = scratch("g_scratch", [4, d.hm, d.t])
        with ExitStack() as one:
            xhi = one.enter_context(nc.sbuf_tensor("xn_hi", [P, d.kc, d.t], F32R))
            xlo = one.enter_context(nc.sbuf_tensor("xn_lo", [P, d.kc, d.t], F32R))
            with stage(nc) as sems:
                embed_and_norm(nc, d, a, sems, c.ident, xhi, xlo, xt_dram)
            with stage(nc) as sems:
                input_projection(nc, d, a, sems, xhi, xlo, z_dram)
        with stage(nc) as sems:
            gates(nc, d, a, sems, z_dram, g_dram, m_prompt, m_sample)
        with ExitStack() as three:
            mix = three.enter_context(nc.sbuf_tensor("mix_t", [P, d.kc, d.t], F32))
            with stage(nc) as sems:
                heads_prepare(nc, d, a, sems, c, z_dram, zn_dram, tokens(k_prompt), tokens(v_prompt),
                              tokens(k_sample), tokens(v_sample))
            with stage(nc) as sems:
                prompt_attention(nc, d, a, sems, c, zn_dram, tokens(v_prompt), mix)
            with stage(nc) as sems:
                mlstm_features(nc, d, a, sems, c, z_dram, qk_dram, kt_dram, vt_dram, conv_prompt, conv_sample)
            with stage(nc) as sems:
                prompt_mlstm(nc, d, a, sems, c, qk_dram, kt_dram, vt_dram, g_dram, mix, c_prompt, n_prompt)
            with stage(nc) as sems:
                sample_mlstm(nc, d, a, sems, c, qk_dram, kt_dram, vt_dram, g_dram, mix, c_sample, n_sample)
            with stage(nc) as sems:
                decode_attention(nc, d, a, sems, c, zn_dram, tokens(v_sample), mix)
            with ExitStack() as four:
                mhi = four.enter_context(nc.sbuf_tensor("mix_hi", [P, d.kc, d.t], F32R))
                mlo = four.enter_context(nc.sbuf_tensor("mix_lo", [P, d.kc, d.t], F32R))
                with stage(nc) as sems:
                    finish_heads(nc, d, a, sems, c, z_dram, mix, mhi, mlo)
                with stage(nc) as sems:
                    output_projection(nc, d, a, sems, mhi, mlo, xt_dram, mix)
            xhi = three.enter_context(nc.sbuf_tensor("xf_hi", [P, d.kc, d.t], F32R))
            xlo = three.enter_context(nc.sbuf_tensor("xf_lo", [P, d.kc, d.t], F32R))
            with stage(nc) as sems:
                second_norm(nc, d, a, sems, mix, xhi, xlo)
            with stage(nc) as sems:
                mlp(nc, d, a, sems, xhi, xlo, mix)
            with stage(nc) as sems:
                emit(nc, d, sems, c, mix, y_prompt, y_sample)


_INS = ["x_prompt", "x_sample", "cache_k", "cache_v", "state_C", "state_n", "state_m", "state_conv", "page_table",
        "meta_tokens", "norm_mix", "w_in", "q_norm", "k_norm", "lambda_qk", "attn_out_norm", "conv_w", "conv_b",
        "w_qm", "w_km", "gate_bias", "mlstm_out_norm", "w_out", "norm_ffn", "w_up", "w_down"]


def kernel(**inputs):
    import numpy as _np
    import concourse.bacc as _bacc
    from concourse import mybir as _mybir
    from concourse.bass_utils import run_bass_kernel_spmd as _run

    nc = _bacc.Bacc("TRN2", target_bir_lowering=False, num_devices=1)
    arrays, a = {}, {}
    for name in _INS:
        x = _np.ascontiguousarray(inputs[name])
        arrays[f"in_{name}"] = x
        a[name] = nc.dram_tensor(f"in_{name}", x.shape, _mybir.dt.from_np(x.dtype), kind="ExternalInput").ap()
    shapes = output_shapes(a)
    outs = [nc.dram_tensor(f"out_{i}", s, F32, kind="ExternalOutput").ap() for i, s in enumerate(shapes)]
    build(nc, a, outs)
    r = _run(nc, [arrays], core_ids=[0])
    return tuple(r.results[0][f"out_{i}"] for i in range(len(shapes)))
```

```python
from contextlib import ExitStack, contextmanager
import math

import concourse.bass as bass
from concourse import mybir

F32 = mybir.dt.float32
F32R = mybir.dt.float32r
I32 = mybir.dt.int32
ALU = mybir.AluOpType
ACT = mybir.ActivationFunctionType
AX = mybir.AxisListType.X

P = 128
N_META = 16
EPS = 1e-6
FILL = -1.0e30
LAM_INIT = 0.8 - 0.6 * math.exp(-0.3 * 0)


class Dims:

    def __init__(self, a):
        _, self.seq, self.dm = a["x_prompt"].shape
        self.nb, self.ns, _ = a["x_sample"].shape
        _, self.pool, self.page, self.ha, self.vd = a["cache_k"].shape
        self.hd = self.vd // 2
        self.pages = a["page_table"].shape[1]
        _, _, self.hm, self.md, _ = a["state_C"].shape
        self.aw = self.ha * self.vd
        self.mw = self.hm * self.md
        self.ff = a["w_up"].shape[2]
        self.pw = a["w_in"].shape[2]
        self.tp = self.seq + N_META
        self.tsmp = self.nb * self.ns
        self.t = self.tp + self.tsmp
        self.kc = self.dm // P
        self.tt = 112
        self.nt = self.t // self.tt
        self.half = self.t // 2
        assert self.nt * self.tt == self.t and self.kc * P == self.dm and self.half <= 512


class Flow:

    RAW = 4
    SPLIT = 2

    def __init__(self, nc, ctx, d, tag, sems):
        sb = lambda n, s, t: ctx.enter_context(nc.sbuf_tensor(f"{tag}_{n}", s, t))
        self.raw = sb("raw", [P, self.RAW, 16 * P], F32)
        self.hi = sb("hi", [P, self.SPLIT, 16 * P], F32R)
        self.lo = sb("lo", [P, self.SPLIT, 16 * P], F32R)
        self.landed = [sems(f"{tag}_landed{i}") for i in range(self.RAW)]
        self.hi_made = sems(f"{tag}_hi_made")
        self.lo_made = sems(f"{tag}_lo_made")
        self.used = sems(f"{tag}_used")


def exact_passes(nc, out, whi, wlo, xhi, xlo, first, last):
    nc.tensor.matmul(out, wlo, xhi, start=first, stop=False)
    nc.tensor.matmul(out, whi, xlo, start=False, stop=False)
    return nc.tensor.matmul(out, whi, xhi, start=False, stop=last)


@contextmanager
def stage(nc):
    with ExitStack() as ctx:
        made = []

        def sems(name):
            sem = ctx.enter_context(nc.semaphore(name))
            made.append(sem)
            return sem

        yield sems
        with nc.Block() as block:
            @block.sync
            def _(sp):
                for sem in made:
                    sp.sem_clear(sem)


class Consts:

    def __init__(self, nc, ctx, d):
        sb = lambda n, s, t=F32: ctx.enter_context(nc.sbuf_tensor(n, s, t))
        self.ident = sb("ident", [P, P])
        self.ones = sb("ones", [P, P])
        self.slopes = sb("slopes", [P, d.ha])
        self.neg_lam = sb("neg_lam", [P, 1])


def setup(nc, d, a, sems, c):
    with ExitStack() as ctx:
        sb = lambda n, s, t=F32: ctx.enter_context(nc.sbuf_tensor(n, s, t))
        lqk = sb("lqk", [1, 4, d.hd])
        prod = sb("lqk_prod", [1, 2, d.hd])
        dots = sb("lqk_dots", [1, 2])
        exps = sb("lqk_exps", [1, 2])
        lam = sb("lam", [1, 1])
        spread = ctx.enter_context(nc.psum_tensor("lam_spread", [P, 512], F32))
        filled, made, lqk_in = sems("consts_filled"), sems("consts_made"), sems("lqk_in")
        dotted, raised, lam_made, lam_spread, lam_done = (sems(n) for n in (
            "lam_dotted", "lam_raised", "lam_made", "lam_spread", "lam_done"))
        block = ctx.enter_context(nc.Block())

        @block.gpsimd
        def _(pool):
            nc.gpsimd.memset(c.ident[:, :], 0.0).then_inc(filled, 1)
            pool.wait_ge(filled, 1)
            nc.gpsimd.affine_select(out=c.ident[:, :], in_=c.ident[:, :], compare_op=ALU.not_equal, fill=1.0,
                                    base=0, pattern=[[-1, P]], channel_multiplier=1).then_inc(made, 1)
            for h in range(d.ha):
                nc.gpsimd.memset(c.slopes[:, h:h + 1], 2.0 ** (-8.0 * (h + 1) / d.ha)).then_inc(made, 1)
                pool.wait_ge(made, 2 + h)

        @block.sync
        def _(sp):
            sp.dma_start(lqk[:, :, :], a["lambda_qk"]).then_inc(lqk_in, 16)

        @block.vector
        def _(dve):
            nc.vector.memset(c.ones[:, :], 1.0).then_inc(dotted, 1)
            dve.wait_ge(lqk_in, 16)
            pairs = lqk[:, :, :].rearrange("o (a b) e -> o a b e", b=2)
            nc.vector.tensor_tensor(prod[:, :, :], pairs[:, :, 0, :], pairs[:, :, 1, :], ALU.mult).then_inc(dotted, 1)
            dve.wait_ge(dotted, 2)
            nc.vector.tensor_reduce(dots[:, :], prod[:, :, :], AX, ALU.add).then_inc(dotted, 1)
            dve.wait_ge(raised, 1)
            nc.vector.tensor_scalar(lam[:, :], exps[:, 0:1], exps[:, 1:2], LAM_INIT, ALU.subtract,
                                    ALU.add).then_inc(lam_made, 1)
            dve.wait_ge(lam_spread, 1)
            nc.vector.tensor_scalar(c.neg_lam[:, :], spread[:, 0:1], -1.0, None, ALU.mult).then_inc(lam_done, 1)
            dve.wait_ge(lam_done, 1)

        @block.scalar
        def _(act):
            act.wait_ge(dotted, 3)
            nc.scalar.activation(exps[:, :], dots[:, :], ACT.Exp).then_inc(raised, 1)

        @block.tensor
        def _(pe):
            pe.wait_ge(lam_made, 1)
            nc.tensor.matmul(spread[:, 0:1], c.ones[0:1, :], lam[:, :], start=True, stop=True).then_inc(lam_spread, 1)


class NormBuffers:

    def __init__(self, nc, ctx, d, sems, tag, sq, mean):
        sb = lambda n, s, t=F32: ctx.enter_context(nc.sbuf_tensor(f"{tag}_{n}", s, t))
        self.sq, self.mean = sq, mean
        self.over = sb("over_width", [P, P])
        self.root = sb("root", [P, d.t])
        self.rstd = sb("rstd", [P, d.t])
        self.xn = sb("xn", [P, 2, d.t])
        self.ready = sems(f"{tag}_over_ready")
        self.squared = sems(f"{tag}_squared")
        self.summed = sems(f"{tag}_summed")
        self.meaned = sems(f"{tag}_meaned")
        self.rooted = sems(f"{tag}_rooted")
        self.inverted = sems(f"{tag}_inverted")
        self.scaled = sems(f"{tag}_scaled")
        self.hi_made = sems(f"{tag}_xhi_made")
        self.lo_made = sems(f"{tag}_xlo_made")


def norm_mean(nc, pe, d, n, k):
    if k == 0:
        pe.wait_ge(n.ready, 1)
    pe.wait_ge(n.squared, k + 1)
    for h in range(2):
        mm = nc.tensor.matmul(n.mean[h][:, 0:d.half], n.over[:, :],
                              n.sq[:, k % 2, h * d.half:(h + 1) * d.half],
                              start=(k == 0), stop=(k == d.kc - 1))
    mm.then_inc(n.summed, 1)


def norm_scalar(nc, act, d, n, xhi, between=lambda: None):
    act.wait_ge(n.meaned, 2)
    nc.scalar.activation(n.root[:, :], n.root[:, :], ACT.Sqrt).then_inc(n.rooted, 1)
    between()
    for k in range(d.kc):
        act.wait_ge(n.scaled, k + 1)
        nc.scalar.activation(xhi[:, k, :], n.xn[:, k % 2, :], ACT.Copy).then_inc(n.hi_made, 1)


def norm_square(nc, dve, n, xt, k):
    if k == 0:
        nc.vector.memset(n.over[:, :], 1.0 / (xt.shape[1] * P)).then_inc(n.ready, 1)
    if k >= 2:
        dve.wait_ge(n.summed, k - 1)
    nc.vector.tensor_tensor(n.sq[:, k % 2, :], xt[:, k, :], xt[:, k, :], ALU.mult).then_inc(n.squared, 1)


def norm_scale(nc, dve, d, n, xt, gain, xhi, xlo, between=lambda: None):
    dve.wait_ge(n.summed, d.kc)
    for h in range(2):
        nc.vector.tensor_scalar(n.root[:, h * d.half:(h + 1) * d.half], n.mean[h][:, 0:d.half],
                                EPS, None, ALU.add).then_inc(n.meaned, 1)
    dve.wait_ge(n.rooted, 1)
    nc.vector.reciprocal(n.rstd[:, :], n.root[:, :]).then_inc(n.inverted, 1)
    between()
    dve.wait_ge(n.inverted, 1)
    for k in range(d.kc):
        if k >= 2:
            dve.wait_ge(n.lo_made, k - 1)
        nc.vector.scalar_tensor_tensor(n.xn[:, k % 2, :], xt[:, k, :], gain[:, k:k + 1], n.rstd[:, :],
                                       ALU.mult, ALU.mult).then_inc(n.scaled, 1)
        if k >= 1:
            norm_trailing(nc, dve, n, xhi, xlo, k - 1)
    norm_trailing(nc, dve, n, xhi, xlo, d.kc - 1)


def norm_trailing(nc, dve, n, xhi, xlo, k):
    dve.wait_ge(n.hi_made, k + 1)
    nc.vector.tensor_tensor(xlo[:, k, :], n.xn[:, k % 2, :], xhi[:, k, :].bitcast(F32),
                            ALU.subtract).then_inc(n.lo_made, 1)


def embed_and_project(nc, d, a, sems, ident, xhi, xlo, xt_dram, z_dram):
    n_tiles = (d.pw - 2 * d.hm) // P
    ng = 2 * d.hm
    GROUP = Flow.RAW
    with ExitStack() as ctx:
        sb = lambda n, s, t=F32: ctx.enter_context(nc.sbuf_tensor(n, s, t))
        flow = Flow(nc, ctx, d, "win", sems)
        zc = sb("z_out", [P, GROUP, d.t])
        gate_raw, gate_hi, gate_lo = sb("gate_raw", [P, d.kc, ng]), sb("gate_hi", [P, d.kc, ng], F32R), \
            sb("gate_lo", [P, d.kc, ng], F32R)
        acc = [[ctx.enter_context(nc.psum_tensor(f"z_acc{i}{h}", [P, 512], F32)) for h in range(2)]
               for i in range(2)]
        xrow = lambda t: flow.raw[0:d.tt, t, :] if t < GROUP else \
            zc[0:d.tt, :, :].rearrange("p j t -> p (j t)")[:, 0:d.dm]
        xt = sb("xt", [P, d.kc, d.t])
        gain = sb("norm_mix_cols", [P, d.kc])
        norm = NormBuffers(nc, ctx, d, sems, "mix", sb("mix_sq", [P, 2, d.t]), acc[1])
        turned = [ctx.enter_context(nc.psum_tensor(f"x_turned{i}", [P, 2, 512], F32)) for i in range(2)]
        rows_in, gain_in = sems("x_rows_in"), sems("norm_mix_in")
        turned_ready, xt_ready, xt_tail, xt_stored = (sems(n) for n in (
            "x_turned_ready", "xt_ready", "xt_tail", "xt_stored"))
        split = 4 * d.tt
        n_last = d.seq - split + N_META
        assert d.nt == GROUP + 1
        copied = sems("z_copied")
        stored = [sems(f"z_stored{i}") for i in range(GROUP)]
        gate_in = sems("gate_in")
        w = a["w_in"][0].rearrange("(k p) n -> p k n", p=P)
        raw = [flow.raw[:, j, :].rearrange("p (k n) -> p k n", k=d.kc) for j in range(GROUP)]
        hi = [flow.hi[:, j, :].rearrange("p (k n) -> p k n", k=d.kc) for j in range(2)]
        lo = [flow.lo[:, j, :].rearrange("p (k n) -> p k n", k=d.kc) for j in range(2)]
        z_rows = z_dram[0:n_tiles * P, :].rearrange("(c p) t -> c p t", p=P)
        block = ctx.enter_context(nc.Block())

        @block.sync
        def _(sp):
            x = a["x_prompt"][0]
            head = d.tt - N_META
            sp.dma_start(xrow(0)[0:N_META, :], a["meta_tokens"]).then_inc(rows_in, 16)
            sp.dma_start(xrow(0)[N_META:d.tt, :], x[0:head, :]).then_inc(rows_in, 16)
            for t in range(1, d.nt - 1):
                r0 = head + (t - 1) * d.tt
                sp.dma_start(xrow(t), x[r0:r0 + d.tt, :]).then_inc(rows_in, 16)
            sp.dma_start(xrow(d.nt - 1)[0:n_last, :], x[d.seq - n_last:d.seq, :]).then_inc(rows_in, 16)
            sp.dma_start(xrow(d.nt - 1)[n_last:d.tt, :], a["x_sample"].rearrange("b s m -> (b s) m")).then_inc(rows_in, 16)
            sp.dma_start(gain[:, :], a["norm_mix"][0].rearrange("(k p) -> p k", p=P),
                         allow_slow_non_contiguous=True).then_inc(gain_in, 16)
            sp.wait_ge(turned_ready, d.kc)
            for j in range(GROUP):
                sp.dma_start(raw[j], w[:, :, j * P:(j + 1) * P]).then_inc(flow.landed[j], 16)
            sp.wait_ge(xt_ready, d.kc)
            sp.wait_ge(xt_tail, d.kc)
            sp.dma_start(xt_dram.rearrange("(k p) t -> p k t", p=P), xt[:, :, :]).then_inc(xt_stored, 16)
            sp.dma_start(gate_raw[:, :, :], w[:, :, n_tiles * P:d.pw]).then_inc(gate_in, 16)
            with sp.Fori(0, n_tiles // GROUP - 1) as g:
                i = g * GROUP
                for j in range(GROUP):
                    sp.wait_ge(flow.lo_made, i + j + 1)
                    sp.dma_start(raw[j], w[:, :, bass.ds((i + GROUP + j) * P, P)]).then_inc(flow.landed[j], 16)
                    sp.wait_ge(copied, 2 * (i + j) + 2)
                    sp.dma_start(z_rows[i + j], zc[:, j, :]).then_inc(stored[j], 16)
            for j in range(GROUP):
                n = n_tiles - GROUP + j
                sp.wait_ge(copied, 2 * n + 2)
                sp.dma_start(z_rows[n], zc[:, j, :]).then_inc(stored[j], 16)
            sp.wait_ge(copied, 2 * n_tiles + 2)
            sp.dma_start(z_dram[n_tiles * P:n_tiles * P + ng, :], zc[0:ng, 0, :]).then_inc(stored[0], 16)
            sp.wait_ge(xt_stored, 16)
            sp.wait_ge(stored[0], 16 * (n_tiles // GROUP + 1))
            for j in range(1, GROUP):
                sp.wait_ge(stored[j], 16 * (n_tiles // GROUP))

        def act_group(act, i, first):
            for j in range(2 if first else 0, GROUP):
                act.wait_ge(flow.landed[j], i * (16 // GROUP) + 16)
                act.wait_ge(flow.used, i + j - 1)
                leading(j)

        def leading(j):
            nc.scalar.activation(flow.hi[:, j % 2, :], flow.raw[:, j, :], ACT.Copy).then_inc(flow.hi_made, 1)

        @block.scalar
        def _(act):
            for k in range(d.kc):
                act.wait_ge(turned_ready, k + 1)
                nc.scalar.activation(xt[:, k, split:d.t], turned[k % 2][:, 1, 0:d.t - split], ACT.Copy).then_inc(xt_tail, 1)

            def first_tiles():
                for j in range(2):
                    act.wait_ge(flow.landed[j], 16)
                    leading(j)
            norm_scalar(nc, act, d, norm, xhi, first_tiles)
            act_group(act, 0, True)
            with act.Fori(1, n_tiles // GROUP) as g:
                act_group(act, g * GROUP, False)
            act.wait_ge(gate_in, 16)
            nc.scalar.activation(gate_hi[:, :, :], gate_raw[:, :, :], ACT.Copy).then_inc(flow.hi_made, 1)

        def dve_copy_out(dve, n, j, rows=P):
            dve.wait_ge(flow.used, n + 1)
            for h in range(2):
                nc.vector.tensor_copy(zc[0:rows, j, h * d.half:(h + 1) * d.half],
                                      acc[j % 2][h][0:rows, 0:d.half]).then_inc(copied, 1)

        def trailing(dve, n, j):
            dve.wait_ge(flow.hi_made, n + 1)
            nc.vector.tensor_tensor(flow.lo[:, j % 2, :], flow.raw[:, j, :],
                                    flow.hi[:, j % 2, :].bitcast(F32), ALU.subtract).then_inc(flow.lo_made, 1)

        def dve_group(dve, i, nth):
            for j in range(GROUP):
                if nth or j >= 2:
                    trailing(dve, i + j, j)
                if nth + (j > 0) >= 2:
                    dve.wait_ge(stored[(j - 1) % GROUP], i * (16 // GROUP) - (16 if j == 0 else 0))
                if nth + (j > 0) >= 1:
                    dve_copy_out(dve, i + j - 1, (j - 1) % GROUP)

        def square(dve, k):
            dve.wait_ge(xt_ready, k + 1)
            dve.wait_ge(xt_tail, k + 1)
            norm_square(nc, dve, norm, xt, k)

        @block.vector
        def _(dve):
            for k in range(d.kc):
                dve.wait_ge(turned_ready, k + 1)
                nc.vector.tensor_copy(xt[:, k, 0:split], turned[k % 2][:, 0, 0:split]).then_inc(xt_ready, 1)
                if k >= 1:
                    square(dve, k - 1)
            square(dve, d.kc - 1)
            dve.wait_ge(gain_in, 16)
            norm_scale(nc, dve, d, norm, xt, gain, xhi, xlo, lambda: [trailing(dve, j, j) for j in range(2)])
            dve_group(dve, 0, 0)
            dve_group(dve, GROUP, 1)
            with dve.Fori(2, n_tiles // GROUP) as g:
                dve_group(dve, g * GROUP, 2)
            dve.wait_ge(flow.hi_made, n_tiles + 1)
            nc.vector.tensor_tensor(gate_lo[:, :, :], gate_raw[:, :, :], gate_hi[:, :, :].bitcast(F32),
                                    ALU.subtract).then_inc(flow.lo_made, 1)
            dve.wait_ge(stored[GROUP - 1], 16 * (n_tiles // GROUP - 1))
            dve_copy_out(dve, n_tiles - 1, GROUP - 1)
            dve.wait_ge(stored[0], 16 * (n_tiles // GROUP))
            dve_copy_out(dve, n_tiles, 0, ng)

        def pe_tile(pe, n, j, whi, wlo, rows=P, first=False):
            pe.wait_ge(flow.lo_made, n + 1)
            if not first:
                pe.wait_ge(copied, 2 * n - 2)
            for h in range(2):
                cols = slice(h * d.half, (h + 1) * d.half)
                for k in range(d.kc):
                    if first and j == 0 and h == 0:
                        pe.wait_ge(norm.lo_made, k + 1)
                    mm = exact_passes(nc, acc[j % 2][h][0:rows, 0:d.half], whi[:, k, :], wlo[:, k, :],
                                      xhi[:, k, cols], xlo[:, k, cols], k == 0, k == d.kc - 1)
            mm.then_inc(flow.used, 1)

        @block.tensor
        def _(pe):
            pe.wait_ge(rows_in, 16 * (d.nt + 2))
            for k in range(d.kc):
                if k >= 2:
                    pe.wait_ge(xt_ready, k - 1)
                    pe.wait_ge(xt_tail, k - 1)
                for t in range(d.nt):
                    out = turned[k % 2][:, t // 4, (t % 4) * d.tt:(t % 4 + 1) * d.tt]
                    mm = nc.tensor.transpose(out, xrow(t)[:, k * P:(k + 1) * P], ident[0:d.tt, 0:d.tt])
                mm.then_inc(turned_ready, 1)
                if k >= 2:
                    norm_mean(nc, pe, d, norm, k - 2)
            for k in range(d.kc - 2, d.kc):
                norm_mean(nc, pe, d, norm, k)
            for j in range(2):
                pe_tile(pe, j, j, hi[j], lo[j], first=True)
            with pe.Fori(1, n_tiles // 2) as g:
                for j in range(2):
                    pe_tile(pe, g * 2 + j, j, hi[j], lo[j])
            pe_tile(pe, n_tiles, 0, gate_hi[:, :, :], gate_lo[:, :, :], ng)


def heads_prepare(nc, d, a, sems, c, z_dram, zn_dram, k_rows, v_rows, ks_rows, vs_rows):
    T, TT, TP, HA, HD = d.t, d.tt, d.tp, d.ha, d.hd
    LAST = TP - 4 * TT
    N = 2 * HA
    R = 2 * N
    SQ, PIECE = 4, HA // 2
    place = lambda n: HA + n if n < HA else n - HA
    with ExitStack() as ctx:
        sb = lambda n, s, t=F32: ctx.enter_context(nc.sbuf_tensor(n, s, t))
        ps = lambda n, s: ctx.enter_context(nc.psum_tensor(n, s, F32))
        z = sb("zqkv", [P, 3 * HA, T])
        sq = [sb(f"qk_sq{s}", [P, T]) for s in range(SQ)]
        root, inv = sb("qk_root", [R, T]), sb("qk_inv", [P, T])
        gather = sb("qk_gather", [P, 2 * R - 2])
        scatter = sb("qk_scatter", [P, N, P])
        gains = sb("qk_gains", [P, 2])
        rows = [sb(f"kv_rows{w}", [TT, 5, d.aw]) for w in range(2)]
        srow = [sb(f"kv_srow{w}", [d.tsmp, d.aw]) for w in range(2)]
        spread = [ps(f"qk_spread{i}", [P, 2, 512]) for i in range(2)]
        mean = spread[0]
        turned = [ps(f"kv_turned{i}", [P, 2, 512]) for i in range(2)]
        gains_in, consts = sems("qk_gains_in"), sems("qk_consts")
        landed = [sems(f"zqkv_in{w}{i}") for w in range(3) for i in range(2)]
        squared, meaned, rooting, rooted, inverted, spread_ready, normed, turned_ready, rows_a, rows_b, stored = (
            sems(f"qk_{n}") for n in (
                "squared", "meaned", "rooting", "rooted", "inverted", "spread_ready", "normed", "turned_ready",
                "rows_a", "rows_b", "stored"))
        zh = z_dram[0:3 * d.aw, :].rearrange("(h p) t -> p h t", p=P)
        znh = zn_dram.rearrange("(h p) t -> p h t", p=P)
        two = lambda x: x.rearrange("p (b t) -> p b t", b=2)
        block = ctx.enter_context(nc.Block())

        def store_rows(sp, w, dst, smp):
            sp.dma_start(dst[0:4 * TT, :].rearrange("(t p) e -> p t e", p=TT), rows[w][:, 0:4, :]).then_inc(stored, 16)
            sp.dma_start(dst[4 * TT:TP, :], rows[w][0:LAST, 4, :]).then_inc(stored, 16)
            sp.dma_start(smp, srow[w][:, :]).then_inc(stored, 16)

        @block.sync
        def _(sp):
            for w in (1, 0, 2):
                for i in range(2):
                    at = slice(w * HA + i * PIECE, w * HA + (i + 1) * PIECE)
                    sp.dma_start(z[:, at, :], zh[:, at, :]).then_inc(landed[2 * w + i], 16)
            for i, name in enumerate(("q_norm", "k_norm")):
                for m in range(2):
                    sp.dma_start(gains[m * HD:(m + 1) * HD, i:i + 1], a[name].rearrange("o e -> e o"),
                                 allow_slow_non_contiguous=True).then_inc(gains_in, 16)
            sp.wait_ge(rows_a, HA)
            sp.wait_ge(rows_b, HA)
            store_rows(sp, 1, v_rows, vs_rows)
            for i in range(N // PIECE):
                sp.wait_ge(normed, (i + 1) * PIECE)
                at = slice(place(i * PIECE), place(i * PIECE) + PIECE)
                sp.dma_start(znh[:, at, :], z[:, at, :]).then_inc(stored, 16)
                if i == 2:
                    sp.wait_ge(rows_a, N)
                    sp.wait_ge(rows_b, N)
                    store_rows(sp, 0, k_rows, ks_rows)
            sp.wait_ge(stored, 16 * (6 + N // PIECE))

        @block.gpsimd
        def _(pool):
            G = nc.gpsimd
            G.memset(gather[:, :], 0.0).then_inc(consts, 1)
            pool.wait_ge(consts, 1)
            for m in range(2):
                G.memset(gather[m * HD:(m + 1) * HD, R - 2 + m:R - 1 + m], 1.0 / HD).then_inc(consts, 1)
                pool.wait_ge(consts, 2 + m)
            G.memset(scatter[:, :, :], 1.0).then_inc(consts, 1)
            G.memset(inv[:, :], 0.0).then_inc(consts, 1)
            pool.wait_ge(consts, 5)
            s4 = scatter[:, :, :].rearrange("r n (m e) -> r n m e", m=2)
            G.affine_select(out=s4, in_=s4, compare_op=ALU.is_equal, fill=0.0, base=0,
                            pattern=[[-2, N], [-1, 2], [0, HD]], channel_multiplier=1).then_inc(consts, 1)

        def turn_order(r):
            return 2 * HA + r if r < HA else r

        @block.tensor
        def _(pe):
            def turn(r):
                if r >= 2:
                    pe.wait_ge(rows_a, r - 1)
                    pe.wait_ge(rows_b, r - 1)
                x, out = z[:, turn_order(r), :], turned[r % 2]
                for t in range(4):
                    nc.tensor.transpose(out[0:TT, 0, t * P:(t + 1) * P], x[:, t * TT:(t + 1) * TT], c.ident[:, :])
                nc.tensor.transpose(out[0:LAST, 1, 0:P], x[:, 4 * TT:TP], c.ident[:, :])
                nc.tensor.transpose(out[0:d.tsmp, 1, P:2 * P], x[:, TP:T], c.ident[:, :]).then_inc(turned_ready, 1)

            pe.wait_ge(consts, 6)
            for n in range(N):
                pe.wait_ge(squared, n + 1)
                for h in range(2):
                    mm = nc.tensor.matmul(mean[0:R, h, 0:d.half], gather[:, R - 2 - 2 * n:2 * R - 2 - 2 * n],
                                          sq[n % SQ][:, h * d.half:(h + 1) * d.half], start=(n == 0),
                                          stop=(n == N - 1))
                mm.then_inc(meaned, 1)
                if n >= HA:
                    if (n - HA) % PIECE == 0:
                        pe.wait_ge(landed[4 + (n - HA) // PIECE], 16)
                    turn(n - HA)
            pe.wait_ge(inverted, 1)
            for n in range(N):
                if n >= 2:
                    pe.wait_ge(normed, n - 1)
                for h in range(2):
                    mm = nc.tensor.matmul(spread[n % 2][:, h, 0:d.half], scatter[:, n, :],
                                          inv[:, h * d.half:(h + 1) * d.half], start=True, stop=True)
                mm.then_inc(spread_ready, 1)
                if 1 <= n <= HA:
                    pe.wait_ge(normed, n)
                    turn(HA + n - 1)

        @block.vector
        def _(dve):
            V = nc.vector

            def edges(r):
                w, at = (1, slice(r * P, (r + 1) * P)) if r < HA else (0, slice((r - HA) * P, (r - HA + 1) * P))
                dve.wait_ge(turned_ready, r + 1)
                V.tensor_copy(rows[w][0:LAST, 4, at], turned[r % 2][0:LAST, 1, 0:P])
                V.tensor_copy(srow[w][:, at], turned[r % 2][0:d.tsmp, 1, P:2 * P]).then_inc(rows_b, 1)

            for n in range(N):
                if n % PIECE == 0:
                    dve.wait_ge(landed[place(n) // PIECE], 16)
                if n >= SQ:
                    dve.wait_ge(meaned, n - SQ + 1)
                x = z[:, place(n), :]
                V.tensor_tensor(sq[n % SQ][:, :], x, x, ALU.mult).then_inc(squared, 1)
                if n > HA:
                    edges(n - HA - 1)
            dve.wait_ge(meaned, N)
            V.tensor_scalar(two(root[:, :]), mean[0:R, :, 0:d.half], EPS, None, ALU.add).then_inc(rooting, 1)
            edges(HA - 1)
            dve.wait_ge(rooted, 1)
            dve.wait_ge(consts, 6)
            V.reciprocal(inv[0:R, :], root[:, :]).then_inc(inverted, 1)
            dve.wait_ge(gains_in, 64)
            for n in range(N):
                dve.wait_ge(spread_ready, n + 1)
                x, w = z[:, place(n), :], 1 if n < HA else 0
                V.scalar_tensor_tensor(two(x), two(x), gains[:, w:w + 1], spread[n % 2][:, :, 0:d.half],
                                       ALU.mult, ALU.mult).then_inc(normed, 1)
                if 2 <= n <= HA + 1:
                    edges(HA + n - 2)

        @block.scalar
        def _(act):
            def main_rows(r):
                w, at = (1, slice(r * P, (r + 1) * P)) if r < HA else (0, slice((r - HA) * P, (r - HA + 1) * P))
                act.wait_ge(turned_ready, r + 1)
                nc.scalar.activation(rows[w][:, 0:4, at], turned[r % 2][0:TT, 0, :].rearrange(
                    "p (t e) -> p t e", e=P), ACT.Copy).then_inc(rows_a, 1)

            for r in range(HA - 1):
                main_rows(r)
            act.wait_ge(rooting, 1)
            nc.scalar.activation(root[:, :], root[:, :], ACT.Sqrt).then_inc(rooted, 1)
            for r in range(HA - 1, N):
                main_rows(r)


def prompt_attention(nc, d, a, sems, c, zn_dram, v_rows, mix):
    TT, NT, TP = d.tt, d.nt, d.tp
    EDGE = 3 * TT
    WIDE = NT * TT
    with ExitStack() as ctx:
        sb = lambda n, s, t=F32: ctx.enter_context(nc.sbuf_tensor(n, s, t))
        ps = lambda n, s: ctx.enter_context(nc.psum_tensor(n, s, F32))
        q = [sb(f"at_q{s}", [P, 2, TP]) for s in range(2)]
        k = [sb(f"at_k{s}", [P, TP]) for s in range(2)]
        v = [sb(f"at_v{s}", [TT, NT, P]) for s in range(2)]
        dist = sb("at_dist", [TT, WIDE])
        mask = sb("at_mask", [TT, WIDE])
        bias = [sb(f"at_bias{s}", [TT, WIDE]) for s in range(2)]
        sc = [[sb(f"at_sc{t}{m}", [TT, (t + 1) * TT]) for m in range(2)] for t in range(NT)]
        top = [sb(f"at_top{u}", [TT, 2]) for u in range(2)]
        low = [sb(f"at_low{u}", [TT, 2]) for u in range(2)]
        den = [sb(f"at_den{u}", [TT, 2]) for u in range(2)]
        inv = [sb(f"at_inv{u}", [TT, 2]) for u in range(2)]
        at = [sb(f"at_t{u}", [TT, NT, TT]) for u in range(2)]
        scores = [ps(f"at_scores{m}", [P, 2, 512]) for m in range(2)]
        turn = ps("at_turn", [P, 2, 512])
        outp = [ps(f"at_out{u}", [P, 512]) for u in range(2)]
        landed, zeroed = [sems(f"at_landed{s}") for s in range(2)], sems("at_zeroed")
        dist_made, bias_made, scored, biased, topped, lowered, raised, inverted, scaled, mixed, turned, turned_out, \
            valued, placed = (sems(n) for n in (
                "at_dist_made", "at_bias_made", "at_scored", "at_biased", "at_topped", "at_lowered", "at_raised",
                "at_inverted", "at_scaled", "at_mixed", "at_turned", "at_turned_out", "at_valued", "at_placed"))
        znh = zn_dram.rearrange("(w h p) t -> h p w t", w=2, p=P)
        vh = v_rows[0:4 * TT, :].rearrange("(t p) (h e) -> h p t e", p=TT, e=P)
        vlast = v_rows[4 * TT:TP, :].rearrange("p (h e) -> h p e", e=P)
        LAST = TP - 4 * TT
        nq = [TT] * (NT - 1) + [LAST]
        keys = [min((t + 1) * TT, TP) for t in range(NT)]
        block = ctx.enter_context(nc.Block())

        def load(sp, h, s):
            for m in range(2):
                half = slice(m * d.hd, (m + 1) * d.hd)
                sp.dma_start(q[s][half, m, :], znh[h][half, 0, 0:TP]).then_inc(landed[s], 16)
            sp.dma_start(k[s][:, :], znh[h][:, 1, 0:TP]).then_inc(landed[s], 16)
            sp.dma_start(v[s][:, 0:4, :], vh[h]).then_inc(landed[s], 16)
            sp.dma_start(v[s][0:LAST, 4, :], vlast[h]).then_inc(landed[s], 16)

        @block.sync
        def _(sp):
            sp.wait_ge(zeroed, 2)
            for s in range(2):
                load(sp, s, s)
            with sp.Fori(0, d.ha // 2 - 1) as g:
                for s in range(2):
                    sp.wait_ge(valued, g * (2 * NT) + (s + 1) * NT)
                    load(sp, g * 2 + (s + 2), s)

        @block.gpsimd
        def _(pool):
            nc.gpsimd.iota(dist[:, :], pattern=[[1, WIDE]], base=-4 * TT, channel_multiplier=-1,
                           allow_small_or_imprecise_dtypes=True).then_inc(dist_made, 1)
            pool.wait_ge(dist_made, 1)
            nc.gpsimd.memset(mask[:, :], 0.0).then_inc(dist_made, 1)
            pool.wait_ge(dist_made, 2)
            nc.gpsimd.affine_select(out=mask[:, :], in_=mask[:, :], compare_op=ALU.is_ge, fill=FILL,
                                    base=4 * TT, pattern=[[-1, WIDE]], channel_multiplier=1).then_inc(dist_made, 1)

        def pe_scores(pe, g, s, t):
            u, n = (s * NT + t) % 2, g * (2 * NT) + (s * NT + t)
            if t == 0:
                pe.wait_ge(landed[s], g * 80 + 80)
            for m in range(2):
                if not (isinstance(n, int) and n == 0):
                    pe.wait_ge(biased, n * 2 - 1 + m)
                lhs = q[s][:, m, t * TT:t * TT + nq[t]]
                first = min(EDGE, keys[t])
                mm = nc.tensor.matmul(scores[m][0:nq[t], 0, 0:first], lhs, k[s][:, 0:first],
                                      start=True, stop=True)
                if keys[t] > EDGE:
                    mm = nc.tensor.matmul(scores[m][0:nq[t], 1, 0:keys[t] - EDGE], lhs,
                                          k[s][:, EDGE:keys[t]], start=True, stop=True)
                mm.then_inc(scored, 1)

        def pe_turn(pe, g, s, t):
            n = g * (2 * NT) + (s * NT + t)
            pe.wait_ge(mixed, n + 1)
            if not (isinstance(n, int) and n == 0):
                pe.wait_ge(turned_out, n * 2)
            for j in range(t + 1):
                mm = nc.tensor.transpose(turn[0:nq[j], j // 4, (j % 4) * TT:(j % 4) * TT + nq[t]],
                                         sc[t][0][0:nq[t], j * TT:j * TT + nq[j]], c.ident[0:nq[t], 0:nq[t]])
            mm.then_inc(turned, 1)

        def pe_values(pe, g, s, t):
            u, n = (s * NT + t) % 2, g * (2 * NT) + (s * NT + t)
            pe.wait_ge(turned_out, n * 2 + 2)
            if not (isinstance(n, int) and n < 2):
                pe.wait_ge(placed, n - 1)
            for j in range(t + 1):
                mm = nc.tensor.matmul(outp[u][:, 0:nq[t]], v[s][0:nq[j], j, :], at[u][0:nq[j], j, 0:nq[t]],
                                      start=(j == 0), stop=(j == t))
            mm.then_inc(valued, 1)

        def pipeline(eng, *steps):
            def back(g, s, t, lag):
                i = s * NT + t - lag
                return (g, i // NT, i % NT) if i >= 0 else (g - 1, (i + 2 * NT) // NT, i % NT)

            def pair(g, first):
                for s in range(2):
                    for t in range(NT):
                        for lag, run in steps:
                            if not (first and s * NT + t < lag):
                                run(eng, *back(g, s, t, lag))
            pair(0, True)
            with eng.Fori(1, d.ha // 2) as g:
                pair(g, False)
            for t in range(max(lag for lag, _ in steps)):
                for lag, run in steps:
                    if t < lag:
                        run(eng, *back(d.ha // 2, 0, t, lag))

        @block.tensor
        def _(pe):
            pipeline(pe, (0, pe_scores), (2, pe_turn), (3, pe_values))

        def dve_scores(dve, g, s, t):
            u, n = (s * NT + t) % 2, g * (2 * NT) + (s * NT + t)
            if t == 0:
                nc.vector.scalar_tensor_tensor(bias[s][:, :], dist[:, :], c.slopes[0:TT, bass.ds(g * 2 + s, 1)],
                                               mask[:, :], ALU.mult, ALU.add).then_inc(bias_made, 1)
                dve.wait_ge(bias_made, g * 2 + s + 1)
            if not (isinstance(n, int) and n < NT):
                dve.wait_ge(turned, n - (NT - 1))
            b0 = (4 - t) * TT
            for m in range(2):
                dve.wait_ge(scored, n * 2 + m + 1)
                first = min(EDGE, keys[t])
                ins = nc.vector.scalar_tensor_tensor(sc[t][m][0:nq[t], 0:first], scores[m][0:nq[t], 0, 0:first],
                                                     d.hd ** -0.5, bias[s][0:nq[t], b0:b0 + first],
                                                     ALU.mult, ALU.add)
                if keys[t] > EDGE:
                    ins = nc.vector.scalar_tensor_tensor(
                        sc[t][m][0:nq[t], EDGE:keys[t]], scores[m][0:nq[t], 1, 0:keys[t] - EDGE], d.hd ** -0.5,
                        bias[s][0:nq[t], b0 + EDGE:b0 + keys[t]], ALU.mult, ALU.add)
                ins.then_inc(biased, 1)
                dve.wait_ge(biased, n * 2 + m + 1)
                nc.vector.tensor_reduce(top[u][0:nq[t], m:m + 1], sc[t][m][0:nq[t], 0:keys[t]], AX,
                                        ALU.max).then_inc(topped, 1)
            dve.wait_ge(topped, n * 2 + 2)
            nc.vector.tensor_scalar(low[u][0:nq[t], :], top[u][0:nq[t], :], -1.0, None, ALU.mult).then_inc(lowered, 1)

        def dve_mix(dve, g, s, t):
            u, n = (s * NT + t) % 2, g * (2 * NT) + (s * NT + t)
            dve.wait_ge(raised, n * 2 + 2)
            nc.vector.reciprocal(inv[u][0:nq[t], :], den[u][0:nq[t], :]).then_inc(inverted, 1)
            dve.wait_ge(inverted, n + 1)
            nc.vector.tensor_scalar(sc[t][1][0:nq[t], 0:keys[t]], sc[t][1][0:nq[t], 0:keys[t]],
                                    inv[u][0:nq[t], 1:2], c.neg_lam[0:nq[t], :], ALU.mult,
                                    ALU.mult).then_inc(scaled, 1)
            dve.wait_ge(scaled, n + 1)
            nc.vector.scalar_tensor_tensor(sc[t][0][0:nq[t], 0:keys[t]], sc[t][0][0:nq[t], 0:keys[t]],
                                           inv[u][0:nq[t], 0:1], sc[t][1][0:nq[t], 0:keys[t]],
                                           ALU.mult, ALU.add).then_inc(mixed, 1)

        @block.vector
        def _(dve):
            for s in range(2):
                nc.vector.memset(q[s][:, :, :], 0.0).then_inc(zeroed, 1)
            dve.wait_ge(dist_made, 3)
            pipeline(dve, (0, dve_scores), (1, dve_mix))

        def act_exp(act, g, s, t):
            u, n = (s * NT + t) % 2, g * (2 * NT) + (s * NT + t)
            act.wait_ge(lowered, n + 1)
            for m in range(2):
                nc.scalar.activation(sc[t][m][0:nq[t], 0:keys[t]], sc[t][m][0:nq[t], 0:keys[t]], ACT.Exp,
                                     bias=low[u][0:nq[t], m:m + 1],
                                     accum_out=den[u][0:nq[t], m:m + 1]).then_inc(raised, 1)

        def act_out(act, g, s, t):
            u, n = (s * NT + t) % 2, g * (2 * NT) + (s * NT + t)
            act.wait_ge(turned, n + 1)
            if not (isinstance(n, int) and n < 2):
                act.wait_ge(valued, n - 1)
            full = min(t + 1, 4) - (1 if t < 4 and nq[t] < TT else 0)
            for j0, j1, rows in ((0, full, TT), (4, t + 1, LAST)):
                if j0 < j1:
                    nc.scalar.activation(at[u][0:rows, j0:j1, 0:nq[t]],
                                         turn[0:rows, j0 // 4, 0:(j1 - j0) * TT].rearrange(
                                             "p (j q) -> p j q", q=TT)[:, :, 0:nq[t]],
                                         ACT.Copy).then_inc(turned_out, 1 if t == 4 else 2)

        def act_place(act, g, s, t):
            u, n = (s * NT + t) % 2, g * (2 * NT) + (s * NT + t)
            act.wait_ge(valued, n + 1)
            nc.scalar.activation(mix[:, bass.ds(g * 2 + s, 1), t * TT:t * TT + nq[t]],
                                 outp[u][:, 0:nq[t]].rearrange("p (o q) -> p o q", o=1),
                                 ACT.Copy).then_inc(placed, 1)

        @block.scalar
        def _(act):
            pipeline(act, (0, act_exp), (2, act_out), (3, act_place))


G_SOURCE, G_NEGTOP, G_FLOOR, G_INTER = range(4)


def gates(nc, d, a, sems, z_dram, g_dram, m_prompt, m_sample):
    H, T, TP = d.hm, d.t, d.tp
    n_z = d.pw - 2 * H
    with ExitStack() as ctx:
        sb = lambda n, s, t=F32: ctx.enter_context(nc.sbuf_tensor(n, s, t))
        gi, gf, neg, mag, soft, lf, b, src, top, m, fl, it, ones = (sb(f"g_{n}", [H, T]) for n in (
            "i", "f", "neg", "mag", "soft", "lf", "b", "src", "top", "m", "floor", "inter", "ones"))
        m0 = sb("g_m0", [H, d.nb])
        gb = sb("g_bias", [H, 2])
        ins, step, sact, outs = sems("g_in"), sems("g_step"), sems("g_act"), sems("g_out")
        rows_ready = sems("g_rows_ready")
        smp = lambda x: x[:, TP:T].rearrange("h (b s) -> h b s", s=d.ns)
        block = ctx.enter_context(nc.Block())

        @block.sync
        def _(sp):
            sp.dma_start(gi[:, :], z_dram[n_z:n_z + H, :]).then_inc(ins, 16)
            sp.dma_start(gf[:, :], z_dram[n_z + H:n_z + 2 * H, :]).then_inc(ins, 16)
            sp.dma_start(m0[:, :], a["state_m"].rearrange("o b h -> h (o b)"),
                         allow_slow_non_contiguous=True).then_inc(ins, 16)
            sp.dma_start(gb[:, :], a["gate_bias"].rearrange("o w h -> h (o w)"),
                         allow_slow_non_contiguous=True).then_inc(ins, 16)
            sp.wait_ge(sact, 4)
            for row, x in ((G_SOURCE, src), (G_NEGTOP, neg), (G_FLOOR, fl), (G_INTER, it)):
                sp.dma_start(g_dram[row], x[:, :]).then_inc(outs, 16)
            sp.dma_start(m_prompt.rearrange("o b h -> h (o b)"), m[:, TP - 1:TP],
                         allow_slow_non_contiguous=True).then_inc(outs, 16)
            sp.dma_start(m_sample.rearrange("o b h -> h (o b)"), smp(m)[:, :, d.ns - 1],
                         allow_slow_non_contiguous=True).then_inc(outs, 16)
            sp.wait_ge(outs, 96)

        @block.vector
        def _(dve):
            n = [0]

            def done(instruction):
                instruction.then_inc(step, 1)
                n[0] += 1
                dve.wait_ge(step, n[0])

            V = nc.vector
            dve.wait_ge(ins, 64)
            done(V.memset(ones[:, :], 1.0))
            done(V.tensor_scalar(gi[:, :], gi[:, :], gb[:, 0:1], None, ALU.add))
            done(V.tensor_scalar(gf[:, :], gf[:, :], gb[:, 1:2], None, ALU.add))
            done(V.tensor_scalar(neg[:, :], gf[:, :], -1.0, None, ALU.mult))
            done(V.tensor_tensor(mag[:, :], gf[:, :], neg[:, :], ALU.max))
            dve.wait_ge(sact, 2)
            done(V.scalar_tensor_tensor(lf[:, :], gf[:, :], 0.0, soft[:, :], ALU.min, ALU.subtract))
            done(V.tensor_tensor_scan(b[:, 0:TP], ones[:, 0:TP], lf[:, 0:TP], 0.0, ALU.mult, ALU.add))
            done(V.tensor_copy(smp(b)[:, :, 0], smp(lf)[:, :, 0]))
            for j in range(1, d.ns):
                done(V.tensor_tensor(smp(b)[:, :, j], smp(b)[:, :, j - 1], smp(lf)[:, :, j], ALU.add))
            done(V.tensor_tensor(src[:, :], gi[:, :], b[:, :], ALU.subtract))
            done(V.tensor_tensor_scan(top[:, 0:TP], src[:, 0:TP], src[:, 0:TP], 0.0, ALU.max, ALU.max))
            done(V.tensor_tensor(smp(top)[:, :, 0], smp(src)[:, :, 0], m0[:, :], ALU.max))
            for j in range(1, d.ns):
                done(V.tensor_tensor(smp(top)[:, :, j], smp(top)[:, :, j - 1], smp(src)[:, :, j], ALU.max))
            done(V.tensor_tensor(m[:, :], b[:, :], top[:, :], ALU.add))
            done(V.tensor_scalar(neg[:, :], top[:, :], -1.0, None, ALU.mult))
            done(V.memset(it[:, 0:TP], 0.0))
            done(V.tensor_tensor(smp(it), m0[:, :].rearrange("h (b o) -> h b o", o=1).to_broadcast(
                [H, d.nb, d.ns]), smp(neg), ALU.add))
            dve.sem_inc(rows_ready, 1)

        @block.scalar
        def _(act):
            act.wait_ge(step, 5)
            nc.scalar.activation(mag[:, :], mag[:, :], ACT.Exp, scale=-1.0).then_inc(sact, 1)
            act.wait_ge(sact, 1)
            nc.scalar.activation(soft[:, :], mag[:, :], ACT.Ln, bias=1.0).then_inc(sact, 1)
            act.wait_ge(rows_ready, 1)
            nc.scalar.activation(fl[:, :], m[:, :], ACT.Exp, scale=-1.0).then_inc(sact, 1)
            nc.scalar.activation(it[:, :], it[:, :], ACT.Exp).then_inc(sact, 1)


def mlstm_features(nc, d, a, sems, c, z_dram, qk_dram, kt_dram, vt_dram, conv_prompt, conv_sample):
    T, TP, TT, NS, NB = d.t, d.tp, d.tt, d.ns, d.nb
    W = a["conv_w"].shape[1]
    PRE = W - 1
    SEG = PRE + TP
    U = SEG + NB * (PRE + NS)
    TAIL = U - TP
    LAST = TP - 4 * TT
    E = d.md // P
    cu, cv = 3 * d.ha, 3 * d.ha + d.hm * E
    with ExitStack() as ctx:
        sb = lambda n, s, t=F32: ctx.enter_context(nc.sbuf_tensor(n, s, t))
        ps = lambda n, s: ctx.enter_context(nc.psum_tensor(n, s, F32))
        u = [sb(f"u{s}", [P, E, U]) for s in range(d.hm)]
        conv = [sb(f"conv{s}", [P, E, U]) for s in range(2)]
        sig = [sb(f"conv_sig{s}", [P, E, U]) for s in range(2)]
        ua = [sb(f"ua{s}", [P, E, T]) for s in range(d.hm)]
        vz = [sb(f"vm{s}", [P, E, T]) for s in range(d.hm)]
        wqk = [sb(f"wqk{s}", [P, 2, E, d.md]) for s in range(d.hm)]
        qk = [sb(f"mqk{s}", [P, 2 * E, T]) for s in range(2)]
        rows = [sb(f"mrows{s}", [TT, 2, 5, d.md]) for s in range(2)]
        srow = [sb(f"msrow{s}", [d.tsmp, 2, d.md]) for s in range(2)]
        tail = [sb(f"conv_tail{s}", [TAIL, d.md]) for s in range(2)]
        srows = sb("state_conv_rows", [NB * PRE, d.mw])
        state = sb("state_conv_t", [P, d.hm * E, NB * PRE])
        cw = sb("conv_w_cols", [P, W, d.hm * E])
        cb = sb("conv_b_cols", [P, d.hm * E])
        proj = [ps(f"mproj{i}", [P, 2, 512]) for i in range(2)]
        turn = [ps(f"mturn{i}", [P, 2, 512]) for i in range(2)]
        cin, state_turned, state_out = sems("conv_in"), sems("conv_state_turned"), sems("conv_state_out")
        landed = [sems(f"mf_landed{h}") for h in range(d.hm)]
        stored = [sems(f"mf_stored{s}") for s in range(2)]
        padded, tapped, gated, active, projected, proj_out, turned, rows_a, rows_b = (sems(f"mf_{n}") for n in (
            "padded", "tapped", "gated", "active", "projected", "proj_out", "turned", "rows_a", "rows_b"))
        STORES, LOADS = 1 + 6 + 1 + NB, 5
        zc = z_dram[0:(cv + d.hm * E) * P, :].rearrange("(c e p) t -> c p e t", e=E, p=P)
        qk_out = qk_dram.rearrange("(h c p) t -> h p c t", h=d.hm, p=P)
        seg = lambda x: x.rearrange("p e (b s) -> p e b s", s=PRE + NS)
        block = ctx.enter_context(nc.Block())

        def load(sp, h):
            zu, zv = zc[h + cu // E], zc[h + cv // E]
            sp.dma_start(u[h][:, :, PRE:SEG], zu[:, :, 0:TP]).then_inc(landed[h], 16)
            sp.dma_start(vz[h][:, :, :], zv).then_inc(landed[h], 16)
            sp.dma_start(ua[h][:, :, TP:T], zu[:, :, TP:T]).then_inc(landed[h], 16)
            for i, name in enumerate(("w_qm", "w_km")):
                sp.dma_start(wqk[h][:, i, :, :], a[name][0][h].rearrange("(k p) n -> p k n", p=P)).then_inc(landed[h], 16)

        def store(sp, g, s):
            h = g * 2 + s
            sp.wait_ge(proj_out, h * 2 * E + 2 * E)
            sp.dma_start(qk_out[h], qk[s][:, :, :]).then_inc(stored[s], 16)
            sp.wait_ge(rows_a, h * 2 * E + 2 * E)
            sp.wait_ge(rows_b, h * (2 * E + 1) + 2 * E + 1)
            for w, dram in enumerate((kt_dram, vt_dram)):
                col = dram.rearrange("t (h n) -> h t n", n=d.md)[h]
                sp.dma_start(col[0:4 * TT].rearrange("(t p) n -> p t n", p=TT),
                             rows[s][:, w, 0:4, :]).then_inc(stored[s], 16)
                sp.dma_start(col[4 * TT:TP], rows[s][0:LAST, w, 4, :]).then_inc(stored[s], 16)
                sp.dma_start(col[TP:T], srow[s][:, w, :]).then_inc(stored[s], 16)
            cols = lambda x: x.rearrange("w (h n) -> h w n", n=d.md)[h]
            sp.dma_start(cols(conv_prompt[0, 0]), tail[s][0:PRE, :]).then_inc(stored[s], 16)
            for b in range(NB):
                r = PRE + b * (PRE + NS) + NS
                sp.dma_start(cols(conv_sample[0, b]), tail[s][r:r + PRE, :]).then_inc(stored[s], 16)

        @block.sync
        def _(sp):
            sp.dma_start(srows[:, :], a["state_conv"].rearrange("o b w n -> (o b w) n")).then_inc(cin, 16)
            for j in range(W):
                sp.dma_start(cw[:, j, :], a["conv_w"][0, j].rearrange("(c p) -> p c", p=P),
                             allow_slow_non_contiguous=True).then_inc(cin, 16)
            sp.dma_start(cb[:, :], a["conv_b"][0].rearrange("(c p) -> p c", p=P),
                         allow_slow_non_contiguous=True).then_inc(cin, 16)
            for h in range(d.hm):
                load(sp, h)
            for g in range(d.hm // 2):
                for s in range(2):
                    store(sp, g, s)
            for s in range(2):
                sp.wait_ge(stored[s], 16 * STORES * (d.hm // 2))

        @block.vector
        def _(dve):
            for h in range(d.hm):
                nc.vector.memset(u[h][:, :, 0:PRE], 0.0).then_inc(padded, 1)
            dve.wait_ge(cin, 16 * (W + 2))
            for k in range(d.hm * E):
                dve.wait_ge(state_turned, k + 1)
                nc.vector.tensor_copy(state[:, k, :], turn[k % 2][:, 0, 0:NB * PRE]).then_inc(state_out, 1)
            dve.wait_ge(state_out, d.hm * E)
            def activate(h):
                s = h % 2
                dve.wait_ge(landed[h], 16 * LOADS)
                nc.vector.tensor_copy(seg(u[h][:, :, SEG:U])[:, :, :, 0:PRE],
                                      state[:, h * E:(h + 1) * E, :].rearrange(
                                          "p e (b w) -> p e b w", w=PRE)).then_inc(padded, 1)
                nc.vector.tensor_copy(seg(u[h][:, :, SEG:U])[:, :, :, PRE:PRE + NS],
                                      ua[h][:, :, TP:T].rearrange("p e (b s) -> p e b s", s=NS)).then_inc(padded, 1)
                dve.wait_ge(padded, 2 * h + 2 + d.hm)
                for j in range(W):
                    for e in range(E):
                        k = h * E + e
                        x = u[h][:, e, j:j + U - PRE]
                        if j == 0:
                            nc.vector.tensor_scalar(conv[s][:, e, 0:U - PRE], x, cw[:, j, k:k + 1], cb[:, k:k + 1],
                                                    ALU.mult, ALU.add).then_inc(tapped, 1)
                        else:
                            nc.vector.scalar_tensor_tensor(conv[s][:, e, 0:U - PRE], x, cw[:, j, k:k + 1],
                                                           conv[s][:, e, 0:U - PRE], ALU.mult, ALU.add).then_inc(tapped, 1)
                    dve.wait_ge(tapped, (h * W + j + 1) * E)
                dve.wait_ge(gated, h + 1)
                for e in range(E):
                    nc.vector.tensor_tensor(ua[h][:, e, 0:TP], conv[s][:, e, 0:TP], sig[s][:, e, 0:TP],
                                            ALU.mult).then_inc(active, 1)
                    nc.vector.tensor_tensor(
                        ua[h][:, e, TP:T].rearrange("p (b s) -> p b s", s=NS),
                        seg(conv[s][:, :, SEG:U])[:, e, :, 0:NS], seg(sig[s][:, :, SEG:U])[:, e, :, 0:NS],
                        ALU.mult).then_inc(active, 1)

            def edges(h):
                s = h % 2
                if h >= 2:
                    dve.wait_ge(stored[s], 16 * STORES * (h // 2))
                for w in range(2):
                    for e in range(E):
                        dve.wait_ge(turned, h * (2 * E + 1) + w * E + e + 1)
                        tp = turn[(w * E + e) % 2]
                        nc.vector.tensor_copy(rows[s][0:LAST, w, 4, e * P:(e + 1) * P], tp[0:LAST, 1, 0:P])
                        nc.vector.tensor_copy(srow[s][:, w, e * P:(e + 1) * P],
                                              tp[0:d.tsmp, 1, P:2 * P]).then_inc(rows_b, 1)
                dve.wait_ge(turned, (h + 1) * (2 * E + 1))
                nc.vector.tensor_copy(tail[s][:, :], turn[0][0:TAIL, 0, 0:d.md]).then_inc(rows_b, 1)

            activate(0)
            for h in range(d.hm):
                if h + 1 < d.hm:
                    activate(h + 1)
                edges(h)

        @block.scalar
        def _(act):
            def sigmoid(h):
                act.wait_ge(tapped, (h + 1) * W * E)
                nc.scalar.activation(sig[h % 2][:, :, 0:U - PRE], conv[h % 2][:, :, 0:U - PRE],
                                     ACT.Sigmoid).then_inc(gated, 1)

            sigmoid(0)
            for h in range(d.hm):
                s = h % 2
                if h >= 2:
                    act.wait_ge(stored[s], 16 * STORES * (h // 2))
                for i in range(2 * E):
                    act.wait_ge(projected, h * 2 * E + i + 1)
                    nc.scalar.activation(qk[s][:, i, :].rearrange("p (b t) -> p b t", b=2),
                                         proj[i % 2][:, :, 0:d.half], ACT.Copy,
                                         scale=1.0 if i < E else d.md ** -0.5).then_inc(proj_out, 1)
                if h + 1 < d.hm:
                    sigmoid(h + 1)
                for w in range(2):
                    for e in range(E):
                        act.wait_ge(turned, h * (2 * E + 1) + w * E + e + 1)
                        nc.scalar.activation(rows[s][:, w, 0:4, e * P:(e + 1) * P],
                                             turn[(w * E + e) % 2][0:TT, 0, :].rearrange("p (t n) -> p t n", n=P),
                                             ACT.Copy).then_inc(rows_a, 1)

        @block.tensor
        def _(pe):
            pe.wait_ge(cin, 16 * (W + 2))
            for k in range(d.hm * E):
                if k >= 2:
                    pe.wait_ge(state_out, k - 1)
                nc.tensor.transpose(turn[k % 2][:, 0, 0:NB * PRE], srows[:, k * P:(k + 1) * P],
                                    c.ident[0:NB * PRE, 0:NB * PRE]).then_inc(state_turned, 1)
            for h in range(d.hm):
                s = h % 2
                pe.wait_ge(active, 2 * E * (h + 1))
                for i in range(2 * E):
                    m, e = i // E, i % E
                    n = h * 2 * E + i
                    if n >= 2:
                        pe.wait_ge(proj_out, n - 1)
                    for half in range(2):
                        for k in range(E):
                            mm = nc.tensor.matmul(proj[i % 2][:, half, 0:d.half],
                                                  wqk[h][:, m, k, e * P:(e + 1) * P],
                                                  ua[h][:, k, half * d.half:(half + 1) * d.half],
                                                  start=(k == 0), stop=(k == E - 1))
                    mm.then_inc(projected, 1)
                for w in range(2):
                    for e in range(E):
                        i = w * E + e
                        tp = turn[i % 2]
                        if w == 0:
                            pe.wait_ge(proj_out, h * 2 * E + E + e + 1)
                        if i < 2:
                            if h:
                                pe.wait_ge(rows_a, h * 2 * E)
                                pe.wait_ge(rows_b, h * (2 * E + 1))
                            else:
                                pe.wait_ge(state_out, d.hm * E)
                        else:
                            pe.wait_ge(rows_a, h * 2 * E + i - 1)
                            pe.wait_ge(rows_b, h * (2 * E + 1) + i - 1)
                        x = qk[s][:, E + e, :] if w == 0 else vz[h][:, e, :]
                        for t in range(4):
                            nc.tensor.transpose(tp[0:TT, 0, t * P:(t + 1) * P], x[:, t * TT:(t + 1) * TT],
                                                c.ident[:, :])
                        nc.tensor.transpose(tp[0:LAST, 1, 0:P], x[:, 4 * TT:TP], c.ident[:, :])
                        nc.tensor.transpose(tp[0:d.tsmp, 1, P:2 * P], x[:, TP:T],
                                            c.ident[:, :]).then_inc(turned, 1)
                pe.wait_ge(rows_a, h * 2 * E + 2 * E - 1)
                pe.wait_ge(rows_b, h * (2 * E + 1) + 2 * E - 1)
                for e in range(E):
                    mm = nc.tensor.transpose(turn[0][0:TAIL, 0, e * P:(e + 1) * P], u[h][:, e, TP:U], c.ident[:, :])
                mm.then_inc(turned, 1)



def prompt_mlstm(nc, d, a, sems, c, qk_dram, kt_dram, vt_dram, g_dram, mix, c_prompt, n_prompt):
    T, TP, TT, NT = d.t, d.tp, d.tt, d.nt
    LAST = TP - (NT - 1) * TT
    E = d.md // P
    n = [TT] * (NT - 1) + [LAST]
    with ExitStack() as ctx:
        sb = lambda x, s, t=F32: ctx.enter_context(nc.sbuf_tensor(x, s, t))
        ps = lambda x, s: ctx.enter_context(nc.psum_tensor(x, s, F32))
        qk = [sb(f"ml_qk{s}", [P, 2 * E, TP]) for s in range(2)]
        v = [sb(f"ml_v{s}", [TT, NT, d.md + 1]) for s in range(2)]
        kt = [sb(f"ml_kt{s}", [TT, NT, d.md]) for s in range(2)]
        negtop = [sb(f"ml_negtop{s}", [TT, TP]) for s in range(2)]
        floor = [sb(f"ml_floor{s}", [P, TP]) for s in range(2)]
        src = [sb(f"ml_src{s}", [TT, NT]) for s in range(2)]
        w = [sb(f"ml_w{s}", [TT, NT, TP]) for s in range(2)]
        tri = sb("ml_tri", [TT, TT])
        mag = [sb(f"ml_mag{i}", [P, TT]) for i in range(2)]
        state = [sb(f"ml_state{s}", [P, E, d.md + 1]) for s in range(2)]
        score = [ps(f"ml_score{i}", [P, 2, 512]) for i in range(2)]
        num = [ps(f"ml_num{i}", [P, 512]) for i in range(2)]
        acc = [ps(f"ml_acc{e}", [P, 512]) for e in range(E)]
        tri_made, ones_made = sems("ml_tri_made"), sems("ml_ones_made")
        landed = [sems(f"ml_landed{s}") for s in range(2)]
        stored = [sems(f"ml_stored{s}") for s in range(2)]
        shifted, raised, keyed, cut, weighed, scored, summed, abs_made, floored, inverted, placed, state_summed, \
            state_out = (sems(f"ml_{x}") for x in (
                "shifted", "raised", "keyed", "cut", "weighed", "scored", "summed", "abs_made", "floored",
                "inverted", "placed", "state_summed", "state_out"))
        LOADS = 9
        qk_in = qk_dram.rearrange("(h c p) t -> h p c t", h=d.hm, p=P)
        block = ctx.enter_context(nc.Block())

        def rows(x, h):
            return x.rearrange("t (h n) -> h t n", n=d.md)[h]

        def load(sp, h, s):
            def get(out, src_ap, **kw):
                sp.dma_start(out, src_ap, **kw).then_inc(landed[s], 16)
            get(qk[s][:, :, :], qk_in[h][:, :, 0:TP])
            for out, x in ((v[s][:, :, 0:d.md], rows(vt_dram, h)), (kt[s][:, :, :], rows(kt_dram, h))):
                get(out[:, 0:NT - 1, :], x[0:(NT - 1) * TT].rearrange("(t p) n -> p t n", p=TT))
                get(out[0:LAST, NT - 1, :], x[(NT - 1) * TT:TP])
            get(negtop[s][:, :], g_dram[G_NEGTOP, h:h + 1, 0:TP].to_broadcast([TT, TP]))
            get(floor[s][:, :], g_dram[G_FLOOR, h:h + 1, 0:TP].to_broadcast([P, TP]))
            get(src[s][:, 0:NT - 1], g_dram[G_SOURCE, h, 0:(NT - 1) * TT].rearrange("(t p) -> p t", p=TT),
                allow_slow_non_contiguous=True)
            get(src[s][0:LAST, NT - 1:NT], g_dram[G_SOURCE, h:h + 1, (NT - 1) * TT:TP].rearrange("o p -> p o"),
                allow_slow_non_contiguous=True)

        @block.sync
        def _(sp):
            for s in range(2):
                load(sp, s, s)
            for h in range(d.hm):
                s = h % 2
                sp.wait_ge(state_out, E * (h + 1))
                sp.dma_start(c_prompt[0, 0, h].rearrange("(e p) n -> p e n", p=P),
                             state[s][:, :, 0:d.md]).then_inc(stored[s], 16)
                sp.dma_start(n_prompt[0, 0, h].rearrange("(e p) -> p e", p=P), state[s][:, :, d.md],
                             allow_slow_non_contiguous=True).then_inc(stored[s], 16)
                if h + 2 < d.hm:
                    sp.wait_ge(placed, NT * (h + 1))
                    load(sp, h + 2, s)
            for s in range(2):
                sp.wait_ge(stored[s], 32 * (d.hm // 2))

        @block.gpsimd
        def _(pool):
            nc.gpsimd.memset(tri[:, :], 1.0).then_inc(tri_made, 1)
            pool.wait_ge(tri_made, 1)
            nc.gpsimd.affine_select(out=tri[:, :], in_=tri[:, :], compare_op=ALU.is_ge, fill=0.0, base=0,
                                    pattern=[[1, TT]], channel_multiplier=-1).then_inc(tri_made, 1)

        def pe_scores(pe, h, j):
            s, i = h % 2, h * NT + j
            if i >= 2:
                pe.wait_ge(weighed, i - 1)
            width = TP - j * TT
            for b, (c0, c1) in enumerate(((0, width // 2), (width // 2, width)) if width > 512 else ((0, width),)):
                for e in range(E):
                    mm = nc.tensor.matmul(score[i % 2][0:n[j], b, 0:c1 - c0],
                                          qk[s][:, E + e, j * TT:j * TT + n[j]],
                                          qk[s][:, e, j * TT + c0:j * TT + c1], start=(e == 0), stop=(e == E - 1))
            mm.then_inc(scored, 1)

        def pe_sum(pe, h, t):
            s, i = h % 2, h * NT + t
            pe.wait_ge(weighed, i + 1)
            if i >= 2:
                pe.wait_ge(placed, i - 1)
            cols = slice(t * TT, t * TT + n[t])
            for e in range(E + 1):
                for j in range(t + 1):
                    lhs = v[s][0:n[j], j, e * P:(e + 1) * P] if e < E else c.ones[0:n[j], :]
                    mm = nc.tensor.matmul(num[i % 2][:, e * TT:e * TT + n[t]], lhs, w[s][0:n[j], j, cols],
                                          start=(j == 0), stop=(j == t))
            mm.then_inc(summed, 1)

        def pe_state(pe, h):
            s = h % 2
            pe.wait_ge(keyed, NT * (h + 1))
            if h:
                pe.wait_ge(state_out, E * h)
            for e in range(E):
                for j in range(NT):
                    mm = nc.tensor.matmul(acc[e][:, 0:d.md + 1], kt[s][0:n[j], j, e * P:(e + 1) * P],
                                          v[s][0:n[j], j, :], start=(j == 0), stop=(j == NT - 1))
                mm.then_inc(state_summed, 1)

        @block.tensor
        def _(pe):
            pe.wait_ge(ones_made, 2)
            for h in range(d.hm):
                pe.wait_ge(landed[h % 2], 16 * LOADS * (h // 2 + 1))
                for j in range(NT):
                    pe_scores(pe, h, j)
                    if j:
                        pe_sum(pe, h, j - 1)
                pe_state(pe, h)
                pe_sum(pe, h, NT - 1)

        def dve_weigh(dve, h, j):
            s, i = h % 2, h * NT + j
            width = TP - j * TT
            dve.wait_ge(raised, i + 1)
            row = w[s][0:n[j], j, :]
            nc.vector.tensor_scalar(kt[s][0:n[j], j, :], kt[s][0:n[j], j, :], row[:, TP - 1:TP], None,
                                    ALU.mult).then_inc(keyed, 1)
            dve.wait_ge(keyed, i + 1)
            nc.vector.tensor_tensor(row[:, j * TT:j * TT + n[j]], row[:, j * TT:j * TT + n[j]],
                                    tri[0:n[j], 0:n[j]], ALU.mult).then_inc(cut, 1)
            dve.wait_ge(cut, i + 1)
            dve.wait_ge(scored, i + 1)
            for b, (c0, c1) in enumerate(((0, width // 2), (width // 2, width)) if width > 512 else ((0, width),)):
                ins = nc.vector.tensor_tensor(row[:, j * TT + c0:j * TT + c1], score[i % 2][0:n[j], b, 0:c1 - c0],
                                              row[:, j * TT + c0:j * TT + c1], ALU.mult)
            ins.then_inc(weighed, 1)

        def dve_place(dve, h, t):
            s, i = h % 2, h * NT + t
            dve.wait_ge(abs_made, i + 1)
            cols = slice(t * TT, t * TT + n[t])
            m = mag[i % 2][:, 0:n[t]]
            nc.vector.tensor_tensor(m, m, floor[s][:, cols], ALU.max).then_inc(floored, 1)
            dve.wait_ge(floored, i + 1)
            nc.vector.reciprocal(m, m).then_inc(inverted, 1)
            dve.wait_ge(inverted, i + 1)
            for e in range(E):
                ins = nc.vector.tensor_tensor(mix[:, d.ha + h * E + e, cols], num[i % 2][:, e * TT:e * TT + n[t]],
                                              m, ALU.mult)
            ins.then_inc(placed, 1)

        @block.vector
        def _(dve):
            for s in range(2):
                nc.vector.memset(v[s][:, :, d.md:d.md + 1], 1.0).then_inc(ones_made, 1)
            dve.wait_ge(tri_made, 2)
            for h in range(d.hm):
                s = h % 2
                dve.wait_ge(landed[s], 16 * LOADS * (h // 2 + 1))
                if h >= 2:
                    dve.wait_ge(summed, NT * (h - 1))
                for j in range(NT):
                    nc.vector.tensor_scalar(w[s][0:n[j], j, j * TT:TP], negtop[s][0:n[j], j * TT:TP],
                                            src[s][0:n[j], j:j + 1], 0.0, ALU.add, ALU.min).then_inc(shifted, 1)
                for j in range(NT):
                    dve_weigh(dve, h, j)
                    if j:
                        dve_place(dve, h, j - 1)
                dve_place(dve, h, NT - 1)

        @block.scalar
        def _(act):
            for h in range(d.hm):
                s = h % 2
                for j in range(NT):
                    act.wait_ge(shifted, h * NT + j + 1)
                    nc.scalar.activation(w[s][0:n[j], j, j * TT:TP], w[s][0:n[j], j, j * TT:TP],
                                         ACT.Exp).then_inc(raised, 1)

                def magnitude(t):
                    i = h * NT + t
                    act.wait_ge(summed, i + 1)
                    if i >= 2:
                        act.wait_ge(placed, i - 1)
                    nc.scalar.activation(mag[i % 2][:, 0:n[t]], num[i % 2][:, E * TT:E * TT + n[t]],
                                         ACT.Abs).then_inc(abs_made, 1)
                for t in range(NT - 1):
                    magnitude(t)
                if h >= 2:
                    act.wait_ge(stored[s], 32 * (h // 2))
                for e in range(E):
                    act.wait_ge(state_summed, E * h + e + 1)
                    nc.scalar.activation(state[s][:, e, :], acc[e][:, 0:d.md + 1], ACT.Copy).then_inc(state_out, 1)
                magnitude(NT - 1)


def sample_mlstm(nc, d, a, sems, c, qk_dram, kt_dram, vt_dram, g_dram, mix, c_sample, n_sample):
    T, TP, NB, NS, TS = d.t, d.tp, d.nb, d.ns, d.tsmp
    E, MD = d.md // P, d.md
    with ExitStack() as ctx:
        sb = lambda x, s, t=F32: ctx.enter_context(nc.sbuf_tensor(x, s, t))
        ps = lambda x, s: ctx.enter_context(nc.psum_tensor(x, s, F32))
        qk = [sb(f"sm_qk{s}", [P, 2 * E, TS]) for s in range(d.hm)]
        qn = [sb(f"sm_qn{s}", [P, E, TS]) for s in range(2)]
        v = [sb(f"sm_v{s}", [P, MD + 1]) for s in range(d.hm)]
        kt = [sb(f"sm_kt{s}", [TS, MD]) for s in range(d.hm)]
        kw = [sb(f"sm_kw{s}", [P, NB, MD]) for s in range(2)]
        negtop = [sb(f"sm_negtop{s}", [TS, TS]) for s in range(d.hm)]
        floor = [sb(f"sm_floor{s}", [P, TS]) for s in range(d.hm)]
        inter = [sb(f"sm_inter{s}", [P, TS]) for s in range(d.hm)]
        src = [sb(f"sm_src{s}", [TS, 1]) for s in range(d.hm)]
        c0 = [sb(f"sm_c0{s}", [P, NB, E, MD + 1]) for s in range(d.hm)]
        w = [sb(f"sm_w{s}", [TS, TS]) for s in range(2)]
        sw = [sb(f"sm_sw{s}", [TS, TS]) for s in range(2)]
        own = sb("sm_own", [TS, TS])
        mag = sb("sm_mag", [P, TS])
        nrows = sb("sm_nrows", [NB * d.hm, MD])
        ncols = sb("sm_ncols", [P, E, NB * d.hm])
        nbh = lambda x: x.rearrange("p e (b h) -> p b e h", h=d.hm)
        score = ps("sm_score", [P, 512])
        num = [ps(f"sm_num{e}", [P, 512]) for e in range(E + 1)]
        acc = [ps(f"sm_acc{i}", [P, 512]) for i in range(4)]
        own_made, ones_made = sems("sm_own_made"), sems("sm_ones_made")
        landed = [sems(f"sm_landed{s}") for s in range(d.hm)]
        states_in, states_turned, states_put, new_put, new_turned, new_out, stored = (sems(f"sm_{x}") for x in (
            "states_in", "states_turned", "states_put", "new_put", "new_turned", "new_out", "stored"))
        shifted, raised, masked, weighed, scaled, normed, scored, summed, abs_made, floored, inverted, placed, \
            keyed, updated, state_new = (sems(f"sm_{x}") for x in (
                "shifted", "raised", "masked", "weighed", "scaled", "normed", "scored", "summed", "abs_made",
                "floored", "inverted", "placed", "keyed", "updated", "state_new"))
        LOADS = 7 + NB
        qk_in = qk_dram.rearrange("(h c p) t -> h p c t", h=d.hm, p=P)
        block = ctx.enter_context(nc.Block())

        def load(sp, h, s):
            def get(out, x, **kw_):
                sp.dma_start(out, x, **kw_).then_inc(landed[s], 16)
            rows = lambda x: x.rearrange("t (h n) -> h t n", n=MD)[h][TP:T]
            get(qk[s][:, :, :], qk_in[h][:, :, TP:T])
            get(v[s][0:TS, 0:MD], rows(vt_dram))
            get(kt[s][:, :], rows(kt_dram))
            get(negtop[s][:, :], g_dram[G_NEGTOP, h:h + 1, TP:T].to_broadcast([TS, TS]))
            get(floor[s][:, :], g_dram[G_FLOOR, h:h + 1, TP:T].to_broadcast([P, TS]))
            get(inter[s][:, :], g_dram[G_INTER, h:h + 1, TP:T].to_broadcast([P, TS]))
            get(src[s][:, :], g_dram[G_SOURCE, h:h + 1, TP:T].rearrange("o p -> p o"),
                allow_slow_non_contiguous=True)
            for b in range(NB):
                get(c0[s][:, b, :, 0:MD], a["state_C"][0, b, h].rearrange("(e p) n -> p e n", p=P))

        @block.sync
        def _(sp):
            sp.dma_start(nrows[:, :], a["state_n"][0].rearrange("b h n -> (b h) n")).then_inc(states_in, 16)
            sp.wait_ge(ones_made, 2 * d.hm)
            for h in range(d.hm):
                load(sp, h, h)
            for h in range(d.hm):
                for b in range(NB):
                    sp.wait_ge(state_new, E * (h * NB + b + 1))
                    sp.dma_start(c_sample[0, b, h].rearrange("(e p) n -> p e n", p=P),
                                 c0[h][:, b, :, 0:MD]).then_inc(stored, 16)
            sp.wait_ge(new_out, E)
            sp.dma_start(n_sample[0].rearrange("b h n -> (b h) n"), nrows[:, :]).then_inc(stored, 16)
            sp.wait_ge(stored, 16 * (NB * d.hm + 1))

        @block.gpsimd
        def _(pool):
            own3 = own[:, :].rearrange("p (b s) -> p b s", s=NS)
            nc.gpsimd.memset(own[:, :], 1.0).then_inc(own_made, 1)
            pool.wait_ge(own_made, 1)
            nc.gpsimd.affine_select(out=own[:, :], in_=own[:, :], compare_op=ALU.is_ge, fill=0.0, base=0,
                                    pattern=[[1, TS]], channel_multiplier=-1).then_inc(own_made, 1)
            pool.wait_ge(own_made, 2)
            nc.gpsimd.affine_select(out=own3, in_=own3, compare_op=ALU.is_ge, fill=0.0, base=0,
                                    pattern=[[-NS, NB], [0, NS]], channel_multiplier=1).then_inc(own_made, 1)

        @block.vector
        def _(dve):
            V = nc.vector
            for s in range(d.hm):
                V.memset(v[s][:, 0:MD], 0.0).then_inc(ones_made, 1)
                V.memset(v[s][:, MD:MD + 1], 1.0).then_inc(ones_made, 1)
            for s in range(2):
                V.memset(kw[s][:, :, :], 0.0).then_inc(ones_made, 1)
            dve.wait_ge(ones_made, 2 * d.hm + 2)
            dve.wait_ge(own_made, 3)
            dve.wait_ge(states_turned, E)
            V.tensor_copy(ncols[:, :, :], acc[0][:, 0:E * NB * d.hm].rearrange("p (e x) -> p e x", e=E))\
                .then_inc(states_put, 1)
            dve.wait_ge(states_put, 1)
            for h in range(d.hm):
                s = h % 2
                dve.wait_ge(landed[h], 16 * LOADS)
                V.tensor_copy(c0[h][:, :, :, MD], nbh(ncols[:, :, :])[:, :, :, h]).then_inc(states_put, 1)
                V.tensor_scalar(w[s][:, :], negtop[h][:, :], src[h][:, :], 0.0, ALU.add, ALU.min).then_inc(shifted, 1)
                if h >= 2:
                    dve.wait_ge(summed, h - 1)
                dve.wait_ge(states_put, h + 2)
                dve.wait_ge(scored, h + 1)
                for e in range(E):
                    V.tensor_tensor(qk[h][:, e, :], qk[h][:, e, :], inter[h][:, :], ALU.mult).then_inc(scaled, 1)
                dve.wait_ge(scaled, E * (h + 1))
                for e in range(E):
                    V.tensor_tensor(qn[s][:, e, :].rearrange("p (b s) -> p b s", s=NS),
                                    qk[h][:, e, :].rearrange("p (b s) -> p b s", s=NS),
                                    c0[h][:, :, e, MD:MD + 1].to_broadcast([P, NB, NS]), ALU.mult).then_inc(normed, 1)
                dve.wait_ge(raised, h + 1)
                V.tensor_tensor(w[s][:, :], w[s][:, :], own[:, :], ALU.mult).then_inc(masked, 1)
                dve.wait_ge(masked, h + 1)
                V.tensor_tensor(sw[s][:, :], score[0:TS, 0:TS], w[s][:, :], ALU.mult).then_inc(weighed, 1)
                if h >= 2:
                    dve.wait_ge(updated, E * NB * (h - 1))
                for b in range(NB):
                    last = b * NS + NS - 1
                    V.tensor_scalar(kw[s][0:TS, b, :], kt[h][:, :], w[s][:, last:last + 1], None,
                                    ALU.mult).then_inc(keyed, 1)
                dve.wait_ge(abs_made, h + 1)
                V.tensor_tensor(mag[:, :], mag[:, :], floor[h][:, :], ALU.max).then_inc(floored, 1)
                dve.wait_ge(floored, h + 1)
                V.reciprocal(mag[:, :], mag[:, :]).then_inc(inverted, 1)
                dve.wait_ge(inverted, h + 1)
                for e in range(E):
                    ins = V.tensor_tensor(mix[:, d.ha + h * E + e, TP:T], num[e][:, 0:TS], mag[:, :], ALU.mult)
                ins.then_inc(placed, 1)
                for b in range(NB):
                    last = b * NS + NS - 1
                    for e in range(E):
                        i = (h * NB + b) * E + e
                        dve.wait_ge(updated, i + 1)
                        V.scalar_tensor_tensor(c0[h][:, b, e, :], c0[h][:, b, e, :], inter[h][:, last:last + 1],
                                               acc[i % 4][:, 0:MD + 1], ALU.mult, ALU.add).then_inc(state_new, 1)
                dve.wait_ge(state_new, E * NB * (h + 1))
                V.tensor_copy(nbh(ncols[:, :, :])[:, :, :, h], c0[h][:, :, :, MD]).then_inc(new_put, 1)
            for e in range(E):
                dve.wait_ge(new_turned, e + 1)
                V.tensor_copy(nrows[:, e * P:(e + 1) * P], acc[e][0:NB * d.hm, 0:P]).then_inc(new_out, 1)

        @block.scalar
        def _(act):
            for h in range(d.hm):
                s = h % 2
                act.wait_ge(shifted, h + 1)
                nc.scalar.activation(w[s][:, :], w[s][:, :], ACT.Exp).then_inc(raised, 1)
                act.wait_ge(summed, h + 1)
                if h:
                    act.wait_ge(placed, h)
                nc.scalar.activation(mag[:, :], num[E][:, 0:TS], ACT.Abs).then_inc(abs_made, 1)

        @block.tensor
        def _(pe):
            pe.wait_ge(ones_made, 2 * d.hm + 2)
            pe.wait_ge(states_in, 16)
            for e in range(E):
                nc.tensor.transpose(acc[0][:, e * NB * d.hm:(e + 1) * NB * d.hm], nrows[:, e * P:(e + 1) * P],
                                    c.ident[0:NB * d.hm, 0:NB * d.hm]).then_inc(states_turned, 1)
            for h in range(d.hm):
                s = h % 2
                pe.wait_ge(landed[h], 16 * LOADS)
                if h:
                    pe.wait_ge(weighed, h)
                for e in range(E):
                    mm = nc.tensor.matmul(score[0:TS, 0:TS], qk[h][:, E + e, :], qk[h][:, e, :],
                                          start=(e == 0), stop=(e == E - 1))
                mm.then_inc(scored, 1)
                pe.wait_ge(weighed, h + 1)
                pe.wait_ge(normed, E * (h + 1))
                if h:
                    pe.wait_ge(placed, h)
                for e in range(E):
                    nc.tensor.matmul(num[e][:, 0:TS], v[h][0:TS, e * P:(e + 1) * P], sw[s][:, :], start=True,
                                     stop=False, skip_group_check=True)
                    for b in range(NB):
                        cols = slice(b * NS, (b + 1) * NS)
                        for k in range(E):
                            nc.tensor.matmul(num[e][:, cols], c0[h][:, b, k, e * P:(e + 1) * P], qk[h][:, k, cols],
                                             start=False, stop=(b == NB - 1 and k == E - 1), skip_group_check=True)
                nc.tensor.matmul(num[E][:, 0:TS], c.ones[0:TS, :], sw[s][:, :], start=True, stop=False)
                for k in range(E):
                    mm = nc.tensor.matmul(num[E][:, 0:TS], c.ones[:, :], qn[s][:, k, :], start=False,
                                          stop=(k == E - 1))
                mm.then_inc(summed, 1)
                for b in range(NB):
                    for e in range(E):
                        i = (h * NB + b) * E + e
                        if e == 0:
                            pe.wait_ge(keyed, h * NB + b + 1)
                        if i >= 4:
                            pe.wait_ge(state_new, i - 3)
                        nc.tensor.matmul(acc[i % 4][:, 0:MD + 1], kw[s][:, b, e * P:(e + 1) * P], v[h][:, :],
                                         start=True, stop=True).then_inc(updated, 1)
            pe.wait_ge(new_put, d.hm)
            for e in range(E):
                nc.tensor.transpose(acc[e][0:NB * d.hm, 0:P], ncols[:, e, :], c.ident[:, :]).then_inc(new_turned, 1)


def decode_attention(nc, d, a, sems, c, zn_dram, vs_rows, mix):
    HA, VD, HD, NS, NB, TP, TS = d.ha, d.vd, d.hd, d.ns, d.nb, d.tp, d.tsmp
    PG, R = d.pages, d.ha * 2 * d.ns
    PAST, KEYS = PG * P, PG * P + TS
    RING = 8
    GR = PG // 2
    EV = GR + 1
    PIECES = 4
    PW = KEYS // PIECES
    assert d.page == P and PG % RING == 0 and KEYS % PIECES == 0 and d.aw == 2 * 512 and NB % 2 == 0
    with ExitStack() as ctx:
        sb = lambda x, s, t=F32: ctx.enter_context(nc.sbuf_tensor(x, s, t))
        ps = lambda x, s: ctx.enter_context(nc.psum_tensor(x, s, F32))
        ring = sb("dc_pages", [P, RING, d.aw])
        kh = [sb(f"dc_kh{i}", [P, HA, 2 * P], F32R) for i in range(2)]
        kl = [sb(f"dc_kl{i}", [P, HA, 2 * P], F32R) for i in range(2)]
        vslot = lambda x, p: x[(p % 4) // 2][:, :, :].rearrange("p h t -> p (h t)")[:, (p % 2) * d.aw:(p % 2 + 1) * d.aw]
        sc = [sb(f"dc_scores{i}", [R, KEYS]) for i in range(2)]
        bias = sb("dc_bias", [R, PAST])
        own_bias = sb("dc_own_bias", [R, NB, TS])
        ph, pl = ([sb(f"dc_{x}{i}", [P, PG, R], F32R) for i in range(2)] for x in ("ph", "pl"))
        pown = [sb(f"dc_pown{i}", [TS, R]) for i in range(2)]
        qs, ks = sb("dc_qs", [P, HA, TS]), sb("dc_ks", [P, HA, TS])
        vown = sb("dc_vown", [TS, d.aw])
        qhl = [sb(f"dc_qhl{i}", [P, HA, 2 * R], F32R) for i in range(2)]
        lower_scores = [sb(f"dc_lower_scores{i}", [R, 2 * P]) for i in range(2)]
        qflat = sb("dc_q", [P, HA * (R + 2 * NS)])
        qf = qflat[:, 0:HA * R].rearrange("p (h r) -> p h r", r=R)
        qdiag = qflat[:, :].rearrange("p (h x) -> p h x", x=R + 2 * NS)
        own_rows = sb("dc_own_rows", [R, d.aw])
        kept = sb("dc_kept", [R, VD])
        comb = sb("dc_comb", [R, TS])
        heads = sb("dc_heads", [R, HA])
        line = sb("dc_line", [1, 3, R])
        cols = sb("dc_cols", [R, 3])
        tops, low, dens, coef = sb("dc_tops", [R, PIECES + 1]), sb("dc_low", [R, 2]), \
            sb("dc_dens", [R, 2, PIECES]), sb("dc_coef", [R, 2])
        ptab = sb("dc_page_table", [1, NB * PG], I32)
        pk = [ps(f"dc_pk{i}", [P, 1024]) for i in range(2)]
        pscore = [ps(f"dc_pscore{i}", [P, 512]) for i in range(2)]
        pout = ps("dc_pout", [P, 1024])
        table_in, inputs_in, lined, columns, consts = (sems(f"dc_{x}") for x in (
            "table_in", "inputs_in", "lined", "columns", "consts"))
        own_bias_steps, lower_out, half_biased = (sems(f"dc_{x}") for x in ("own_bias_steps", "lower_out", "half_biased"))
        assert 2 * R == P
        page_in = [sems(f"dc_page_in{i}") for i in range(RING)]
        kturned, khi, klo, q_laid, qhi, qlo, scored, biased, topped, lowered, raised, pturned, phi, plo, \
            own_turned, own_out, vhi, vlo, valued, summed, inverted, kept_all, kept_one, combined, placed = (
                sems(f"dc_{x}") for x in (
                    "kturned", "khi", "klo", "q_laid", "qhi", "qlo", "scored", "biased", "topped",
                    "lowered", "raised", "pturned", "phi", "plo", "own_turned", "own_out", "vhi", "vlo", "valued",
                    "summed", "inverted", "kept_all", "kept_one", "combined", "placed"))
        pages = [x[0].rearrange("n p h e -> n p (h e)") for x in (a["cache_k"], a["cache_v"])]
        block = ctx.enter_context(nc.Block())

        def load_phase(sp, which, b, freed, freed_before):
            def page(p, slot, given_back, count):
                idx = sp.value_load(ptab[0:1, bass.ds(b * PG + p, 1)], min_val=0, max_val=d.pool - 1)
                if given_back is not None:
                    sp.wait_ge(given_back, count)
                sp.dma_start(ring[:, slot, :], pages[which][idx]).then_inc(page_in[slot], 16)
            for slot in range(RING):
                if freed_before is None:
                    page(slot, slot, None, 0)
                else:
                    page(slot, slot, freed_before[0], freed_before[1] + (slot + 1))
            with sp.Fori(0, PG // RING - 1) as i:
                for slot in range(RING):
                    page((i + 1) * RING + slot, slot, freed, b * PG + i * RING + (slot + 1))

        @block.sync
        def _(sp):
            sp.dma_start(ptab[:, :], a["page_table"].rearrange("(o b) g -> o (b g)", o=1)).then_inc(table_in, 16)
            zs = zn_dram.rearrange("(w h p) t -> w p h t", w=2, p=P)
            sp.dma_start(qs[:, :, :], zs[0][:, :, TP:d.t]).then_inc(inputs_in, 16)
            sp.dma_start(ks[:, :, :], zs[1][:, :, TP:d.t]).then_inc(inputs_in, 16)
            sp.dma_start(vown[:, :], vs_rows).then_inc(inputs_in, 16)
            sp.wait_ge(table_in, 16)
            last = PG - RING
            load_phase(sp, 0, 0, kturned, None)
            load_phase(sp, 0, 1, kturned, (kturned, last))
            load_phase(sp, 1, 0, vlo, (kturned, PG + last))
            with sp.Fori(1, NB // 2) as g:
                b = g * 2
                load_phase(sp, 0, b, kturned, (vlo, (b - 2) * PG + last))
                load_phase(sp, 1, b - 1, vlo, (kturned, b * PG + last))
                load_phase(sp, 0, b + 1, kturned, (vlo, (b - 1) * PG + last))
                load_phase(sp, 1, b, vlo, (kturned, (b + 1) * PG + last))
            load_phase(sp, 1, NB - 1, vlo, (vlo, (NB - 2) * PG + last))

        @block.gpsimd
        def _(pool):
            n = [0]

            def done(instruction):
                instruction.then_inc(lined, 1)
                n[0] += 1
                pool.wait_ge(lined, n[0])
            G = nc.gpsimd
            l3 = lambda i: line[:, i, :].rearrange("o (h m q) -> o h m q", m=2, q=NS)
            for h in range(HA):
                done(G.memset(l3(0)[:, h, :, :], 2.0 ** (-8.0 * (h + 1) / HA)))
            done(G.iota(line[:, 1, :], pattern=[[0, 2 * HA], [1, NS]], base=0, channel_multiplier=0,
                        allow_small_or_imprecise_dtypes=True))
            done(G.memset(line[:, 2, :], 1.0))
            done(G.iota(bias[:, :], pattern=[[1, PAST]], base=-PAST, channel_multiplier=0,
                        allow_small_or_imprecise_dtypes=True))
            done(G.iota(own_bias[:, :, :], pattern=[[0, NB * NB], [1, NS]], base=0, channel_multiplier=0,
                        allow_small_or_imprecise_dtypes=True))
            done(G.memset(heads[:, :], 1.0))
            done(G.affine_select(out=heads[:, :], in_=heads[:, :], compare_op=ALU.is_ge, fill=0.0, base=0,
                                 pattern=[[-2 * NS, HA]], channel_multiplier=1))
            done(G.affine_select(out=heads[:, :], in_=heads[:, :], compare_op=ALU.is_ge, fill=0.0,
                                 base=2 * NS - 1, pattern=[[2 * NS, HA]], channel_multiplier=-1))
            pool.wait_ge(consts, 5)
            ob = own_bias[:, :, :].rearrange("r b (s j) -> r b s j", j=NS)
            G.affine_select(out=ob, in_=ob, compare_op=ALU.is_equal, fill=FILL, base=0,
                            pattern=[[1, NB], [-1, NB], [0, NS]], channel_multiplier=0).then_inc(consts, 1)

        LINED = HA + 7
        TURNED_AT = (PG - 3, PG - 1)
        TURN_AT = PG - 5

        def pe_k(pe, b, s, f, hook=None, very_first=False):
            pe.wait_ge(qlo, b + 1)

            def body(i, first):
                for slot in range(RING):
                    n = b * PG + i * RING + slot
                    pe.wait_ge(page_in[slot], f * (16 * PG // RING) + i * 16 + 16)
                    if first and slot == 0 and hook is not None:
                        pe.wait_ge(plo, b * 2)
                    if not (very_first and first and slot < 2):
                        pe.wait_ge(klo, n - 1)
                    for h in range(HA):
                        mm = nc.tensor.transpose(pk[slot % 2][:, h * P:(h + 1) * P],
                                                 ring[:, slot, h * P:(h + 1) * P], c.ident[:, :])
                    mm.then_inc(kturned, 1)
                    if slot % 2 == 1 and not (first and slot == 1):
                        group(i * (RING // 2) + slot // 2 - 1, (slot // 2 - 1) % 2, first and slot <= 5)
                    if first and slot == 3 and hook is not None:
                        pe_combine(pe, hook)

            def group(g, k, early):
                pe.wait_ge(klo, b * PG + g * 2 + 2)
                if hook is not None and early and k == 0:
                    pe.wait_ge(own_out, b)
                if hook is not None and early and k == 1:
                    pe.wait_ge(placed, hook + 1)
                if not (very_first and early):
                    pe.wait_ge(biased, b * EV if early else b * EV + g - 1)
                for h in range(HA):
                    leading = lambda: nc.tensor.matmul(pscore[k][:, 0:2 * P], qhl[s][:, h, :], kh[k][:, h, :],
                                                       start=(h == 0), stop=(h == HA - 1))
                    if h == 0:
                        leading()
                    mm = nc.tensor.matmul(pscore[k][0:R, 0:2 * P], qhl[s][:, h, 0:R], kl[k][:, h, :],
                                          start=False, stop=False)
                    if h:
                        mm = leading()
                mm.then_inc(scored, 1)

            body(0, True)
            with pe.Fori(1, PG // RING) as i:
                body(i, False)
            group(GR - 1, (GR - 1) % 2, False)
            pe.wait_ge(biased, b * EV + (GR - 1))
            for h in range(HA):
                mm = nc.tensor.matmul(pscore[0][0:R, 0:TS], qf[:, h, :], ks[:, h, :], start=(h == 0),
                                      stop=(h == HA - 1))
            mm.then_inc(scored, 1)

        def pe_turn(pe, b, s, kphases):
            pe.wait_ge(raised, b * PIECES + PIECES)
            pe.wait_ge(klo, kphases * PG)
            pe.wait_ge(biased, kphases * EV)
            for i in range(2):
                for j in range(PG // 2):
                    p = i * (PG // 2) + j
                    out, x = pk[i][:, j * R:(j + 1) * R], sc[s][:, p * P:(p + 1) * P]
                    mm = nc.tensor.matmul(out, x, c.ident[0:R, 0:R], start=True, stop=True) if p == 0 else \
                        nc.tensor.transpose(out, x, c.ident[0:R, 0:R])
                mm.then_inc(pturned, 1)
            nc.tensor.transpose(pscore[0][0:TS, 0:R], sc[s][:, PAST:KEYS], c.ident[0:R, 0:R]).then_inc(own_turned, 1)

        def pe_v(pe, b, s, following):
            for p in range(PG):
                if p % (PG // 2) == 0:
                    pe.wait_ge(plo, b * 2 + 1 + p // (PG // 2))
                pe.wait_ge(vlo, b * PG + p + 1)
                if p == 0 and not (isinstance(b, int) and b == 0):
                    pe.wait_ge(kept_all, b)
                for half in range(2):
                    cs = slice(half * 512, half * 512 + 512)
                    mm = exact_passes(nc, pout[0:R, cs], ph[s][:, p, :], pl[s][:, p, :], vslot(kh, p)[:, cs],
                                      vslot(kl, p)[:, cs], p == 0, False)
                mm.then_inc(valued, 1)
                if following is not None and p == TURN_AT:
                    pe_turn(pe, following, 1 - s, following + 1)
            pe.wait_ge(own_out, b + 1)
            for half in range(2):
                cs = slice(half * 512, half * 512 + 512)
                mm = nc.tensor.matmul(pout[0:R, cs], pown[s][:, :], vown[:, cs], start=False, stop=True)
            mm.then_inc(summed, 1)

        def pe_combine(pe, b):
            pe.wait_ge(kept_one, b + 1)
            nc.tensor.matmul(pscore[1][:, 0:TS], kept[:, :], comb[:, :], start=True, stop=True).then_inc(combined, 1)

        @block.tensor
        def _(pe):
            pe.wait_ge(lined, LINED)
            pe.wait_ge(columns, 1)
            for i in range(3):
                mm = nc.tensor.matmul(pscore[1][0:R, i:i + 1], line[0:1, i, :], c.ones[0:1, 0:1], start=True, stop=True)
            mm.then_inc(columns, 1)
            pe_k(pe, 0, 0, 0, very_first=True)
            pe_k(pe, 1, 1, 1)
            pe_turn(pe, 0, 0, 2)
            pe_v(pe, 0, 0, 1)

            def pair(g):
                b = g * 2
                pe_k(pe, b, 0, g * 4 - 1, hook=b - 2)
                pe_v(pe, b - 1, 1, b)
                pe_k(pe, b + 1, 1, g * 4 + 1, hook=b - 1)
                pe_v(pe, b, 0, b + 1)
            with pe.Fori(1, NB // 2 - 1) as g:
                pair(g)
            pair(NB // 2 - 1)
            pe_combine(pe, NB - 2)
            pe.wait_ge(placed, NB - 1)
            pe_v(pe, NB - 1, 1, None)
            pe_combine(pe, NB - 1)

        def dve_q(dve, b, s, first):
            if not first:
                dve.wait_ge(scored, b * EV)
            for m in range(2):
                rows = slice(m * HD, (m + 1) * HD)
                nc.vector.tensor_copy(qdiag[rows, :, m * NS:(m + 1) * NS],
                                      qs[rows, :, bass.ds(b * NS, NS)]).then_inc(q_laid, 1)

        def dve_q_low(dve, b, s):
            dve.wait_ge(qhi, b + 1)
            nc.vector.tensor_tensor(qhl[s][:, :, R:2 * R], qf[:, :, :], qhl[s][:, :, 0:R].bitcast(F32),
                                    ALU.subtract).then_inc(qlo, 1)

        def dve_k(dve, b, s, hook=None):
            def take(g, k):
                dve.wait_ge(scored, b * EV + g + 1)
                at = slice(g * 2 * P, (g + 1) * 2 * P) if isinstance(g, int) else bass.ds(g * 2 * P, 2 * P)
                nc.vector.scalar_tensor_tensor(sc[s][:, at], pscore[k][0:R, 0:2 * P], HD ** -0.5, bias[:, at],
                                               ALU.mult, ALU.add).then_inc(half_biased, 1)
                dve.wait_ge(half_biased, b * GR + g + 1)
                dve.wait_ge(lower_out, b * GR + g + 1)
                nc.vector.tensor_tensor(sc[s][:, at], sc[s][:, at], lower_scores[k][:, :], ALU.add).then_inc(biased, 1)

            def body(i, first):
                for slot in range(RING):
                    n = b * PG + i * RING + slot
                    k = (slot // 2) % 2
                    dve.wait_ge(khi, n + 1)
                    nc.vector.tensor_tensor(kl[k][:, :, (slot % 2) * P:(slot % 2 + 1) * P],
                                            pk[slot % 2][:, :].rearrange("p (h t) -> p h t", h=HA),
                                            kh[k][:, :, (slot % 2) * P:(slot % 2 + 1) * P].bitcast(F32),
                                            ALU.subtract).then_inc(klo, 1)
                    if first and slot == 1 and hook is not None:
                        dve_rows(dve, hook, s)
                    if slot % 2 == 1 and not (first and slot == 1):
                        take(i * (RING // 2) + slot // 2 - 1, (slot // 2 - 1) % 2)
            body(0, True)
            with dve.Fori(1, PG // RING) as i:
                body(i, False)
            take(GR - 1, (GR - 1) % 2)
            dve.wait_ge(scored, b * EV + EV)
            nc.vector.scalar_tensor_tensor(sc[s][:, PAST:KEYS], pscore[0][0:R, 0:TS], HD ** -0.5,
                                           own_bias[:, bass.ds(b, 1), :].rearrange("r o t -> r (o t)"),
                                           ALU.mult, ALU.add).then_inc(biased, 1)

        def dve_top(dve, b, s, i):
            if i == 0:
                dve.wait_ge(biased, b * EV + EV)
            if i < PIECES:
                nc.vector.tensor_reduce(tops[:, i:i + 1], sc[s][:, i * PW:(i + 1) * PW], AX,
                                        ALU.max).then_inc(topped, 1)
            else:
                dve.wait_ge(topped, b * (PIECES + 1) + PIECES)
                nc.vector.tensor_reduce(tops[:, PIECES:PIECES + 1], tops[:, 0:PIECES], AX,
                                        ALU.max).then_inc(topped, 1)
                dve.wait_ge(topped, b * (PIECES + 1) + PIECES + 1)
                nc.vector.tensor_scalar(low[:, s:s + 1], tops[:, PIECES:PIECES + 1], -1.0, None,
                                        ALU.mult).then_inc(lowered, 1)

        def dve_turn(dve, b, s, i):
            dve.wait_ge(phi, b * 2 + i + 1)
            half = slice(i * (PG // 2), (i + 1) * (PG // 2))
            nc.vector.tensor_tensor(pl[s][:, half, :], pk[i][:, :].rearrange("p (j r) -> p j r", r=R),
                                    ph[s][:, half, :].bitcast(F32), ALU.subtract).then_inc(plo, 1)

        def dve_v(dve, b, s, following, next_q):
            for p in range(PG):
                dve.wait_ge(vhi, b * PG + p + 1)
                nc.vector.tensor_tensor(vslot(kl, p), ring[:, p % RING, :], vslot(kh, p).bitcast(F32),
                                        ALU.subtract).then_inc(vlo, 1)
                if following is not None and p % 3 == 1 and p // 3 <= PIECES:
                    dve_top(dve, following, 1 - s, p // 3)
                if next_q is not None and p == 16:
                    dve_q(dve, next_q, s, False)
                if next_q is not None and p == 20:
                    dve_q_low(dve, next_q, s)
                if following is not None and p in TURNED_AT:
                    dve_turn(dve, following, 1 - s, TURNED_AT.index(p))

        def dve_rows(dve, b, s):
            nc.vector.tensor_reduce(coef[:, 0:1], dens[:, s, :], AX, ALU.add).then_inc(inverted, 1)
            dve.wait_ge(inverted, b * 3 + 1)
            nc.vector.reciprocal(coef[:, 1:2], coef[:, 0:1]).then_inc(inverted, 1)
            dve.wait_ge(inverted, b * 3 + 2)
            nc.vector.tensor_tensor(coef[:, 0:1], coef[:, 1:2], cols[:, 2:3], ALU.mult).then_inc(inverted, 1)
            dve.wait_ge(inverted, b * 3 + 3)
            dve.wait_ge(summed, b + 1)
            if not (isinstance(b, int) and b == 0):
                dve.wait_ge(kept_one, b)
            for h in range(2):
                ins = nc.vector.scalar_tensor_tensor(
                    own_rows[:, h * 512:(h + 1) * 512].rearrange("r (h e) -> r h e", e=VD),
                    pout[0:R, h * 512:(h + 1) * 512].rearrange("r (h e) -> r h e", e=VD), coef[:, 0:1],
                    heads[:, h * 4:h * 4 + 4].rearrange("r (h o) -> r h o", o=1).to_broadcast([R, 4, VD]),
                    ALU.mult, ALU.mult)
            ins.then_inc(kept_all, 1)
            dve.wait_ge(kept_all, b + 1)
            if not (isinstance(b, int) and b == 0):
                dve.wait_ge(combined, b)
            nc.vector.tensor_reduce(kept[:, :], own_rows[:, :].rearrange("r (h e) -> r e h", e=VD), AX,
                                    ALU.add).then_inc(kept_one, 1)

        @block.vector
        def _(dve):
            V = nc.vector
            dve.wait_ge(lined, LINED)
            l3 = line[:, 2, :].rearrange("o (h m q) -> o h m q", m=2, q=NS)
            V.tensor_scalar(l3[:, :, 1, :], l3[:, :, 1, :], c.neg_lam[0:1, :], None, ALU.mult).then_inc(columns, 1)
            idn = c.ident[0:R, 0:R].rearrange("r (h m q) -> r h m q", m=2, q=NS)
            V.tensor_tensor(comb[:, :].rearrange("r (h q) -> r h q", q=NS), idn[:, :, 0, :], idn[:, :, 1, :],
                            ALU.add).then_inc(consts, 1)
            V.memset(qflat[:, :], 0.0).then_inc(consts, 1)
            dve.wait_ge(columns, 2)
            V.tensor_copy(cols[:, :], pscore[1][0:R, 0:3]).then_inc(consts, 1)
            dve.wait_ge(consts, 3)
            V.tensor_scalar(bias[:, :], bias[:, :], cols[:, 1:2], cols[:, 0:1], ALU.subtract, ALU.mult)\
                .then_inc(consts, 1)
            ob = own_bias[:, :, :].rearrange("r b t -> r (b t)")
            V.tensor_scalar(sc[0][:, 0:NB * TS], ob, cols[:, 1:2], 0.0, ALU.subtract, ALU.is_gt).then_inc(own_bias_steps, 1)
            dve.wait_ge(own_bias_steps, 1)
            V.tensor_scalar(ob, ob, cols[:, 1:2], cols[:, 0:1], ALU.subtract, ALU.mult).then_inc(own_bias_steps, 1)
            dve.wait_ge(own_bias_steps, 2)
            V.scalar_tensor_tensor(ob, sc[0][:, 0:NB * TS], FILL, ob, ALU.mult, ALU.add).then_inc(consts, 1)
            dve.wait_ge(consts, 6)
            dve.wait_ge(inputs_in, 48)
            dve_q(dve, 0, 0, True)
            dve_q_low(dve, 0, 0)
            dve_k(dve, 0, 0)
            for i in range(PIECES + 1):
                dve_top(dve, 0, 0, i)
            dve_q(dve, 1, 1, False)
            dve_q_low(dve, 1, 1)
            dve_k(dve, 1, 1)
            for i in range(2):
                dve_turn(dve, 0, 0, i)
            dve_v(dve, 0, 0, 1, 2)

            def pair(g, next_q):
                b = g * 2
                dve_k(dve, b, 0, b - 2)
                dve_v(dve, b - 1, 1, b, b + 1)
                dve_k(dve, b + 1, 1, b - 1)
                dve_v(dve, b, 0, b + 1, b + 2 if next_q else None)
            with dve.Fori(1, NB // 2 - 1) as g:
                pair(g, True)
            pair(NB // 2 - 1, False)
            dve_rows(dve, NB - 2, 0)
            dve_v(dve, NB - 1, 1, None, None)
            dve_rows(dve, NB - 1, 1)

        def act_q(act, b, s):
            act.wait_ge(q_laid, b * 2 + 2)
            nc.scalar.activation(qhl[s][:, :, 0:R], qf[:, :, :], ACT.Copy).then_inc(qhi, 1)

        def act_k(act, b, s, hook=None):
            if not (isinstance(b, int) and b == 0) and hook is None:
                act.wait_ge(scored, b * EV)

            def take_lower(g, k, early):
                act.wait_ge(scored, b * EV + g + 1)
                if not (early and isinstance(b, int) and b == 0):
                    act.wait_ge(biased, b * EV if early else b * EV + g - 1)
                nc.scalar.activation(lower_scores[k][:, :], pscore[k][R:2 * R, 0:2 * P], ACT.Copy,
                                     scale=HD ** -0.5).then_inc(lower_out, 1)

            def body(i, first):
                for slot in range(RING):
                    n = b * PG + i * RING + slot
                    k = (slot // 2) % 2
                    act.wait_ge(kturned, n + 1)
                    if first and slot == 0 and hook is not None:
                        act.wait_ge(valued, (b - 1) * PG)
                    if slot % 2 == 0 and not (first and slot < 4):
                        act.wait_ge(scored, b * EV + i * (RING // 2) + (slot // 2 - 1))
                    nc.scalar.activation(kh[k][:, :, (slot % 2) * P:(slot % 2 + 1) * P],
                                         pk[slot % 2][:, :].rearrange("p (h t) -> p h t", h=HA),
                                         ACT.Copy).then_inc(khi, 1)
                    if slot % 2 == 1 and not (first and slot == 1):
                        take_lower(i * (RING // 2) + slot // 2 - 1, (slot // 2 - 1) % 2, first and slot <= 5)
                    if first and slot == 3 and hook is not None:
                        act_place(act, hook)
            body(0, True)
            with act.Fori(1, PG // RING) as i:
                body(i, False)
            take_lower(GR - 1, (GR - 1) % 2, False)

        def act_exp(act, b, s, i):
            if i == 0:
                act.wait_ge(lowered, b + 1)
            nc.scalar.activation(sc[s][:, i * PW:(i + 1) * PW], sc[s][:, i * PW:(i + 1) * PW], ACT.Exp,
                                 bias=low[:, s:s + 1], accum_out=dens[:, s, i:i + 1]).then_inc(raised, 1)

        def act_place(act, b):
            act.wait_ge(combined, b + 1)
            nc.scalar.activation(mix[:, 0:HA, bass.ds(TP + b * NS, NS)],
                                 pscore[1][:, 0:TS].rearrange("p (h q) -> p h q", q=NS), ACT.Copy).then_inc(placed, 1)

        def act_turn(act, b, s, i):
            act.wait_ge(pturned, b * 2 + i + 1)
            nc.scalar.activation(ph[s][:, i * (PG // 2):(i + 1) * (PG // 2), :],
                                 pk[i][:, :].rearrange("p (j r) -> p j r", r=R), ACT.Copy).then_inc(phi, 1)
            if i == 1:
                act.wait_ge(own_turned, b + 1)
                nc.scalar.activation(pown[s][:, :], pscore[0][0:TS, 0:R], ACT.Copy).then_inc(own_out, 1)

        def act_v(act, b, s, f, following, next_q, kphases):
            act.wait_ge(scored, kphases * EV)
            for p in range(PG):
                act.wait_ge(page_in[p % RING], f * (16 * PG // RING) + (p // RING + 1) * 16)
                if p >= 4:
                    act.wait_ge(valued, b * PG + p - 3)
                elif following is None:
                    act.wait_ge(valued, (b - 1) * PG + (PG + p - 3))
                nc.scalar.activation(vslot(kh, p), ring[:, p % RING, :], ACT.Copy).then_inc(vhi, 1)
                if following is not None and p in (15, 18, 21, 24):
                    act_exp(act, following, 1 - s, (p - 15) // 3)
                if next_q is not None and p == 17:
                    act_q(act, next_q, s)
                if following is not None and p in TURNED_AT:
                    act_turn(act, following, 1 - s, TURNED_AT.index(p))

        @block.scalar
        def _(act):
            act_q(act, 0, 0)
            act_k(act, 0, 0)
            for i in range(PIECES):
                act_exp(act, 0, 0, i)
            act_q(act, 1, 1)
            act_k(act, 1, 1)
            for i in range(2):
                act_turn(act, 0, 0, i)
            act_v(act, 0, 0, 2, 1, 2, 2)

            def pair(g, next_q):
                b = g * 2
                act_k(act, b, 0, b - 2)
                act_v(act, b - 1, 1, g * 4, b, b + 1, b + 1)
                act_k(act, b + 1, 1, b - 1)
                act_v(act, b, 0, g * 4 + 2, b + 1, b + 2 if next_q else None, b + 2)
            with act.Fori(1, NB // 2 - 1) as g:
                pair(g, True)
            pair(NB // 2 - 1, False)
            act_place(act, NB - 2)
            act_v(act, NB - 1, 1, 2 * NB - 1, None, None, NB)
            act_place(act, NB - 1)


def finish_and_project(nc, d, a, sems, c, z_dram, mix, mhi, mlo, x_dram):
    T, E, NH, N, GROUP = d.t, d.md // P, d.ha + d.hm, d.kc, Flow.RAW
    cog = (3 * d.aw + 2 * d.mw) // P
    xt = mix
    with ExitStack() as ctx:
        sb = lambda x, s, t=F32: ctx.enter_context(nc.sbuf_tensor(x, s, t))
        ps = lambda x: ctx.enter_context(nc.psum_tensor(x, [P, 2, 512], F32))
        flow = Flow(nc, ctx, d, "wout", sems)
        sq = [sb(f"fh_sq{i}", [P, T]) for i in range(2)]
        og = sb("fh_og", [P, 2, E, T])
        root, inv = sb("fh_root", [NH, T]), sb("fh_inv", [P, T])
        gains = sb("fh_gains", [P, 1 + E])
        gather, scatter = sb("fh_gather", [P, 2, 2 * NH - 1]), sb("fh_scatter", [P, NH, P])
        acc = [ps(f"o_acc{i}") for i in range(2)]
        spread = [ps(f"fh_spread{i}") for i in range(2)]
        mean = spread[0]
        gains_in, consts, residual_in, added = (sems(x) for x in ("fh_gains_in", "fh_consts", "o_residual_in", "o_added"))
        og_in = [sems(f"fh_og_in{i}") for i in range(2)]
        squared, summed, rooting, rooted, inverted, sigmoid_made, gated, spread_ready, scaled, hi_made, lo_made = (
            sems(f"fh_{x}") for x in ("squared", "summed", "rooting", "rooted", "inverted", "sigmoid_made", "gated",
                                      "spread_ready", "scaled", "hi_made", "lo_made"))
        head = lambda n: n if n < d.ha else d.ha + (n - d.ha) // E
        two = lambda x: x.rearrange("p (b t) -> p b t", b=2)
        ogv = z_dram[0:(cog + d.hm * E) * P, :].rearrange("(c e p) t -> c p e t", e=E, p=P)
        w = a["w_out"][0].rearrange("(k p) n -> p k n", p=P)
        tile = lambda x, j: x[:, j, :].rearrange("p (k n) -> p k n", k=d.kc)
        block = ctx.enter_context(nc.Block())

        @block.sync
        def _(sp):
            sp.dma_start(gains[:, 0:1], a["attn_out_norm"].rearrange("o p -> p o"),
                         allow_slow_non_contiguous=True).then_inc(gains_in, 16)
            sp.dma_start(gains[:, 1:1 + E], a["mlstm_out_norm"][0].rearrange("(e p) -> p e", p=P),
                         allow_slow_non_contiguous=True).then_inc(gains_in, 16)
            for h in range(2):
                sp.dma_start(og[:, h, :, :], ogv[cog // E + h]).then_inc(og_in[h], 16)
            for j in range(GROUP):
                sp.dma_start(tile(flow.raw, j), w[:, :, j * P:(j + 1) * P]).then_inc(flow.landed[j], 16)
            for h in range(2, d.hm):
                sp.wait_ge(gated, (h - 1) * E)
                sp.dma_start(og[:, h % 2, :, :], ogv[cog // E + h]).then_inc(og_in[h % 2], 16)
            sp.wait_ge(lo_made, d.kc)
            sp.dma_start(xt[:, :, :], x_dram.rearrange("(k p) t -> p k t", p=P)).then_inc(residual_in, 16)
            with sp.Fori(0, N // GROUP - 1) as g:
                for j in range(GROUP):
                    sp.wait_ge(flow.lo_made, g * GROUP + (j + 1))
                    sp.dma_start(tile(flow.raw, j), w[:, :, bass.ds((g * GROUP + (GROUP + j)) * P, P)])\
                        .then_inc(flow.landed[j], 16)

        @block.gpsimd
        def _(pool):
            G = nc.gpsimd
            G.memset(gather[:, :, :], 0.0).then_inc(consts, 1)
            pool.wait_ge(consts, 1)
            for i, width in enumerate((d.vd, d.md)):
                G.memset(gather[:, i, NH - 1:NH], 1.0 / width).then_inc(consts, 1)
                pool.wait_ge(consts, 2 + i)
            G.memset(scatter[:, :, :], 1.0).then_inc(consts, 1)
            G.memset(inv[:, :], 0.0).then_inc(consts, 1)
            pool.wait_ge(consts, 5)
            G.affine_select(out=scatter[:, :, :], in_=scatter[:, :, :], compare_op=ALU.is_equal, fill=0.0, base=0,
                            pattern=[[-1, NH], [0, P]], channel_multiplier=1).then_inc(consts, 1)

        def leading(j):
            nc.scalar.activation(flow.hi[:, j % 2, :], flow.raw[:, j, :], ACT.Copy).then_inc(flow.hi_made, 1)

        def act_group(act, g, first):
            for j in range(2 if first else 0, GROUP):
                act.wait_ge(flow.landed[j], g * 16 + 16)
                act.wait_ge(flow.used, g * GROUP + (j - 1))
                leading(j)

        @block.scalar
        def _(act):
            for h in range(d.hm):
                act.wait_ge(og_in[h % 2], 16 * (h // 2 + 1))
                nc.scalar.activation(og[:, h % 2, :, :], og[:, h % 2, :, :], ACT.Sigmoid).then_inc(sigmoid_made, 1)
                if h < 2:
                    act.wait_ge(flow.landed[h], 16)
                    leading(h)
            act.wait_ge(rooting, 1)
            nc.scalar.activation(root[:, :], root[:, :], ACT.Sqrt).then_inc(rooted, 1)
            for n in range(d.kc):
                act.wait_ge(scaled, n + 1)
                nc.scalar.activation(mhi[:, n, :], mix[:, n, :], ACT.Copy).then_inc(hi_made, 1)
            act_group(act, 0, True)
            with act.Fori(1, N // GROUP) as g:
                act_group(act, g, False)

        def trailing(dve, n, j):
            dve.wait_ge(flow.hi_made, n + 1)
            nc.vector.tensor_tensor(flow.lo[:, j % 2, :], flow.raw[:, j, :], flow.hi[:, j % 2, :].bitcast(F32),
                                    ALU.subtract).then_inc(flow.lo_made, 1)

        def add(dve, n, j):
            dve.wait_ge(flow.used, n + 1)
            x = xt[:, bass.ds(n, 1), :].rearrange("p o (h t) -> p (o h) t", h=2)
            nc.vector.tensor_tensor(x, x, acc[j % 2][:, :, 0:d.half], ALU.add).then_inc(added, 1)

        def dve_group(dve, g, first):
            for j in range(GROUP):
                n = g * GROUP + j
                if not (first and j < 2):
                    trailing(dve, n, j)
                if first and j == 1:
                    dve.wait_ge(residual_in, 16)
                if not (first and j == 0):
                    add(dve, n - 1, (j - 1) % 2)

        @block.vector
        def _(dve):
            V = nc.vector
            order = list(range(d.ha, d.kc)) + list(range(d.ha))
            for i, n in enumerate(order):
                if i >= 2:
                    dve.wait_ge(summed, i - 1)
                V.tensor_tensor(sq[i % 2][:, :], mix[:, n, :], mix[:, n, :], ALU.mult).then_inc(squared, 1)
                if i % 2 and i // 2 < d.hm:
                    h = i // 2
                    dve.wait_ge(sigmoid_made, h + 1)
                    dve.wait_ge(squared, i + 1)
                    x = mix[:, d.ha + h * E:d.ha + (h + 1) * E, :]
                    V.tensor_tensor(x, x, og[:, h % 2, :, :], ALU.mult).then_inc(gated, E)
                if i in (9, 11):
                    trailing(dve, (i - 9) // 2, (i - 9) // 2)
            dve.wait_ge(gains_in, 32)
            V.tensor_scalar(gains[:, 0:1], gains[:, 0:1], 1.0 - LAM_INIT, None, ALU.mult).then_inc(gated, 1)
            dve.wait_ge(gated, d.hm * E + 1)
            dve.wait_ge(summed, d.kc)
            V.tensor_scalar(two(root[:, :]), mean[0:NH, :, 0:d.half], EPS, None, ALU.add).then_inc(rooting, 1)
            dve.wait_ge(rooted, 1)
            dve.wait_ge(consts, 6)
            V.reciprocal(inv[0:NH, :], root[:, :]).then_inc(inverted, 1)

            def trail(n):
                dve.wait_ge(hi_made, n + 1)
                V.tensor_tensor(mlo[:, n, :], mix[:, n, :], mhi[:, n, :].bitcast(F32), ALU.subtract)\
                    .then_inc(lo_made, 1)

            for n in range(d.kc):
                h = head(n)
                gain = gains[:, 0:1] if n < d.ha else gains[:, 1 + (n - d.ha) % E:2 + (n - d.ha) % E]
                dve.wait_ge(spread_ready, h + 1)
                V.scalar_tensor_tensor(two(mix[:, n, :]), two(mix[:, n, :]), gain, spread[h % 2][:, :, 0:d.half],
                                       ALU.mult, ALU.mult).then_inc(scaled, 1)
                if n >= 1:
                    trail(n - 1)
            trail(d.kc - 1)
            dve_group(dve, 0, True)
            with dve.Fori(1, N // GROUP) as g:
                dve_group(dve, g, False)
            add(dve, N - 1, 1)

        def pe_tile(pe, n, j, first=False):
            pe.wait_ge(flow.lo_made, n + 1)
            if not first:
                pe.wait_ge(added, n - 1)
            whi, wlo = tile(flow.hi, j), tile(flow.lo, j)
            for h in range(2):
                cs = slice(h * d.half, (h + 1) * d.half)
                for k in range(d.kc):
                    if first and j == 0 and h == 0:
                        pe.wait_ge(lo_made, k + 1)
                    mm = exact_passes(nc, acc[j][:, h, 0:d.half], whi[:, k, :], wlo[:, k, :], mhi[:, k, cs],
                                      mlo[:, k, cs], k == 0, k == d.kc - 1)
            mm.then_inc(flow.used, 1)

        @block.tensor
        def _(pe):
            pe.wait_ge(consts, 6)
            for i in range(d.kc):
                n = d.ha + i if i < d.kc - d.ha else i - (d.kc - d.ha)
                h = head(n)
                pe.wait_ge(squared, i + 1)
                for b in range(2):
                    mm = nc.tensor.matmul(mean[0:NH, b, 0:d.half], gather[:, int(n >= d.ha), NH - 1 - h:2 * NH - 1 - h],
                                          sq[i % 2][:, b * d.half:(b + 1) * d.half], start=(i == 0),
                                          stop=(i == d.kc - 1))
                mm.then_inc(summed, 1)
            pe.wait_ge(inverted, 1)
            for h in range(NH):
                if h >= 2:
                    pe.wait_ge(scaled, h - 1 if h - 2 < d.ha else d.ha + (h - 1 - d.ha) * E)
                for b in range(2):
                    mm = nc.tensor.matmul(spread[h % 2][:, b, 0:d.half], scatter[:, h, :],
                                          inv[:, b * d.half:(b + 1) * d.half], start=True, stop=True)
                mm.then_inc(spread_ready, 1)
            for j in range(2):
                pe_tile(pe, j, j, True)
            with pe.Fori(1, N // 2) as g:
                for j in range(2):
                    pe_tile(pe, g * 2 + j, j)


def mlp(nc, d, a, sems, xhi, xlo, xt):
    G, GROUPS = 4, d.ff // (4 * P)
    OUT = d.kc // G
    assert OUT == 4 and Flow.RAW == G
    with ExitStack() as ctx:
        sb = lambda x, s, t=F32: ctx.enter_context(nc.sbuf_tensor(x, s, t))
        flow = Flow(nc, ctx, d, "ffn", sems)
        hid = sb("hidden", [P, 2, d.t])
        hhi, hlo = (sb(f"hidden_{x}", [P, G, d.t], F32R) for x in ("hi", "lo"))
        acc = [ctx.enter_context(nc.psum_tensor(f"f_acc{i}", [P, 2, 512], F32)) for i in range(4)]
        relued, squared, h_hi, h_lo, added = (sems(f"ffn_{x}") for x in ("relued", "squared", "h_hi", "h_lo", "added"))
        up = a["w_up"][0].rearrange("(k p) n -> p k n", p=P)
        down = a["w_down"][0].rearrange("(g k p) n -> g p k n", k=G, p=P)
        up_tile = lambda x, j: x[:, j, :].rearrange("p (k n) -> p k n", k=d.kc)
        down_tile = lambda x, j: x[:, j, :].rearrange("p (k n) -> p k n", k=G)
        halves = lambda x: x.rearrange("p (h t) -> p h t", h=2)
        gain = sb("norm_ffn_cols", [P, d.kc])
        gain_in = sems("norm_ffn_in")
        norm = NormBuffers(nc, ctx, d, sems, "ffn_norm", hid, [acc[3][:, h, :] for h in range(2)])
        block = ctx.enter_context(nc.Block())

        def groups(eng, run):
            run(0, True)
            with eng.Fori(1, GROUPS) as g:
                run(g, False)

        @block.sync
        def _(sp):
            sp.dma_start(gain[:, :], a["norm_ffn"][0].rearrange("(k p) -> p k", p=P),
                         allow_slow_non_contiguous=True).then_inc(gain_in, 16)

            def load(g, first):
                for j in range(G):
                    if not first:
                        sp.wait_ge(flow.lo_made, g * (2 * G) - (G - 1 - j))
                    sp.dma_start(up_tile(flow.raw, j), up[:, :, bass.ds((g * G + j) * P, P)])\
                        .then_inc(flow.landed[j], 16)
                for j in range(G):
                    sp.wait_ge(flow.lo_made, g * (2 * G) + j + 1)
                    sp.dma_start(down_tile(flow.raw, j), down[g][:, :, j * OUT * P:(j + 1) * OUT * P])\
                        .then_inc(flow.landed[j], 16)
            groups(sp, load)

        @block.scalar
        def _(act):
            def split(g, i, first):
                act.wait_ge(flow.landed[i % G], g * 32 + 16 * (i // G + 1))
                if not (first and i < 2):
                    act.wait_ge(flow.used, g * 32 + (4 * i - 4))
                nc.scalar.activation(flow.hi[:, i % 2, :], flow.raw[:, i % G, :], ACT.Copy).then_inc(flow.hi_made, 1)

            def hidden(g, j, first):
                act.wait_ge(flow.used, g * 32 + 4 * (j + 1))
                if not (first and j < 2):
                    act.wait_ge(h_lo, g * G + (j - 1))
                nc.scalar.activation(halves(hid[:, j % 2, :]), acc[j % 2][:, :, 0:d.half], ACT.Relu)\
                    .then_inc(relued, 1)
                act.wait_ge(squared, g * G + (j + 1))
                nc.scalar.activation(hhi[:, j, :], hid[:, j % 2, :], ACT.Copy).then_inc(h_hi, 1)

            def run(g, first):
                for i in range(2 * G):
                    if not (first and i < 2):
                        split(g, i, first)
                    if 1 <= i <= G:
                        hidden(g, i - 1, first)
            for i in range(2):
                split(0, i, True)
            norm_scalar(nc, act, d, norm, xhi)
            groups(act, run)

        @block.vector
        def _(dve):
            def hidden(g, j):
                n = g * G + (j + 1)
                dve.wait_ge(relued, n)
                nc.vector.tensor_tensor(hid[:, j % 2, :], hid[:, j % 2, :], hid[:, j % 2, :], ALU.mult)\
                    .then_inc(squared, 1)
                dve.wait_ge(h_hi, n)
                nc.vector.tensor_tensor(hlo[:, j, :], hid[:, j % 2, :], hhi[:, j, :].bitcast(F32), ALU.subtract)\
                    .then_inc(h_lo, 1)

            def add(g, j):
                for i in range(OUT):
                    oc = j * OUT + i
                    dve.wait_ge(flow.used, g * 32 + (4 * (G + j) + i + 1))
                    nc.vector.tensor_tensor(halves(xt[:, oc, :]), halves(xt[:, oc, :]),
                                            acc[2 + i % 2][:, :, 0:d.half], ALU.add).then_inc(added, 1)

            def split(g, i):
                dve.wait_ge(flow.hi_made, g * (2 * G) + (i + 1))
                nc.vector.tensor_tensor(flow.lo[:, i % 2, :], flow.raw[:, i % G, :],
                                        flow.hi[:, i % 2, :].bitcast(F32), ALU.subtract).then_inc(flow.lo_made, 1)

            def run(g, first):
                for i in range(2 * G):
                    if not (first and i < 2):
                        split(g, i)
                    if i == 0 and not first:
                        add(g - 1, G - 1)
                    if 1 <= i <= G:
                        hidden(g, i - 1)
                    if i > G:
                        add(g, i - G - 1)
            for k in range(d.kc):
                norm_square(nc, dve, norm, xt, k)
            for i in range(2):
                split(0, i)
            dve.wait_ge(gain_in, 16)
            norm_scale(nc, dve, d, norm, xt, gain, xhi, xlo)
            groups(dve, run)
            add(GROUPS - 1, G - 1)

        @block.tensor
        def _(pe):
            def run(g, first):
                for j in range(G):
                    pe.wait_ge(flow.lo_made, g * (2 * G) + (j + 1))
                    if not (first and j < 2):
                        pe.wait_ge(relued, g * G + (j - 1))
                    whi, wlo = up_tile(flow.hi, j % 2), up_tile(flow.lo, j % 2)
                    for h in range(2):
                        cs = slice(h * d.half, (h + 1) * d.half)
                        for k in range(d.kc):
                            if first and j == 0 and h == 0:
                                pe.wait_ge(norm.lo_made, k + 1)
                            mm = exact_passes(nc, acc[j % 2][:, h, 0:d.half], whi[:, k, :], wlo[:, k, :],
                                              xhi[:, k, cs], xlo[:, k, cs], k == 0, k == d.kc - 1)
                            if h and k % 4 == 3:
                                mm.then_inc(flow.used, 1)
                for j in range(G):
                    pe.wait_ge(flow.lo_made, g * (2 * G) + (G + j + 1))
                    whi, wlo = down_tile(flow.hi, j % 2), down_tile(flow.lo, j % 2)
                    for i in range(OUT):
                        if not (first and j == 0 and i < 2):
                            pe.wait_ge(added, g * d.kc + (j * OUT + i - 1))
                        ws = slice(i * P, (i + 1) * P)
                        for ks in (range(G - 1), (G - 1,)):
                            if j == 0 and i == 0 and ks == (G - 1,):
                                pe.wait_ge(h_lo, g * G + G)
                            elif j == 0 and i == 0:
                                pe.wait_ge(h_lo, g * G + (G - 1))
                            for h in range(2):
                                cs = slice(h * d.half, (h + 1) * d.half)
                                for k in ks:
                                    mm = exact_passes(nc, acc[2 + i % 2][:, h, 0:d.half], whi[:, k, ws], wlo[:, k, ws],
                                                      hhi[:, k, cs], hlo[:, k, cs], k == 0, k == G - 1)
                        mm.then_inc(flow.used, 1)
            for k in range(d.kc):
                norm_mean(nc, pe, d, norm, k)
            groups(pe, run)


def emit(nc, d, sems, c, xt, y_prompt, y_sample):
    tiles = [(N_META + i * P, P) for i in range(d.seq // P)] + [(d.tp, d.tsmp)]
    QUAD = 4
    with ExitStack() as ctx:
        y = [ctx.enter_context(nc.sbuf_tensor(f"y_rows{i}", [P, d.dm], F32)) for i in range(2)]
        turned = [ctx.enter_context(nc.psum_tensor(f"y_turned{i}", [P, d.kc * P], F32)) for i in range(2)]
        ready, out_a, out_b = sems("y_turned_ready"), sems("y_out_a"), sems("y_out_b")
        stored = [sems(f"y_stored{i}") for i in range(2)]
        block = ctx.enter_context(nc.Block())
        mid = d.dm // 2

        @block.tensor
        def _(pe):
            for i, (t0, n) in enumerate(tiles):
                if i >= 2:
                    pe.wait_ge(out_a, i - 1)
                    pe.wait_ge(out_b, i - 1)
                for k in range(d.kc):
                    mm = nc.tensor.transpose(turned[i % 2][0:n, k * P:(k + 1) * P], xt[:, k, t0:t0 + n], c.ident[:, :])
                mm.then_inc(ready, 1)

        @block.scalar
        def _(act):
            for i, (t0, n) in enumerate(tiles):
                act.wait_ge(ready, i + 1)
                if i >= 2:
                    act.wait_ge(stored[i % 2], 16 * (i // 2))
                nc.scalar.activation(y[i % 2][0:n, 0:mid], turned[i % 2][0:n, 0:mid], ACT.Copy).then_inc(out_a, 1)

        @block.vector
        def _(dve):
            for i, (t0, n) in enumerate(tiles):
                dve.wait_ge(ready, i + 1)
                if i >= 2:
                    dve.wait_ge(stored[i % 2], 16 * (i // 2))
                nc.vector.tensor_copy(y[i % 2][0:n, mid:], turned[i % 2][0:n, mid:]).then_inc(out_b, 1)

        @block.sync
        def _(sp):
            for i, (t0, n) in enumerate(tiles):
                sp.wait_ge(out_a, i + 1)
                sp.wait_ge(out_b, i + 1)
                dst = y_prompt[0][t0 - N_META:t0 - N_META + n, :] if t0 < d.tp else \
                    y_sample.rearrange("b s m -> (b s) m")
                sp.dma_start(dst, y[i % 2][0:n, :]).then_inc(stored[i % 2], 16)
            for i in range(2):
                sp.wait_ge(stored[i], 16 * ((len(tiles) - i + 1) // 2))


def output_shapes(a):
    d = Dims(a)
    return [(1, d.seq, d.dm), (d.nb, d.ns, d.dm),
            (1, 1, d.tp, d.ha, d.vd), (1, 1, d.tp, d.ha, d.vd), (1, 1, d.hm, d.md, d.md), (1, 1, d.hm, d.md),
            (1, 1, d.hm), (1, 1, a["conv_w"].shape[1] - 1, d.mw),
            (1, d.nb, d.ns, d.ha, d.vd), (1, d.nb, d.ns, d.ha, d.vd), (1, d.nb, d.hm, d.md, d.md),
            (1, d.nb, d.hm, d.md), (1, d.nb, d.hm), (1, d.nb, a["conv_w"].shape[1] - 1, d.mw)]


def build(nc, a, outs):
    d = Dims(a)
    y_prompt, y_sample, k_prompt, v_prompt, c_prompt, n_prompt, m_prompt, conv_prompt, \
        k_sample, v_sample, c_sample, n_sample, m_sample, conv_sample = outs
    with ExitStack() as ctx:
        scratch = lambda n, s: nc.dram_tensor(n, s, F32).ap()
        tokens = lambda x: x.rearrange("o b t h e -> (o b t) (h e)")
        c = Consts(nc, ctx, d)
        with stage(nc) as sems:
            setup(nc, d, a, sems, c)
        xt_dram = scratch("xt_scratch", [d.dm, d.t])
        z_dram = scratch("z_scratch", [d.pw, d.t])
        zn_dram = scratch("zn_scratch", [2 * d.aw, d.t])
        qk_dram = scratch("qk_scratch", [2 * d.mw, d.t])
        kt_dram = scratch("kt_scratch", [d.t, d.mw])
        vt_dram = scratch("vt_scratch", [d.t, d.mw])
        g_dram = scratch("g_scratch", [4, d.hm, d.t])
        with ExitStack() as one:
            xhi = one.enter_context(nc.sbuf_tensor("xn_hi", [P, d.kc, d.t], F32R))
            xlo = one.enter_context(nc.sbuf_tensor("xn_lo", [P, d.kc, d.t], F32R))
            with stage(nc) as sems:
                embed_and_project(nc, d, a, sems, c.ident, xhi, xlo, xt_dram, z_dram)
        with stage(nc) as sems:
            gates(nc, d, a, sems, z_dram, g_dram, m_prompt, m_sample)
        with ExitStack() as three:
            mix = three.enter_context(nc.sbuf_tensor("mix_t", [P, d.kc, d.t], F32))
            with stage(nc) as sems:
                heads_prepare(nc, d, a, sems, c, z_dram, zn_dram, tokens(k_prompt), tokens(v_prompt),
                              tokens(k_sample), tokens(v_sample))
            with stage(nc) as sems:
                prompt_attention(nc, d, a, sems, c, zn_dram, tokens(v_prompt), mix)
            with stage(nc) as sems:
                mlstm_features(nc, d, a, sems, c, z_dram, qk_dram, kt_dram, vt_dram, conv_prompt, conv_sample)
            with stage(nc) as sems:
                prompt_mlstm(nc, d, a, sems, c, qk_dram, kt_dram, vt_dram, g_dram, mix, c_prompt, n_prompt)
            with stage(nc) as sems:
                sample_mlstm(nc, d, a, sems, c, qk_dram, kt_dram, vt_dram, g_dram, mix, c_sample, n_sample)
            with stage(nc) as sems:
                decode_attention(nc, d, a, sems, c, zn_dram, tokens(v_sample), mix)
            with ExitStack() as four:
                mhi = four.enter_context(nc.sbuf_tensor("mix_hi", [P, d.kc, d.t], F32R))
                mlo = four.enter_context(nc.sbuf_tensor("mix_lo", [P, d.kc, d.t], F32R))
                with stage(nc) as sems:
                    finish_and_project(nc, d, a, sems, c, z_dram, mix, mhi, mlo, xt_dram)
            xhi = three.enter_context(nc.sbuf_tensor("xf_hi", [P, d.kc, d.t], F32R))
            xlo = three.enter_context(nc.sbuf_tensor("xf_lo", [P, d.kc, d.t], F32R))
            with stage(nc) as sems:
                mlp(nc, d, a, sems, xhi, xlo, mix)
            with stage(nc) as sems:
                emit(nc, d, sems, c, mix, y_prompt, y_sample)


_INS = ["x_prompt", "x_sample", "cache_k", "cache_v", "state_C", "state_n", "state_m", "state_conv", "page_table",
        "meta_tokens", "norm_mix", "w_in", "q_norm", "k_norm", "lambda_qk", "attn_out_norm", "conv_w", "conv_b",
        "w_qm", "w_km", "gate_bias", "mlstm_out_norm", "w_out", "norm_ffn", "w_up", "w_down"]


def kernel(**inputs):
    import numpy as _np
    import concourse.bacc as _bacc
    from concourse import mybir as _mybir
    from concourse.bass_utils import run_bass_kernel_spmd as _run

    nc = _bacc.Bacc("TRN2", target_bir_lowering=False, num_devices=1)
    arrays, a = {}, {}
    for name in _INS:
        x = _np.ascontiguousarray(inputs[name])
        arrays[f"in_{name}"] = x
        a[name] = nc.dram_tensor(f"in_{name}", x.shape, _mybir.dt.from_np(x.dtype), kind="ExternalInput").ap()
    shapes = output_shapes(a)
    outs = [nc.dram_tensor(f"out_{i}", s, F32, kind="ExternalOutput").ap() for i, s in enumerate(shapes)]
    build(nc, a, outs)
    r = _run(nc, [arrays], core_ids=[0])
    return tuple(r.results[0][f"out_{i}"] for i in range(len(shapes)))
```
